# Optimizing a Trainium2 kernel written in Bass

```python
import math
import jax
import jax.numpy as jnp
from jax import lax
import numpy as np

D_MODEL = 1024
BATCH = 1
SEQ = 1024
DEPTH = 1
DEC_BATCH = 8
DEC_SEQ = 8
PAST_LEN = 2048
PAGE_SIZE = 128

MIX_WIDTH = D_MODEL
DA_WIDTH = MIX_WIDTH // 2
DA_HEAD_DIM = 64
DA_HEADS = DA_WIDTH // (2 * DA_HEAD_DIM)
HG_WIDTH = MIX_WIDTH - DA_WIDTH
HG_EXPAND = 128
HG_HEADS = HG_WIDTH // HG_EXPAND
HG_DV = HG_WIDTH // HG_HEADS
HG_CHUNK = 64
Q_BLOCK = 128
N_GROUPS = 4
EXPERTS_PER_GROUP = 4
N_EXPERTS = N_GROUPS * EXPERTS_PER_GROUP
TOP_K_INNER = 2
EXPERT_FF = D_MODEL // 4
IN_COLS = 3 * DA_WIDTH + 4 * HG_WIDTH
EPS = 1e-6
NEG_INF = -1e30

kernel_name = "hymba_diffattn_hgrn2_hiermoe_step"

def _rms(x, w):
    xf = x.astype(jnp.float32)
    y = xf * lax.rsqrt(jnp.mean(xf * xf, axis=-1, keepdims=True) + EPS)
    return y.astype(x.dtype) * w

def _split_proj(xn, w_in):
    z = jnp.einsum("btd,dc->btc", xn, w_in)
    bounds = np.cumsum([0, DA_WIDTH, DA_WIDTH, DA_WIDTH, HG_WIDTH, HG_WIDTH, HG_WIDTH, HG_WIDTH])
    return [z[..., int(bounds[i]):int(bounds[i + 1])] for i in range(7)]

def _da_qkv(zq, zk, zv, qn_w, kn_w):
    B, T, _ = zq.shape
    q = _rms(zq.reshape(B, T, DA_HEADS, 2, DA_HEAD_DIM), qn_w) * (DA_HEAD_DIM ** -0.5)
    k = _rms(zk.reshape(B, T, DA_HEADS, 2, DA_HEAD_DIM), kn_w)
    v = zv.reshape(B, T, DA_HEADS, 2 * DA_HEAD_DIM)
    return q, k, v

def _da_lambda(lq1, lk1, lq2, lk2, layer_idx):
    lam_init = 0.8 - 0.6 * math.exp(-0.3 * layer_idx)
    f32 = jnp.float32
    lam = (jnp.exp(jnp.sum(lq1.astype(f32) * lk1.astype(f32)))
           - jnp.exp(jnp.sum(lq2.astype(f32) * lk2.astype(f32))) + lam_init)
    return lam, lam_init

def _diff_map(s, lam):
    p = jax.nn.softmax(s, axis=-1)
    return p[:, :, 0] - lam * p[:, :, 1]

def _da_prompt(q, k, v, lam):
    B, T = q.shape[:2]
    qb = math.gcd(T, Q_BLOCK)
    nb = T // qb
    q_blocks = q.reshape(B, nb, qb, DA_HEADS, 2, DA_HEAD_DIM).swapaxes(0, 1)
    kpos = jnp.arange(T)

    def one(args):
        i, qblk = args
        qpos = i * qb + jnp.arange(qb)
        s = jnp.einsum("bqhmd,bshmd->bhmqs", qblk, k).astype(jnp.float32)
        s = jnp.where(kpos[None, :] <= qpos[:, None], s, NEG_INF)
        a = _diff_map(s, lam).astype(v.dtype)
        return jnp.einsum("bhqs,bshe->bqhe", a, v)

    out = lax.map(one, (jnp.arange(nb), q_blocks))
    return out.swapaxes(0, 1).reshape(B, T, DA_HEADS, 2 * DA_HEAD_DIM)

def _da_decode(q, k_new, v_new, past_k, past_v, lam):
    T = q.shape[1]
    P = past_k.shape[1]
    s_past = jnp.einsum("bqhmd,bshmd->bhmqs", q, past_k).astype(jnp.float32)
    s_new = jnp.einsum("bqhmd,bshmd->bhmqs", q, k_new).astype(jnp.float32)
    causal = jnp.tril(jnp.ones((T, T), dtype=bool))
    s_new = jnp.where(causal, s_new, NEG_INF)
    a = _diff_map(jnp.concatenate([s_past, s_new], axis=-1), lam).astype(v_new.dtype)
    return (jnp.einsum("bhqs,bshe->bqhe", a[..., :P], past_v)
            + jnp.einsum("bhqs,bshe->bqhe", a[..., P:], v_new))

def _hgrn2_scan(q, k, v, logf, S0):
    B, T, H, DK = q.shape
    C = math.gcd(T, HG_CHUNK)
    n = T // C

    def chunks(a):
        return a.reshape(B, n, C, *a.shape[2:]).swapaxes(0, 1)

    causal = jnp.tril(jnp.ones((C, C), dtype=bool))[None, :, :, None, None]

    def step(S, inp):
        qc, kc, vc, gc = inp
        b = jnp.cumsum(gc, axis=1)
        decay = jnp.exp(jnp.where(causal, b[:, :, None] - b[:, None, :], -jnp.inf))
        A = jnp.einsum("bthk,bshk,btshk->bhts", qc, kc, decay)
        o = (jnp.einsum("bhts,bshv->bthv", A, vc)
             + jnp.einsum("bthk,bhkv->bthv", qc * jnp.exp(b), S))
        b_end = b[:, -1]
        S_new = (jnp.exp(b_end)[..., None] * S
                 + jnp.einsum("bshk,bshv->bhkv", kc * jnp.exp(b_end[:, None] - b), vc))
        return S_new, o

    S_fin, o = lax.scan(step, S0, (chunks(q), chunks(k), chunks(v), chunks(logf)))
    return S_fin, o.swapaxes(0, 1).reshape(B, T, H, v.shape[-1])

def _hgrn2(zq, zf, zi, zg, lb, S0, norm_w):
    B, T, _ = zq.shape
    shp = (B, T, HG_HEADS, HG_EXPAND)
    f = lb + (1.0 - lb) * jax.nn.sigmoid(zf.astype(jnp.float32))
    q = jax.nn.silu(zq.astype(jnp.float32)).reshape(shp)
    kk = (1.0 - f).reshape(shp)
    logf = jnp.log(f).reshape(shp)
    v = zi.astype(jnp.float32).reshape(B, T, HG_HEADS, HG_DV)
    S_fin, o = _hgrn2_scan(q, kk, v, logf, S0.astype(jnp.float32))
    o = _rms(o.astype(zq.dtype), norm_w) * jax.nn.silu(zg).reshape(B, T, HG_HEADS, HG_DV)
    return o.reshape(B, T, HG_WIDTH), S_fin.astype(S0.dtype)

def _hier_moe(xn, w_rg, b_rg, w_re, b_re, w_gate, w_up, w_down):
    B, T, _ = xn.shape
    g_logit = (jnp.einsum("btd,dg->btg", xn, w_rg) + b_rg).astype(jnp.float32)
    g_idx = jnp.argmax(g_logit, axis=-1)
    g_w = jnp.take_along_axis(jax.nn.softmax(g_logit, axis=-1), g_idx[..., None], axis=-1)
    e_logit = (jnp.einsum("btd,de->bte", xn, w_re) + b_re).astype(jnp.float32)
    e_logit = e_logit.reshape(B, T, N_GROUPS, EXPERTS_PER_GROUP)
    e_sel = jnp.take_along_axis(e_logit, g_idx[..., None, None], axis=2)[:, :, 0]
    top_v, top_i = lax.top_k(e_sel, TOP_K_INNER)
    w_pair = jax.nn.softmax(top_v, axis=-1) * g_w
    expert_id = g_idx[..., None] * EXPERTS_PER_GROUP + top_i
    gates = jnp.sum(jax.nn.one_hot(expert_id, N_EXPERTS, dtype=jnp.float32) * w_pair[..., None], axis=-2)
    h = jax.nn.silu(jnp.einsum("btd,edf->btef", xn, w_gate)) * jnp.einsum("btd,edf->btef", xn, w_up)
    h = h * gates[..., None].astype(h.dtype)
    return jnp.einsum("btef,efd->btd", h, w_down)

def _layer(x, S0, past_k, past_v, layer_idx, norm1_w, w_in, qn_w, kn_w, lq1, lk1, lq2, lk2,
           subln_w, lb, hg_norm_w, w_out, norm2_w, w_rg, b_rg, w_re, b_re, w_gate, w_up, w_down):
    B, T, _ = x.shape
    xn = _rms(x, norm1_w)
    zq, zk, zv, hq, hf, hi, hg = _split_proj(xn, w_in)
    q, k, v = _da_qkv(zq, zk, zv, qn_w, kn_w)
    lam, lam_init = _da_lambda(lq1, lk1, lq2, lk2, layer_idx)
    if past_k is None:
        o_da = _da_prompt(q, k, v, lam)
    else:
        o_da = _da_decode(q, k, v, past_k, past_v, lam)
    o_da = (_rms(o_da, subln_w) * (1.0 - lam_init)).reshape(B, T, DA_WIDTH)
    o_hg, S_new = _hgrn2(hq, hf, hi, hg, lb, S0, hg_norm_w)
    h = x + jnp.einsum("btc,cd->btd", jnp.concatenate([o_da, o_hg], axis=-1), w_out)
    y = h + _hier_moe(_rms(h, norm2_w), w_rg, b_rg, w_re, b_re, w_gate, w_up, w_down)
    return y, k.reshape(B, T, DA_HEADS, 2 * DA_HEAD_DIM), v, S_new

def setup_inputs(seed: int = 0) -> dict:
    key = jax.random.key(seed)
    ks = jax.random.split(key, 26)
    f32 = jnp.float32

    def nrm(k, shape, scale):
        return jax.random.normal(k, shape, f32) * scale

    n_pages = PAST_LEN // PAGE_SIZE
    n_phys = (5 * DEC_BATCH * n_pages) // 4
    page_table = jax.random.permutation(ks[5], n_phys)[: DEC_BATCH * n_pages]
    page_table = page_table.reshape(DEC_BATCH, n_pages).astype(jnp.int32)
    return {
        "x_prompt": nrm(ks[0], (BATCH, SEQ, D_MODEL), 1.0),
        "x_sample": nrm(ks[1], (DEC_BATCH, DEC_SEQ, D_MODEL), 1.0),
        "cache_k": nrm(ks[2], (DEPTH, n_phys, PAGE_SIZE, DA_HEADS, 2 * DA_HEAD_DIM), 1.0),
        "cache_v": nrm(ks[3], (DEPTH, n_phys, PAGE_SIZE, DA_HEADS, 2 * DA_HEAD_DIM), 1.0),
        "state_hgrn": nrm(ks[4], (DEPTH, DEC_BATCH, HG_HEADS, HG_EXPAND, HG_DV), 0.3),
        "page_table": page_table,
        "norm1_w": 1.0 + nrm(ks[6], (DEPTH, D_MODEL), 0.02),
        "w_in": nrm(ks[7], (DEPTH, D_MODEL, IN_COLS), D_MODEL ** -0.5),
        "q_norm_w": 1.0 + nrm(ks[8], (DEPTH, DA_HEAD_DIM), 0.02),
        "k_norm_w": 1.0 + nrm(ks[9], (DEPTH, DA_HEAD_DIM), 0.02),
        "lambda_q1": nrm(ks[10], (DEPTH, DA_HEAD_DIM), 0.1),
        "lambda_k1": nrm(ks[11], (DEPTH, DA_HEAD_DIM), 0.1),
        "lambda_q2": nrm(ks[12], (DEPTH, DA_HEAD_DIM), 0.1),
        "lambda_k2": nrm(ks[13], (DEPTH, DA_HEAD_DIM), 0.1),
        "subln_w": 1.0 + nrm(ks[14], (DEPTH, 2 * DA_HEAD_DIM), 0.02),
        "hg_lb": nrm(ks[15], (DEPTH + 1, HG_WIDTH), 0.5),
        "hg_norm_w": 1.0 + nrm(ks[16], (DEPTH, HG_DV), 0.02),
        "w_out": nrm(ks[17], (DEPTH, MIX_WIDTH, D_MODEL), MIX_WIDTH ** -0.5),
        "norm2_w": 1.0 + nrm(ks[18], (DEPTH, D_MODEL), 0.02),
        "w_router_grp": nrm(ks[19], (DEPTH, D_MODEL, N_GROUPS), D_MODEL ** -0.5),
        "b_router_grp": nrm(ks[20], (DEPTH, N_GROUPS), 0.01),
        "w_router_exp": nrm(ks[21], (DEPTH, D_MODEL, N_EXPERTS), D_MODEL ** -0.5),
        "b_router_exp": nrm(ks[22], (DEPTH, N_EXPERTS), 0.01),
        "w_gate": nrm(ks[23], (DEPTH, N_EXPERTS, D_MODEL, EXPERT_FF), D_MODEL ** -0.5),
        "w_up": nrm(ks[24], (DEPTH, N_EXPERTS, D_MODEL, EXPERT_FF), D_MODEL ** -0.5),
        "w_down": nrm(ks[25], (DEPTH, N_EXPERTS, EXPERT_FF, D_MODEL), EXPERT_FF ** -0.5),
    }

def reference(x_prompt, x_sample, cache_k, cache_v, state_hgrn, page_table, norm1_w, w_in,
              q_norm_w, k_norm_w, lambda_q1, lambda_k1, lambda_q2, lambda_k2, subln_w, hg_lb,
              hg_norm_w, w_out, norm2_w, w_router_grp, b_router_grp, w_router_exp, b_router_exp,
              w_gate, w_up, w_down):
    dec_batch, n_pages = page_table.shape
    past_len = n_pages * cache_k.shape[2]
    lb_all = jnp.cumsum(jax.nn.softmax(hg_lb.astype(jnp.float32), axis=0), axis=0)
    yp, ys = x_prompt, x_sample
    kp, vp, sp, kss, vss, sss = [], [], [], [], [], []
    for l in range(DEPTH):
        w = (norm1_w[l], w_in[l], q_norm_w[l], k_norm_w[l], lambda_q1[l], lambda_k1[l],
             lambda_q2[l], lambda_k2[l], subln_w[l], lb_all[l], hg_norm_w[l], w_out[l], norm2_w[l],
             w_router_grp[l], b_router_grp[l], w_router_exp[l], b_router_exp[l],
             w_gate[l], w_up[l], w_down[l])
        S0p = jnp.zeros((x_prompt.shape[0], HG_HEADS, HG_EXPAND, HG_DV), x_prompt.dtype)
        yp, k_r, v_r, s_r = _layer(yp, S0p, None, None, l, *w)
        past_k = cache_k[l][page_table].reshape(dec_batch, past_len, DA_HEADS, 2, DA_HEAD_DIM)
        past_v = cache_v[l][page_table].reshape(dec_batch, past_len, DA_HEADS, 2 * DA_HEAD_DIM)
        ys, k_s, v_s, s_s = _layer(ys, state_hgrn[l], past_k, past_v, l, *w)
        kp.append(k_r); vp.append(v_r); sp.append(s_r)
        kss.append(k_s); vss.append(v_s); sss.append(s_s)
    y_prompt = yp
    y_sample = ys
    k_prompt = jnp.stack(kp)
    v_prompt = jnp.stack(vp)
    hgrn_prompt = jnp.stack(sp)
    k_sample = jnp.stack(kss)
    v_sample = jnp.stack(vss)
    hgrn_sample = jnp.stack(sss)
    return (y_prompt, y_sample, k_prompt, v_prompt, hgrn_prompt, k_sample, v_sample, hgrn_sample)


_drawn_inputs = setup_inputs


def setup_inputs(seed=0):
    import zlib

    import numpy as np

    out = dict(_drawn_inputs(seed))
    spreads = {}
    factors = {'lambda_q1': 26.814,
     'hg_norm_w': 4.251,
     'b_router_grp': 16.543,
     'b_router_exp': 18.13,
     'q_norm_w': 5.621,
     'lambda_q2': 34.496,
     'subln_w': 6.87,
     'norm2_w': 3.559,
     'lambda_k2': 4.341}
    for name, (base, spread) in spreads.items():
        noise = np.random.default_rng([zlib.crc32(name.encode()), seed]).standard_normal(out[name].shape)
        drawn = base * np.exp(spread * noise) if base else spread * noise
        out[name] = jnp.asarray(drawn.astype(out[name].dtype))
    for name, factor in factors.items():
        out[name] = (out[name] * factor).astype(out[name].dtype)
    return out
```

```python
from contextlib import ExitStack


import concourse.bass as bass
from concourse import mybir

F32 = mybir.dt.float32
I32 = mybir.dt.int32
U8 = mybir.dt.uint8
ALU = mybir.AluOpType
ACT = mybir.ActivationFunctionType
AX = mybir.AxisListType

D = 1024
KD = D // 128
SEQ = 1024
NT = SEQ // 128
DB, DS = 8, 8
NS = DB * DS
TOK = SEQ + NS
TILES = NT + 1
GROUPS = [(0, 384), (384, 384), (768, 320)]
HEADS = 4
PAGE = 128
PAGES = 16
PG = 4
NPG = PAGES // PG
NE, NG, EG = 16, 4, 4
FF = 256
LEVELS = 7
SAMPLE_LEVELS = 3
EPS = 1e-6
NEG = -1e30
LAM_INIT = 0.2
BIG = 3e38
LN_EXP_SET = 6


class Named:
    pass


class Steps:

    def __init__(self, eng, sem):
        self.eng, self.sem, self.n, self.turn, self.per = eng, sem, 0, 0, 0

    def __call__(self, ins):
        ins.then_inc(self.sem, 1)
        self.n += 1

    def wait(self):
        self.eng.wait_ge(self.sem, self.turn * self.per + self.n)

    def begin(self, turn, per):
        self.turn, self.per, self.start = turn, per, self.n

    def end(self, turns):
        assert self.n - self.start == self.per, (self.n - self.start, self.per)
        self.n = self.start + turns * self.per
        self.turn, self.per = 0, 0


def rows(t):
    return 128 if t < NT else NS


def cols(t):
    return slice(t * 128, t * 128 + rows(t))


def build(nc, a, out):
    with ExitStack() as ctx:
        m = Named()
        sb = lambda n, s, dt=F32: ctx.enter_context(nc.sbuf_tensor(n, s, dt))
        m.ident = sb("ident", [128, 128])
        m.ones = sb("ones", [128, 128])
        m.halves = sb("halves", [128, 128])
        m.causal = sb("causal", [128, 128])
        m.eps = sb("eps", [128, 1])
        m.n1w = sb("n1w", [128, KD])
        m.n2w = sb("n2w", [128, KD])
        m.qw = sb("qw", [128, 1])
        m.kw = sb("kw", [128, 1])
        m.subw = sb("subw", [128, 1])
        m.hgw = sb("hgw", [128, 1])
        m.coef = sb("coef", [128, 2])
        m.lb = sb("lb", [128, HEADS])
        m.lb1 = sb("lb1", [128, HEADS])
        m.mixT = sb("mixT", [128, KD, TOK])
        m.xT = sb("xT", [128, KD, TOK])
        m.qbd = sb("qbd", [128, HEADS, DB, 32])
        m.kS = sb("kS", [128, HEADS, NS])
        m.ps = ctx.enter_context(nc.psum_tensor("ps", [128, 8, 512], F32))
        norm_phase(nc, a, m)
        attention_phase(nc, a, out, m)
        hgrn_phase(nc, a, out, m)
        decode_phase(nc, a, out, m)
        with ExitStack() as late:
            m.Y = late.enter_context(nc.sbuf_tensor("Y", [128, TILES, D], F32))
            m.gates = late.enter_context(nc.sbuf_tensor("gates", [128, TILES, NE], F32))
            mix_phase(nc, a, m)
            moe_phase(nc, a, out, m)


def scope(nc, ctx):
    sb = lambda n, s, dt=F32: ctx.enter_context(nc.sbuf_tensor(n, s, dt))
    sem = lambda n: ctx.enter_context(nc.semaphore(n))
    return sb, sem


def load_ln_exp(nc, act):
    act.add_instruction(mybir.InstLoadActFuncSet(name=nc.get_next_instruction_name(), engine=mybir.EngineType.Activation,
                                                 act_func_set_id=LN_EXP_SET, ins=[], outs=[]))


def column(v, n):
    return v.rearrange("(p o) -> p o", o=1)


def norm_phase(nc, a, m):
    with ExitStack() as ctx:
        sb, sem = scope(nc, ctx)
        xb = sb("n_xb", [128, 2, D])
        junk = sb("n_junk", [128, D])
        xs = sb("n_xs", [128, 2, D])
        ss = sb("n_ss", [128, 2])
        rs = sb("n_rs", [128, 2])
        lam = sb("n_lam", [128, 4, 64])
        prod = sb("n_prod", [128, 2, 64])
        dots = sb("n_dots", [128, 2])
        hb = sb("n_hb", [128, 2, HEADS])
        hm = sb("n_hm", [128, HEADS])
        hs = sb("n_hs", [128, HEADS])
        x_in = [sem("n_x_in0"), sem("n_x_in1")]
        w_in = sem("n_w_in")
        xs_ready = sem("n_xs_ready")
        act_step = sem("n_act_step")
        dve_step = sem("n_dve_step")
        pool_step = sem("n_pool_step")
        transposed = sem("n_transposed")
        evacuated = sem("n_evacuated")
        small = sem("n_small")
        small_exp = sem("n_small_exp")
        block = ctx.enter_context(nc.Block())
        xp = a.x_prompt[0, :, :].rearrange("(t p) d -> t p d", p=128)
        SMALL = [(m.n1w[:, :], a.norm1_w[0, :].rearrange("(c p) -> p c", p=128)),
                 (m.n2w[:, :], a.norm2_w[0, :].rearrange("(c p) -> p c", p=128)),
                 (m.qw[0:64, :], column(a.q_norm_w[0, :], 64)),
                 (m.qw[64:128, :], column(a.q_norm_w[0, :], 64)),
                 (m.kw[0:64, :], column(a.k_norm_w[0, :], 64)),
                 (m.kw[64:128, :], column(a.k_norm_w[0, :], 64)),
                 (m.subw[:, :], column(a.subln_w[0, :], 128)),
                 (m.hgw[:, :], column(a.hg_norm_w[0, :], 128)),
                 (hb[:, :, :], a.hg_lb.rearrange("l (h p) -> p l h", p=128))]
        SMALL += [(lam[:, n, :], v[0, :].partition_broadcast(128)) for n, v in
                  enumerate((a.lambda_q1, a.lambda_k1, a.lambda_q2, a.lambda_k2))]

        @block.gpsimd
        def _(pool):
            step = Steps(pool, pool_step)
            for t, v in ((m.ident, 0.0), (m.ones, 1.0 / 128), (m.halves, 0.0), (m.causal, 0.0), (m.eps, EPS)):
                step(pool.memset(t[:, :], v))
            step(pool.memset(m.coef[:, 0:1], 1.0))
            step(pool.memset(m.qbd[:, :, :, :], 0.0))
            step.wait()
            step(pool.affine_select(out=m.ident[:, :], in_=m.ident[:, :], compare_op=ALU.not_equal, fill=1.0,
                                    base=0, pattern=[[-1, 128]], channel_multiplier=1))
            step(pool.affine_select(out=m.causal[:, :], in_=m.causal[:, :], compare_op=ALU.is_ge, fill=NEG,
                                    base=0, pattern=[[-1, 128]], channel_multiplier=1))
            step.wait()
            step(pool.memset(m.halves[0:64, 0:64], 1.0 / 64))
            step.wait()
            step(pool.memset(m.halves[64:128, 64:128], 1.0 / 64))
            step.wait()
        POOL_ALL = 11

        @block.sync
        def _(sp):
            def load(t, u, free):
                if free is not None:
                    sp.wait_ge(xs_ready, free)
                n = 128 if not isinstance(t, int) or t < NT else NS
                src = xp[t, :, :] if n == 128 else a.x_sample.rearrange("b t d -> (b t) d")
                sp.dma_start(xb[0:n, u, :], src).then_inc(x_in[u], 16)
            load(0, 0, None)
            load(1, 1, None)
            with nc.allow_non_contiguous_dma("small weight vectors"):
                for dst, src in SMALL:
                    sp.dma_start(dst, src).then_inc(w_in, 16)
            with sp.Fori(1, NT // 2) as j:
                for u in range(2):
                    load(j * 2 + u, u, j * 2 + u - 1)
            load(NT, 0, NT - 1)

        @block.scalar
        def _(act):
            step = Steps(act, act_step)

            def scale_tile(t, u, n, turn):
                act.wait_ge(x_in[u], turn * 16 + 16)
                step(act.activation(junk[0:n, :], xb[0:n, u, :], ACT.Square, accum_out=ss[0:n, u:u + 1]))
                step.wait()
                step(act.activation(rs[0:n, u:u + 1], ss[0:n, u:u + 1], ACT.Ln, scale=1.0 / D, bias=m.eps[0:n, :]))
                step.wait()
                step(act.activation(rs[0:n, u:u + 1], rs[0:n, u:u + 1], ACT.Exp, scale=-0.5))
                step.wait()
                if not isinstance(t, int) or t >= 2:
                    act.wait_ge(transposed, (t - 1) * 2)
                act.activation(xs[0:n, u, :], xb[0:n, u, :], ACT.Copy, scale=rs[0:n, u:u + 1]).then_inc(xs_ready, 1)
            load_ln_exp(nc, act)
            act.wait_ge(pool_step, POOL_ALL)
            for u in range(2):
                scale_tile(u, u, 128, 0)
            with act.Fori(1, NT // 2) as j:
                step.begin(j - 1, 6)
                for u in range(2):
                    scale_tile(j * 2 + u, u, 128, j)
                step.end(NT // 2 - 1)
            scale_tile(NT, 0, NS, NT // 2)
            act.wait_ge(small, 1)
            act.activation(dots[:, :], dots[:, :], ACT.Exp).then_inc(small_exp, 1)
            act.activation(hb[:, :, :], hb[:, :, :], ACT.Exp).then_inc(small_exp, 1)

        @block.tensor
        def _(pe):
            pe.wait_ge(pool_step, POOL_ALL)

            def transpose_tile(t, u, n):
                pe.wait_ge(xs_ready, t + 1)
                for b in range(2):
                    if not isinstance(t, int) or t >= 2:
                        pe.wait_ge(evacuated, (t - 2) * 2 + b + 1)
                    for c in range(4):
                        k = b * 4 + c
                        last = pe.transpose(m.ps[:, 2 * u + b, c * 128:c * 128 + n],
                                            xs[0:n, u, k * 128:(k + 1) * 128], m.ident[0:n, 0:n])
                    last.then_inc(transposed, 1)
            for u in range(2):
                transpose_tile(u, u, 128)
            with pe.Fori(1, NT // 2) as j:
                for u in range(2):
                    transpose_tile(j * 2 + u, u, 128)
            transpose_tile(NT, 0, NS)

        @block.vector
        def _(dve):
            step = Steps(dve, dve_step)
            dve.wait_ge(w_in, 16 * len(SMALL))
            dve.wait_ge(pool_step, POOL_ALL)
            for n in range(2):
                step(dve.tensor_tensor(prod[:, n, :], lam[:, 2 * n, :], lam[:, 2 * n + 1, :], ALU.mult))
            step(dve.tensor_scalar(m.qw[:, :], m.qw[:, :], 0.125, None, ALU.mult))
            step(dve.tensor_scalar(m.subw[:, :], m.subw[:, :], 1.0 - LAM_INIT, None, ALU.mult))
            step(dve.tensor_tensor(hm[:, :], hb[:, 0, :], hb[:, 1, :], ALU.max))
            step.wait()
            step(dve.tensor_reduce(dots[:, :], prod[:, :, :], AX.X, ALU.add))
            for n in range(2):
                step(dve.tensor_tensor(hb[:, n, :], hb[:, n, :], hm[:, :], ALU.subtract))
            step.wait()
            dve.sem_inc(small, 1)

            def evacuate(t, u, n):
                for b in range(2):
                    dve.wait_ge(transposed, t * 2 + b + 1)
                    o = m.xT[:, 4 * b:4 * b + 4, bass.ds(t * 128, n)]
                    i = m.ps[:, 2 * u + b, :].rearrange("p (c n) -> p c n", c=4)[:, :, 0:n]
                    w = m.n1w[:, 4 * b:4 * b + 4].unsqueeze(2).to_broadcast([128, 4, n])
                    dve.tensor_tensor(o, i, w, ALU.mult).then_inc(evacuated, 1)
            with dve.Fori(0, NT // 2) as j:
                for u in range(2):
                    evacuate(j * 2 + u, u, 128)
            evacuate(NT, 0, NS)
            dve.wait_ge(small_exp, 2)
            step(dve.tensor_tensor(prod[:, 0, 0:1], dots[:, 1:2], dots[:, 0:1], ALU.subtract))
            step(dve.tensor_tensor(hs[:, :], hb[:, 0, :], hb[:, 1, :], ALU.add))
            step.wait()
            step(dve.tensor_scalar(m.coef[:, 1:2], prod[:, 0, 0:1], LAM_INIT, None, ALU.subtract))
            step(dve.reciprocal(hm[:, :], hs[:, :]))
            step.wait()
            step(dve.tensor_tensor(m.lb[:, :], hb[:, 0, :], hm[:, :], ALU.mult))
            step.wait()
            step(dve.tensor_scalar(m.lb1[:, :], m.lb[:, :], -1.0, 1.0, ALU.mult, ALU.add))
            step.wait()


def attention_phase(nc, a, out, m):
    w_in_d = a.w_in[0, :, :].rearrange("(k p) c -> p k c", p=128)
    with ExitStack() as ctx:
        sb, sem = scope(nc, ctx)
        wq, wk, wv = (sb(f"a_{n}", [128, KD, 128]) for n in ("wq", "wk", "wv"))
        zq, zk, sq, sk, rq, rk, qT, kT = (sb(f"a_{n}", [128, TOK]) for n in
                                         ("zq", "zk", "sq", "sk", "rq", "rk", "qT", "kT"))
        v = sb("a_v", [128, TILES, 128])
        kt = sb("a_kt", [128, TILES, 128])
        P = sb("a_P", [128, 2, SEQ])
        A = sb("a_A", [128, SEQ])
        AT = sb("a_AT", [128, SEQ])
        oT = sb("a_oT", [128, SEQ])
        so = sb("a_so", [128, SEQ])
        ro = sb("a_ro", [128, SEQ])
        nmx = sb("a_nmx", [128, 2])
        l = sb("a_l", [128, 2])
        r = sb("a_r", [128, 2])
        w_in = [sem(f"a_w_in{n}") for n in "qkv"]
        projected = [sem(f"a_projected_{n}") for n in "qkv"]
        v8_done = sem("a_v8_projected")
        squared = [sem("a_squared_q"), sem("a_squared_k")]
        meaned = [sem("a_meaned_q"), sem("a_meaned_k")]
        ms_read = [sem("a_ms_read_q"), sem("a_ms_read_k")]
        r_ready = [sem("a_rq_ready"), sem("a_rk_ready")]
        q_ready, k_ready, v_ready = sem("a_q_ready"), sem("a_k_ready"), sem("a_v_ready")
        kt_done, kt_ready = sem("a_kt_done"), sem("a_kt_ready")
        stored = sem("a_stored")
        saved = sem("a_saved")
        scored, max_ready, exp_done = sem("a_scored"), sem("a_max_ready"), sem("a_exp_done")
        a_ready, at_done, at_ready, av_done = sem("a_a_ready"), sem("a_at_done"), sem("a_at_ready"), sem("a_av_done")
        o_squared, o_meaned, o_read, ro_ready = (sem(n) for n in ("a_o_squared", "a_o_meaned", "a_o_read", "a_ro_ready"))
        head_done = sem("a_head_done")
        act_step, dve_step = sem("a_act_step"), sem("a_dve_step")
        block = ctx.enter_context(nc.Block())
        flat = m.ps[:, :, :].rearrange("p b n -> p (b n)")

        @block.sync
        def _(sp):
            kp = out.k_prompt[0, 0, :, :, :].rearrange("(t p) h e -> h p t e", p=128)
            vp = out.v_prompt[0, 0, :, :, :].rearrange("(t p) h e -> h p t e", p=128)
            ks = out.k_sample[0, :, :, :, :].rearrange("b t h e -> h (b t) e")
            vs = out.v_sample[0, :, :, :, :].rearrange("b t h e -> h (b t) e")
            sp.sem_inc(stored, 1)
            with sp.Fori(0, HEADS) as h:
                for n, w in enumerate((wq, wk, wv)):
                    sp.wait_ge(projected[n] if n < 2 else v8_done, h + 1)
                    sp.dma_start(w[:, :, :], w_in_d[:, :, bass.ds(h * 128 + n * 512, 128)]).then_inc(w_in[n], 16)
                sp.wait_ge(v_ready, h + 1)
                sp.dma_start(vp[h, :, :, :], v[:, 0:NT, :]).then_inc(stored, 16)
                sp.dma_start(vs[h, :, :], v[0:NS, NT, :]).then_inc(stored, 16)
                sp.wait_ge(kt_ready, h + 1)
                sp.dma_start(kp[h, :, :, :], kt[:, 0:NT, :]).then_inc(stored, 16)
                sp.dma_start(ks[h, :, :], kt[0:NS, NT, :]).then_inc(stored, 16)
            sp.wait_ge(stored, 64 * HEADS + 1)

        @block.gpsimd
        def _(pool):
            pool.sem_inc(saved, 1)
            with pool.Fori(0, HEADS) as h:
                pool.wait_ge(q_ready, h + 1)
                for mm in range(2):
                    o = m.qbd[64 * mm:64 * mm + 64, h, :, 8 * mm:8 * mm + 8]
                    i = qT[64 * mm:64 * mm + 64, SEQ:TOK].rearrange("p (b t) -> p b t", b=DB)
                    pool.tensor_copy(o, i).then_inc(saved, 1)
                    pool.wait_ge(saved, h * 3 + mm + 1 + 1)
                pool.wait_ge(k_ready, h + 1)
                pool.tensor_copy(m.kS[:, h, :], kT[:, SEQ:TOK]).then_inc(saved, 1)
                pool.wait_ge(saved, h * 3 + 3 + 1)

        @block.tensor
        def _(pe):
            def project(n, w, banks):
                for (c0, w0), b in zip(GROUPS, banks):
                    for k in range(KD):
                        last = pe.matmul(m.ps[:, b, 0:w0], w[:, k, :], m.xT[:, k, c0:c0 + w0],
                                         start=(k == 0), stop=(k == KD - 1))
                last.then_inc(projected[n], 1)

            def project_v(t, b, o):
                n = rows(t)
                for k in range(KD):
                    last = pe.matmul(m.ps[0:n, b, o:o + 128], m.xT[:, k, cols(t)], wv[:, k, :],
                                     start=(k == 0), stop=(k == KD - 1))
                return last

            def mean(n, s, banks):
                for (c0, w0), b in zip(GROUPS, banks):
                    last = pe.matmul(m.ps[:, b, 0:w0], m.halves[:, :], s[:, c0:c0 + w0], start=True, stop=True)
                last.then_inc(meaned[n], 1)

            for s in (*projected, v8_done, at_done):
                pe.sem_inc(s, 1)
            with pe.Fori(0, HEADS) as h:
                pe.wait_ge(w_in[0], h * 16 + 16)
                pe.wait_ge(o_read, h + 1)
                project(0, wq, (0, 1, 2))
                pe.wait_ge(w_in[1], h * 16 + 16)
                project(1, wk, (3, 4, 5))
                pe.wait_ge(squared[0], h + 1)
                mean(0, sq, (0, 1, 2))
                pe.wait_ge(w_in[2], h * 16 + 16)
                for t in range(NT):
                    last = project_v(t, 6 + t // 4, t % 4 * 128)
                last.then_inc(projected[2], 1)
                pe.wait_ge(squared[1], h + 1)
                mean(1, sk, (3, 4, 5))
                pe.wait_ge(ms_read[0], h + 1)
                project_v(NT, 0, 0).then_inc(v8_done, 1)
                pe.wait_ge(k_ready, h + 1)
                for t in range(TILES):
                    last = pe.transpose(m.ps[0:rows(t), 3 + t // 4, t % 4 * 128:t % 4 * 128 + 128],
                                        kT[:, cols(t)], m.ident[:, :])
                last.then_inc(kt_done, 1)
                pe.wait_ge(kt_ready, h + 1)

                def score(i):
                    L = (i + 1) * 128
                    for mm in range(2):
                        if i:
                            pe.wait_ge(exp_done, h * 16 + 2 * i - 1 + mm)
                        for c in range(0, L, 512):
                            w0 = min(512, L - c)
                            last = pe.matmul(m.ps[:, 2 * mm + c // 512, 0:w0],
                                             qT[64 * mm:64 * mm + 64, i * 128:i * 128 + 128],
                                             kT[64 * mm:64 * mm + 64, c:c + w0], start=True, stop=True)
                        last.then_inc(scored, 1)
                score(0)
                for i in range(NT):
                    if i + 1 < NT:
                        score(i + 1)
                    pe.wait_ge(a_ready, h * NT + i + 1)
                    if i:
                        pe.wait_ge(at_ready, h * NT + i)
                    for j in range(i + 1):
                        last = pe.transpose(flat[:, 2048 + j * 128:2048 + j * 128 + 128],
                                            A[:, j * 128:j * 128 + 128], m.ident[:, :])
                    last.then_inc(at_done, 1)
                    pe.wait_ge(at_ready, h * NT + i + 1)
                    for j in range(i + 1):
                        last = pe.matmul(flat[:, 3072 + i * 128:3072 + i * 128 + 128], v[:, j, :],
                                         AT[:, j * 128:j * 128 + 128], start=(j == 0), stop=(j == i))
                    last.then_inc(av_done, 1)
                pe.wait_ge(o_squared, h + 1)
                for g in range(2):
                    last = pe.matmul(m.ps[:, g, :], m.ones[:, :], so[:, g * 512:g * 512 + 512], start=True, stop=True)
                last.then_inc(o_meaned, 1)

        @block.scalar
        def _(act):
            step = Steps(act, act_step)
            act.sem_inc(o_read, 1)
            load_ln_exp(nc, act)
            with act.Fori(0, HEADS) as h:
                step.begin(h, 2)
                for n, (z, s, banks) in enumerate(((zq, sq, (0, 1, 2)), (zk, sk, (3, 4, 5)))):
                    act.wait_ge(projected[n], h + 1 + 1)
                    for (c0, w0), b in zip(GROUPS, banks):
                        act.activation(z[:, c0:c0 + w0], m.ps[:, b, 0:w0], ACT.Copy)
                        last = act.activation(s[:, c0:c0 + w0], m.ps[:, b, 0:w0], ACT.Square)
                    last.then_inc(squared[n], 1)
                for n, (rr, banks) in enumerate(((rq, (0, 1, 2)), (rk, (3, 4, 5)))):
                    act.wait_ge(meaned[n], h + 1)
                    for (c0, w0), b in zip(GROUPS, banks):
                        last = act.activation(rr[:, c0:c0 + w0], m.ps[:, b, 0:w0], ACT.Ln, bias=m.eps[:, :])
                    last.then_inc(ms_read[n], 1)
                    act.wait_ge(ms_read[n], h + 1)
                    act.activation(rr[:, :], rr[:, :], ACT.Exp, scale=-0.5).then_inc(r_ready[n], 1)

                def exps(i):
                    L = (i + 1) * 128
                    for mm in range(2):
                        act.wait_ge(max_ready, h * 16 + 2 * i + mm + 1)
                        act.activation(P[:, mm, 0:L], flat[:, 1024 * mm:1024 * mm + L], ACT.Exp,
                                       bias=nmx[:, mm:mm + 1], accum_out=l[:, mm:mm + 1]).then_inc(exp_done, 1)
                exps(0)
                for i in range(NT):
                    act.wait_ge(at_done, h * NT + i + 1 + 1)
                    L = (i + 1) * 128
                    act.activation(AT[:, 0:L], flat[:, 2048:2048 + L], ACT.Copy).then_inc(at_ready, 1)
                    if i + 1 < NT:
                        exps(i + 1)
                act.wait_ge(av_done, h * NT + NT)
                act.wait_ge(head_done, h + 1)
                for g in range(2):
                    step(act.activation(oT[:, g * 512:g * 512 + 512], m.ps[:, 6 + g, :], ACT.Copy))
                    last = act.activation(so[:, g * 512:g * 512 + 512], m.ps[:, 6 + g, :], ACT.Square)
                last.then_inc(o_squared, 1)
                act.wait_ge(o_meaned, h + 1)
                for g in range(2):
                    last = act.activation(ro[:, g * 512:g * 512 + 512], m.ps[:, g, :], ACT.Ln, bias=m.eps[:, :])
                last.then_inc(o_read, 1)
                act.wait_ge(o_read, h + 1 + 1)
                act.activation(ro[:, :], ro[:, :], ACT.Exp, scale=-0.5).then_inc(ro_ready, 1)
                step.end(HEADS)

        @block.vector
        def _(dve):
            step = Steps(dve, dve_step)
            dve.sem_inc(head_done, 1)
            with dve.Fori(0, HEADS) as h:
                step.begin(h, 44)
                dve.wait_ge(r_ready[0], h + 1)
                dve.wait_ge(saved, h * 3 + 1)
                dve.scalar_tensor_tensor(qT[:, :], zq[:, :], m.qw[:, :], rq[:, :], ALU.mult, ALU.mult).then_inc(q_ready, 1)
                dve.wait_ge(projected[2], h + 1 + 1)
                dve.wait_ge(stored, h * 64 + 1)
                for g in range(2):
                    step(dve.tensor_copy(v[:, 4 * g:4 * g + 4, :], m.ps[:, 6 + g, :].rearrange("p (t e) -> p t e", t=4)))
                dve.wait_ge(r_ready[1], h + 1)
                dve.scalar_tensor_tensor(kT[:, :], zk[:, :], m.kw[:, :], rk[:, :], ALU.mult, ALU.mult).then_inc(k_ready, 1)
                dve.wait_ge(v8_done, h + 1 + 1)
                dve.tensor_copy(v[0:NS, NT, :], m.ps[0:NS, 0, 0:128]).then_inc(v_ready, 1)
                dve.wait_ge(kt_done, h + 1)
                for g in range(2):
                    step(dve.tensor_copy(kt[:, 4 * g:4 * g + 4, :], m.ps[:, 3 + g, :].rearrange("p (t e) -> p t e", t=4)))
                dve.tensor_copy(kt[0:NS, NT, :], m.ps[0:NS, 5, 0:128]).then_inc(kt_ready, 1)

                def maxes(i):
                    L = (i + 1) * 128
                    for mm in range(2):
                        dve.wait_ge(scored, h * 16 + 2 * i + mm + 1)
                        d = flat[:, 1024 * mm + L - 128:1024 * mm + L]
                        step(dve.tensor_tensor(d, d, m.causal[:, :], ALU.add))
                        step.wait()
                        dve.tensor_reduce(nmx[:, mm:mm + 1], flat[:, 1024 * mm:1024 * mm + L], AX.X, ALU.max,
                                          negate=True).then_inc(max_ready, 1)
                maxes(0)
                for i in range(NT):
                    L = (i + 1) * 128
                    dve.wait_ge(exp_done, h * 16 + 2 * i + 2)
                    step(dve.reciprocal(r[:, :], l[:, :]))
                    step.wait()
                    step(dve.tensor_tensor(r[:, :], r[:, :], m.coef[:, :], ALU.mult))
                    step.wait()
                    dve.wait_ge(at_done, h * NT + i + 1)
                    step(dve.tensor_scalar(A[:, 0:L], P[:, 0, 0:L], r[:, 0:1], None, ALU.mult))
                    step.wait()
                    dve.scalar_tensor_tensor(A[:, 0:L], P[:, 1, 0:L], r[:, 1:2], A[:, 0:L],
                                             ALU.mult, ALU.add).then_inc(a_ready, 1)
                    if i + 1 < NT:
                        maxes(i + 1)
                dve.wait_ge(ro_ready, h + 1)
                dve.scalar_tensor_tensor(m.mixT[:, h, 0:SEQ], oT[:, :], m.subw[:, :], ro[:, :],
                                         ALU.mult, ALU.mult).then_inc(head_done, 1)
                step.end(HEADS)


def hgrn_phase(nc, a, out, m):
    w_in_d = a.w_in[0, :, :].rearrange("(k p) c -> p k c", p=128)
    NL = LEVELS + 1
    SL = list(range(SAMPLE_LEVELS)) + [LEVELS]
    ORDER = ("f", "q", "v", "g")
    FIRST = {"q": 1536, "f": 2048, "v": 2560, "g": 3072}
    with ExitStack() as ctx:
        sb, sem = scope(nc, ctx)
        w = {n: sb(f"h_w{n}", [128, KD, 128]) for n in ORDER}
        si = sb("h_si", [128, 128], I32)
        ti = sb("h_ti", [128, 128], I32)
        xi = sb("h_xi", [128, 128], I32)
        sh = sb("h_sh", [128, 128], I32)
        gt = sb("h_gt", [128, 128], I32)
        mask = sb("h_mask", [128, NL, 128], U8)
        bmask = sb("h_bmask", [NS, DB])
        keep = sb("h_keep", [128, TOK])
        sg, q, g, f, kk, lf, b, eb, qe, kd, oT, so, ro = (sb(f"h_{n}", [128, TOK]) for n in (
            "sg", "q", "g", "f", "kk", "lf", "b", "eb", "qe", "kd", "oT", "so", "ro"))
        E = sb("h_E", [128, 2, TOK])
        X = sb("h_X", [128, 2, TOK])
        AT = sb("h_AT", [128, TILES, 128])
        v = sb("h_v", [128, TILES, 128])
        ket = sb("h_ket", [128, TILES, 128])
        eB = sb("h_eB", [128, NT + DB])
        S = sb("h_S", [128, NT + 1, 128])
        Ss = sb("h_Ss", [128, DB, 128])
        Sn = sb("h_Sn", [128, DB, 128])
        vblk = sb("h_vblk", [NS, DB, 128])
        w_in = {n: sem(f"h_w_in_{n}") for n in ORDER}
        projected = {n: sem(f"h_projected_{n}") for n in ORDER}
        v8_done = sem("h_v8_done")
        sig = {n: sem(f"h_sigmoid_{n}") for n in ("f", "q", "g")}
        s_in, stored = sem("h_s_in"), sem("h_stored")
        f_ready, lf_ready, b_ready, q_ready, g_ready, v_ready, v8_ready = (sem(f"h_{n}_ready") for n in (
            "f", "lf", "b", "q", "g", "v", "v8"))
        sub_done, exp_done, x_ready, level_done, level_read = (sem(f"h_{n}") for n in (
            "sub_done", "exp_done", "x_ready", "level_done", "level_read"))
        kd_sub, kd_exp, eb_ready, ke_ready, qe_ready = (sem(f"h_{n}") for n in (
            "kd_sub", "kd_exp", "eb_ready", "ke_ready", "qe_ready"))
        ket_done, ket_ready, u_done, us_done, s_ready = (sem(f"h_{n}") for n in (
            "ket_done", "ket_ready", "u_done", "us_done", "s_ready"))
        at_zero, o_done, o_squared, o_meaned, o_read, ro_ready, head_done = (sem(f"h_{n}") for n in (
            "at_zero", "o_done", "o_squared", "o_meaned", "o_read", "ro_ready", "head_done"))
        gate, gate_pool = sem("h_gate"), sem("h_gate_pool")
        mixed = sem("h_mixed")
        iota_done, setup_step, dve_step = sem("h_iota_done"), sem("h_setup_step"), sem("h_dve_step")
        block = ctx.enter_context(nc.Block())
        flat = m.ps[:, :, :].rearrange("p b n -> p (b n)")

        def halves(t, lv):
            c = 1 << lv
            wd = TOK if lv < SAMPLE_LEVELS else SEQ
            x = t[:, 0:wd].rearrange("p (n two c) -> p n two c", two=2, c=c)
            n = wd // (2 * c)
            return x[:, :, 0, :], x[:, :, 1, :], x[:, :, 0, c - 1:c].to_broadcast([128, n, c])

        @block.sync
        def _(sp):
            state = a.state_hgrn[0, :, :, :, :].rearrange("b h k v -> h k b v")
            new = out.hgrn_sample[0, :, :, :, :].rearrange("b h k v -> h k b v")
            sp.sem_inc(stored, 1)
            with sp.Fori(0, HEADS) as h:
                for n in ORDER:
                    sp.wait_ge(v8_done if n == "v" else projected[n], h + 1)
                    sp.dma_start(w[n][:, :, :], w_in_d[:, :, bass.ds(h * 128 + FIRST[n], 128)]).then_inc(w_in[n], 16)
                sp.wait_ge(head_done, h + 1)
                sp.dma_start(Ss[:, :, :], state[h, :, :, :]).then_inc(s_in, 16)
                sp.wait_ge(s_ready, h * 2 + 2)
                sp.dma_start(out.hgrn_prompt[0, 0, h, :, :], S[:, NT, :]).then_inc(stored, 16)
                sp.dma_start(new[h, :, :, :], Sn[:, :, :]).then_inc(stored, 16)
            sp.wait_ge(stored, 32 * HEADS + 1)

        @block.gpsimd
        def _(pool):
            pool.iota(si[:, :], [[0, 128]], base=0, channel_multiplier=1).then_inc(iota_done, 1)
            pool.iota(ti[:, :], [[1, 128]], base=0, channel_multiplier=0).then_inc(iota_done, 1)
            pool.memset(S[:, 0, :], 0.0).then_inc(iota_done, 1)
            pool.memset(keep[:, :], 1.0).then_inc(iota_done, 1)
            pool.wait_ge(iota_done, 4)
            pool.memset(keep[:, 0:SEQ].rearrange("p (n c) -> p n c", c=128)[:, :, 0:1], 0.0).then_inc(iota_done, 1)
            pool.memset(keep[:, SEQ:TOK].rearrange("p (n c) -> p n c", c=DS)[:, :, 0:1], 0.0).then_inc(iota_done, 1)
            with pool.Fori(0, HEADS) as h:
                pool.wait_ge(o_done, h + 1)
                pool.sem_inc(gate_pool, 1)
                pool.memset(AT[:, :, :], 0.0).then_inc(at_zero, 1)
                pool.wait_ge(kd_exp, h + 1)
                pool.tensor_tensor(kd[:, :], kd[:, :], kk[:, :], ALU.mult).then_inc(ke_ready, 1)
                pool.wait_ge(q_ready, h + 1)
                pool.wait_ge(eb_ready, h + 1)
                pool.tensor_tensor(qe[:, :], eb[:, :], q[:, :], ALU.mult).then_inc(qe_ready, 1)
                for lv in range(LEVELS):
                    u = lv % 2
                    pool.wait_ge(exp_done, h * LEVELS + lv + 1)
                    if lv >= 2:
                        pool.wait_ge(level_done, h * NL + lv - 1)
                    ke, _, _ = halves(kk, lv)
                    _, qo, _ = halves(q, lv)
                    ee, eo, _ = halves(E[:, u, :], lv)
                    xe, xo, _ = halves(X[:, u, :], lv)
                    pool.tensor_tensor(xe, ee, ke, ALU.mult)
                    pool.tensor_tensor(xo, eo, qo, ALU.mult).then_inc(x_ready, 1)

        @block.tensor
        def _(pe):
            def project(n, banks):
                for (c0, w0), bk in zip(GROUPS, banks):
                    for k in range(KD):
                        last = pe.matmul(m.ps[:, bk, 0:w0], w[n][:, k, :], m.xT[:, k, c0:c0 + w0],
                                         start=(k == 0), stop=(k == KD - 1))
                last.then_inc(projected[n], 1)

            def project_v(t, bk, o):
                for k in range(KD):
                    last = pe.matmul(m.ps[0:rows(t), bk, o:o + 128], m.xT[:, k, cols(t)], w["v"][:, k, :],
                                     start=(k == 0), stop=(k == KD - 1))
                return last

            for s in (*projected.values(), v8_done, o_done):
                pe.sem_inc(s, 1)
            with pe.Fori(0, HEADS) as h:
                pe.wait_ge(o_read, h + 1)
                pe.wait_ge(w_in["f"], h * 16 + 16)
                project("f", (0, 1, 2))
                pe.wait_ge(w_in["q"], h * 16 + 16)
                project("q", (3, 4, 5))
                pe.wait_ge(w_in["v"], h * 16 + 16)
                for t in range(NT):
                    last = project_v(t, 6 + t // 4, t % 4 * 128)
                last.then_inc(projected["v"], 1)
                pe.wait_ge(w_in["g"], h * 16 + 16)
                pe.wait_ge(sig["f"], h + 1)
                project("g", (0, 1, 2))
                pe.wait_ge(q_ready, h + 1)
                project_v(NT, 3, 0).then_inc(v8_done, 1)
                pe.wait_ge(ke_ready, h + 1)
                pe.wait_ge(v_ready, h + 1)
                for t in range(TILES):
                    last = pe.transpose(flat[0:rows(t), (3072 + t * 128 if t < NT else 2560):(3200 + t * 128 if t < NT else 2688)],
                                        kd[:, cols(t)], m.ident[:, :])
                last.then_inc(ket_done, 1)
                pe.wait_ge(g_ready, h + 1)
                pe.wait_ge(v8_ready, h + 1)
                pe.wait_ge(ket_ready, h + 1)
                for t in range(NT):
                    last = pe.matmul(flat[:, 3072 + t * 128:3200 + t * 128], ket[:, t, :], v[:, t, :], start=True, stop=True)
                last.then_inc(u_done, 1)
                for lv in range(NL):
                    u = lv % 2
                    if lv < LEVELS:
                        pe.wait_ge(x_ready, h * LEVELS + lv + 1)
                        left = right = X[:, u, :]
                    else:
                        left, right = kk, q
                    if lv >= 2:
                        pe.wait_ge(level_read, h * NL + lv - 1)
                    for t in range(NT):
                        last = pe.matmul(flat[:, 1024 * u + t * 128:1024 * u + t * 128 + 128],
                                         left[:, cols(t)], right[:, cols(t)], start=True, stop=True)
                    if lv in SL:
                        last = pe.matmul(m.ps[0:NS, 4 + u, 0:NS], left[:, cols(NT)], right[:, cols(NT)], start=True, stop=True)
                    last.then_inc(level_done, 1)
                pe.wait_ge(level_read, h * NL + NL)
                for n in range(2):
                    last = pe.matmul(m.ps[:, 4 + n, :], ket[0:NS, NT, :],
                                     vblk[:, 4 * n:4 * n + 4, :].rearrange("p b e -> p (b e)"), start=True, stop=True)
                last.then_inc(us_done, 1)
                pe.wait_ge(s_ready, h * 2 + 1)
                pe.wait_ge(s_in, h * 16 + 16)
                for t in range(NT):
                    o = flat[:, t * 128:t * 128 + 128]
                    pe.matmul(o, S[:, t, :], qe[:, cols(t)], start=True, stop=False)
                    pe.matmul(o, v[:, t, :], AT[:, t, :], start=False, stop=True)
                for n in range(DB):
                    pe.matmul(m.ps[:, 2, n * DS:n * DS + DS], Ss[:, n, :], qe[:, SEQ + n * DS:SEQ + n * DS + DS],
                              start=(n == 0), stop=False, skip_group_check=True)
                last = pe.matmul(m.ps[:, 2, 0:NS], v[0:NS, NT, :], AT[0:NS, NT, 0:NS], start=False, stop=True,
                                 skip_group_check=True)
                last.then_inc(o_done, 1)
                pe.wait_ge(o_squared, h + 1)
                for o, s0, n0 in ((3 * 512, 0, 512), (6 * 512, 512, 512), (7 * 512, 1024, NS)):
                    last = pe.matmul(flat[:, o:o + n0], m.ones[:, :], so[:, s0:s0 + n0], start=True, stop=True)
                last.then_inc(o_meaned, 1)

        @block.scalar
        def _(act):
            OG = ((0, 0, 512), (1, 512, 512), (2, 1024, NS))
            act.sem_inc(o_read, 1)
            with act.Fori(0, HEADS) as h:
                for n, banks in (("f", (0, 1, 2)), ("q", (3, 4, 5)), ("g", (0, 1, 2))):
                    act.wait_ge(projected[n], h + 1 + 1)
                    if n == "g":
                        act.wait_ge(mixed, h + 1)
                    dst = {"f": f, "q": q, "g": g}[n]
                    for (c0, w0), bk in zip(GROUPS, banks):
                        last = act.activation(dst[:, c0:c0 + w0], m.ps[:, bk, 0:w0], ACT.Sigmoid)
                    last.then_inc(sig[n], 1)
                load_ln_exp(nc, act)
                act.wait_ge(f_ready, h + 1)
                act.activation(lf[:, :], f[:, :], ACT.Ln).then_inc(lf_ready, 1)
                act.wait_ge(b_ready, h + 1)
                bp = b[:, 0:SEQ].rearrange("p (n c) -> p n c", c=128)[:, :, 127:128]
                bs = b[:, SEQ:TOK].rearrange("p (n c) -> p n c", c=DS)[:, :, DS - 1:DS]
                act.activation(eB[:, 0:NT].unsqueeze(2), bp, ACT.Exp)
                act.activation(eB[:, NT:NT + DB].unsqueeze(2), bs, ACT.Exp)
                act.activation(eb[:, :], b[:, :], ACT.Exp).then_inc(eb_ready, 1)
                act.wait_ge(kd_sub, h + 1)
                act.activation(kd[:, :], kd[:, :], ACT.Exp).then_inc(kd_exp, 1)
                for lv in range(LEVELS):
                    wd = TOK if lv < SAMPLE_LEVELS else SEQ
                    act.wait_ge(sub_done, h * LEVELS + lv + 1)
                    act.activation(E[:, lv % 2, 0:wd], E[:, lv % 2, 0:wd], ACT.Exp).then_inc(exp_done, 1)
                act.wait_ge(o_done, h + 1 + 1)
                act.wait_ge(head_done, h + 1)
                for bk, s0, n0 in OG:
                    act.activation(oT[:, s0:s0 + n0], m.ps[:, bk, 0:n0], ACT.Copy)
                    last = act.activation(so[:, s0:s0 + n0], m.ps[:, bk, 0:n0], ACT.Square)
                last.then_inc(o_squared, 1)
                act.wait_ge(o_meaned, h + 1)
                for bk, (_, s0, n0) in zip((3, 6, 7), OG):
                    last = act.activation(ro[:, s0:s0 + n0], m.ps[:, bk, 0:n0], ACT.Ln, bias=m.eps[:, :])
                last.then_inc(o_read, 1)
                act.wait_ge(o_read, h + 1 + 1)
                act.activation(ro[:, :], ro[:, :], ACT.Exp, scale=-0.5).then_inc(ro_ready, 1)

        @block.vector
        def _(dve):
            setup = Steps(dve, setup_step)
            dve.wait_ge(iota_done, 6)
            setup(dve.tensor_tensor(xi[:, :], si[:, :], ti[:, :], ALU.bitwise_xor))
            setup(dve.tensor_tensor(gt[:, :], ti[:, :], si[:, :], ALU.is_gt))
            setup(dve.tensor_tensor(mask[:, LEVELS, :], ti[:, :], si[:, :], ALU.is_equal))
            setup.wait()
            setup(dve.tensor_scalar(sh[:, :], si[:, :], 3, None, ALU.logical_shift_right))
            setup.wait()
            setup(dve.tensor_tensor(bmask[:, :], sh[0:NS, 0:DB], ti[0:NS, 0:DB], ALU.is_equal))
            setup.wait()
            for lv in range(LEVELS):
                setup(dve.tensor_scalar(sh[:, :], xi[:, :], lv, None, ALU.logical_shift_right))
                setup.wait()
                setup(dve.scalar_tensor_tensor(mask[:, lv, :], sh[:, :], 1, gt[:, :], ALU.is_equal, ALU.mult))
                setup.wait()
            step = Steps(dve, dve_step)
            dve.sem_inc(head_done, 1)
            dve.sem_inc(mixed, 1)
            with dve.Fori(0, HEADS) as h:
                step.begin(h, 19)
                dve.wait_ge(sig["f"], h + 1)
                step(dve.tensor_scalar(f[:, :], f[:, :], m.lb1[:, bass.ds(h, 1)], m.lb[:, bass.ds(h, 1)], ALU.mult, ALU.add))
                step.wait()
                dve.sem_inc(f_ready, 1)
                step(dve.tensor_scalar(kk[:, :], f[:, :], -1.0, 1.0, ALU.mult, ALU.add))
                dve.wait_ge(lf_ready, h + 1)
                dve.tensor_tensor_scan(b[:, :], keep[:, :], lf[:, :], 0.0, ALU.mult, ALU.add).then_inc(b_ready, 1)
                dve.wait_ge(b_ready, h + 1)
                for c0, c1, c in ((0, SEQ, 128), (SEQ, TOK, DS)):
                    bv = b[:, c0:c1].rearrange("p (n c) -> p n c", c=c)
                    kv = kd[:, c0:c1].rearrange("p (n c) -> p n c", c=c)
                    last = dve.tensor_tensor(kv, bv[:, :, c - 1:c].to_broadcast([128, (c1 - c0) // c, c]), bv, ALU.subtract)
                last.then_inc(kd_sub, 1)

                def subs(lv):
                    if lv >= 2:
                        dve.wait_ge(x_ready, h * LEVELS + lv - 1)
                    be, bo, br = halves(b, lv)
                    ee, eo, _ = halves(E[:, lv % 2, :], lv)
                    dve.tensor_tensor(ee, br, be, ALU.subtract)
                    dve.tensor_tensor(eo, bo, br, ALU.subtract).then_inc(sub_done, 1)

                def collect(lv):
                    dve.wait_ge(level_done, h * NL + lv + 1)
                    if lv:
                        dve.wait_ge(level_read, h * NL + lv)
                    dve.sem_inc(gate, 1)
                    u = lv % 2
                    mk = mask[:, lv, :].unsqueeze(1).to_broadcast([128, 4, 128])
                    for g2 in range(2):
                        last = dve.copy_predicated(AT[:, 4 * g2:4 * g2 + 4, :], mk,
                                                   m.ps[:, 2 * u + g2, :].rearrange("p (t n) -> p t n", t=4))
                    if lv in SL:
                        last = dve.copy_predicated(AT[0:NS, NT, 0:NS], mask[0:NS, lv, 0:NS], m.ps[0:NS, 4 + u, 0:NS])
                    last.then_inc(level_read, 1)

                subs(0)
                subs(1)
                dve.wait_ge(sig["q"], h + 1)
                for (c0, w0), bk in zip(GROUPS, (3, 4, 5)):
                    last = dve.tensor_tensor(q[:, c0:c0 + w0], q[:, c0:c0 + w0], m.ps[:, bk, 0:w0], ALU.mult)
                last.then_inc(q_ready, 1)
                dve.wait_ge(projected["v"], h + 1 + 1)
                for n in range(2):
                    last = dve.tensor_copy(v[:, 4 * n:4 * n + 4, :], m.ps[:, 6 + n, :].rearrange("p (t e) -> p t e", t=4))
                last.then_inc(v_ready, 1)
                dve.wait_ge(sig["g"], h + 1)
                for (c0, w0), bk in zip(GROUPS, (0, 1, 2)):
                    last = dve.tensor_tensor(g[:, c0:c0 + w0], g[:, c0:c0 + w0], m.ps[:, bk, 0:w0], ALU.mult)
                last.then_inc(g_ready, 1)
                dve.wait_ge(v8_done, h + 1 + 1)
                step(dve.tensor_copy(v[0:NS, NT, :], m.ps[0:NS, 3, 0:128]))
                step.wait()
                dve.tensor_tensor(vblk[:, :, :], v[0:NS, NT, :].unsqueeze(1).to_broadcast([NS, DB, 128]),
                                  bmask[:, :].unsqueeze(2).to_broadcast([NS, DB, 128]), ALU.mult).then_inc(v8_ready, 1)
                dve.wait_ge(ket_done, h + 1)
                for n in range(2):
                    dve.tensor_copy(ket[:, 4 * n:4 * n + 4, :], m.ps[:, 6 + n, :].rearrange("p (t e) -> p t e", t=4))
                dve.tensor_copy(ket[0:NS, NT, :], m.ps[0:NS, 5, 0:128]).then_inc(ket_ready, 1)
                dve.wait_ge(at_zero, h + 1)
                collect(0)
                subs(2)
                dve.wait_ge(eb_ready, h + 1)
                dve.wait_ge(u_done, h + 1)
                dve.wait_ge(stored, h * 32 + 1)
                for t in range(NT):
                    ins = dve.scalar_tensor_tensor(S[:, t + 1, :], S[:, t, :], eB[:, t:t + 1],
                                                   flat[:, 3072 + t * 128:3200 + t * 128], ALU.mult, ALU.add)
                    step(ins)
                    step.wait()
                dve.sem_inc(s_ready, 1)
                for lv in range(1, NL):
                    collect(lv)
                    if lv + 2 < LEVELS:
                        subs(lv + 2)
                dve.wait_ge(us_done, h + 1)
                dve.wait_ge(s_in, h * 16 + 16)
                for n in range(DB):
                    step(dve.scalar_tensor_tensor(Sn[:, n, :], Ss[:, n, :], eB[:, NT + n:NT + n + 1],
                                                  flat[:, 2048 + n * 128:2176 + n * 128], ALU.mult, ALU.add))
                step.wait()
                dve.sem_inc(s_ready, 1)
                dve.wait_ge(ro_ready, h + 1)
                dve.scalar_tensor_tensor(oT[:, :], oT[:, :], m.hgw[:, :], ro[:, :], ALU.mult, ALU.mult).then_inc(head_done, 1)
                dve.wait_ge(head_done, h + 1 + 1)
                dve.tensor_tensor(m.mixT[:, bass.ds(h + HEADS, 1), :].squeeze(1), oT[:, :], g[:, :], ALU.mult).then_inc(mixed, 1)
                step.end(HEADS)


def decode_phase(nc, a, out, m):
    KEYS = PAGES * PAGE
    with ExitStack() as ctx:
        sb, sem = scope(nc, ctx)
        pt = sb("d_pt", [1, DB * PAGES], I32)
        K = sb("d_K", [128, 2, PG, 512])
        V = sb("d_V", [128, 2, PAGES, 512])
        Vn = sb("d_Vn", [DS, 2, 512])
        sN = sb("d_sN", [128, DS])
        KT = sb("d_KT", [128, 2, HEADS, PG * PAGE])
        qb = sb("d_qb", [128, 2, HEADS, 32])
        kb = sb("d_kb", [128, 2, HEADS, DS])
        P = sb("d_P", [128, 2, KEYS + DS])
        AT = sb("d_AT", [128, PAGES * 32])
        ATn = sb("d_ATn", [DS, 32])
        pat0 = sb("d_pat0", [128, 32])
        pat1 = sb("d_pat1", [128, 32])
        pat = sb("d_pat", [128, 32])
        C = sb("d_C", [128, 2, 32])
        cmask = sb("d_cmask", [128, DS])
        pr = sb("d_pr", [128, 1], I32)
        tq = sb("d_tq", [128, 1], I32)
        tk = sb("d_tk", [128, DS], I32)
        tqf = sb("d_tqf", [128, 1])
        mx = sb("d_mx", [128, 2])
        nmx = sb("d_nmx", [128, 1])
        l = sb("d_l", [128, 2])
        r = sb("d_r", [128, 1])
        oS = sb("d_oS", [128, HEADS, NS])
        so = sb("d_so", [128, HEADS, NS])
        ro = sb("d_ro", [128, HEADS, NS])
        gate = sem("d_gate")
        pt_in = sem("d_pt_in")
        k_in = [sem("d_k_in0"), sem("d_k_in1")]
        v_in = [sem("d_v_in0"), sem("d_v_in1")]
        k_used = sem("d_k_used")
        kt_done = sem("d_kt_done")
        kt_ready = [sem("d_kt_ready_even"), sem("d_kt_ready_odd")]
        qb_ready, scored, max_ready, exp_done, c_ready = (sem(f"d_{n}") for n in (
            "qb_ready", "scored", "max_ready", "exp_done", "c_ready"))
        at_done, at_ready, at_done_lag, av_done, o_ready = (sem(f"d_{n}") for n in (
            "at_done", "at_ready", "at_done_lag", "av_done", "o_ready"))
        o_squared, o_meaned, o_read, ro_ready = (sem(f"d_{n}") for n in ("o_squared", "o_meaned", "o_read", "ro_ready"))
        iota_done, setup_step, dve_step, act_step = (sem(f"d_{n}") for n in (
            "iota_done", "setup_step", "dve_step", "act_step"))
        block = ctx.enter_context(nc.Block())
        flat = m.ps[:, :, :].rearrange("p b n -> p (b n)")
        kc = a.cache_k[0, :, :, :, :].rearrange("n p h e -> n p (h e)")
        vc = a.cache_v[0, :, :, :, :].rearrange("n p h e -> n p (h e)")
        S_NEW, AT_NEW, OT = m.ps[:, 6, 0:DS], m.ps[0:DS, 4, 0:32], m.ps[:, 5, 0:32]
        VROUND = (PAGES + 1) * 16

        def requests(eng, unit):
            unit(0, 0, None)
            with eng.Fori(0, DB // 2 - 1) as i:
                unit(i * 2 + 1, 1, i)
                unit(i * 2 + 2, 0, i)
            unit(DB - 1, 1, DB // 2 - 1)

        @block.sync
        def _(sp):
            sp.dma_start(pt[:, :], a.page_table.rearrange("(o b) n -> o (b n)", o=1)).then_inc(pt_in, 16)
            sp.wait_ge(pt_in, 16)

            def load(b, u, early):
                for g in range(NPG):
                    s = g % 2
                    for j in range(PG):
                        page = sp.value_load(pt[0:1, bass.ds(b * PAGES + g * PG + j, 1)], min_val=0,
                                             max_val=a.cache_k.shape[1] - 1)
                        if j == 0 and (not early or b * NPG + g >= 2):
                            sp.wait_ge(k_used, b * NPG + g - 1)
                            sp.sem_inc(gate, 1)
                        if j == 0 and g == 0 and not early:
                            sp.wait_ge(av_done, b - 1)
                            sp.sem_inc(gate, 1)
                        sp.dma_start(K[:, s, j, :], kc[page, :, :]).then_inc(k_in[s], 16)
                        sp.dma_start(V[:, u, g * PG + j, :], vc[page, :, :]).then_inc(v_in[u], 16)
                sp.dma_start(Vn[:, u, :], out.v_sample[0, b, :, :, :].rearrange("t h e -> t (h e)")).then_inc(v_in[u], 16)
            load(0, 0, True)
            load(1, 1, True)
            with sp.Fori(1, DB // 2) as i:
                for u in range(2):
                    load(i * 2 + u, u, False)

        @block.gpsimd
        def _(pool):
            pool.memset(pat0[:, :], 0.0).then_inc(iota_done, 1)
            pool.memset(pat1[:, :], 0.0).then_inc(iota_done, 1)
            pool.iota(pr[:, :], [[0, 1]], base=0, channel_multiplier=1).then_inc(iota_done, 1)
            pool.iota(tk[:, :], [[1, DS]], base=0, channel_multiplier=0).then_inc(iota_done, 1)
            pool.wait_ge(iota_done, 4)
            for p, base in ((pat0, 0), (pat1, -DS)):
                v = p[:, :].rearrange("p (h t) -> p h t", h=HEADS)
                pool.affine_select(out=v, in_=v, compare_op=ALU.not_equal, fill=1.0, base=base,
                                   pattern=[[-32, HEADS], [-1, DS]], channel_multiplier=1).then_inc(iota_done, 1)

        @block.tensor
        def _(pe):
            def scores(b, u, first):
                for g in range(NPG):
                    pe.wait_ge(k_in[g % 2], (b * 2 + g // 2 + 1) * PG * 16)
                    for h in range(HEADS):
                        if not (first and g == 0 and h < 2):
                            pe.wait_ge(kt_ready[h % 2], b * 8 + g * 2 + h // 2)
                        if g == 0 and h == 1 and not first:
                            pe.wait_ge(o_ready, b)
                        for j in range(PG):
                            ins = pe.transpose(m.ps[:, 4 + h % 2, j * 128:j * 128 + 128],
                                               K[:, g % 2, j, h * 128:h * 128 + 128], m.ident[:, :])
                        ins.then_inc(kt_done, 1)
                    if g == 0:
                        pe.wait_ge(qb_ready, b + 1)
                        if not first:
                            pe.wait_ge(exp_done, b)
                    for p in range(2):
                        pe.wait_ge(kt_ready[p], b * 8 + g * 2 + 2)
                    for h in range(HEADS):
                        ins = pe.matmul(m.ps[32 * h:32 * h + 32, g, :], qb[:, u, h, :], KT[:, g % 2, h, :],
                                        start=True, stop=True)
                    ins.then_inc(k_used, 1)
                for h in range(HEADS):
                    ins = pe.matmul(m.ps[32 * h:32 * h + 32, 6, 0:DS], qb[:, u, h, :],
                                    kb[:, u, h, :], start=True, stop=True)
                ins.then_inc(scored, 1)

            def values(b, u, i):
                pe.wait_ge(c_ready, b + 1)
                pe.wait_ge(at_ready, b + 1)
                for j in range(PAGES):
                    pe.matmul(m.ps[:, 7, j * 32:j * 32 + 32], P[:, u, j * 128:j * 128 + 128], C[:, u, :],
                              start=True, stop=True)
                pe.matmul(AT_NEW, P[:, u, KEYS:KEYS + DS], C[:, u, :], start=True, stop=True).then_inc(at_done, 1)
                pe.wait_ge(v_in[u], i * VROUND + VROUND)
                pe.wait_ge(at_ready, b + 2)
                for h in range(HEADS):
                    o = m.ps[:, 5, h * DS:h * DS + DS]
                    for j in range(PAGES):
                        pe.matmul(o, V[:, u, j, h * 128:h * 128 + 128],
                                  AT[:, j * 32 + h * DS:j * 32 + h * DS + DS], start=(j == 0), stop=False)
                    ins = pe.matmul(o, Vn[:, u, h * 128:h * 128 + 128], ATn[:, h * DS:h * DS + DS],
                                    start=False, stop=True)
                ins.then_inc(av_done, 1)

            def unit(b, u, i):
                scores(b, u, i is None)
                if i is not None:
                    values(b - 1, 1 - u, i)
            requests(pe, unit)
            values(DB - 1, 1, DB // 2 - 1)
            pe.wait_ge(o_squared, 1)
            pe.matmul(m.ps[:, 0, 0:HEADS * NS], m.ones[:, :], so[:, :, :].rearrange("p h t -> p (h t)"),
                      start=True, stop=True).then_inc(o_meaned, 1)

        @block.scalar
        def _(act):
            load_ln_exp(nc, act)

            def unit(b, u, i):
                for g in range(NPG):
                    for h in (1, 3):
                        act.wait_ge(kt_done, b * 16 + g * 4 + h + 1)
                        act.activation(KT[:, g % 2, h, :], m.ps[:, 5, :], ACT.Copy).then_inc(kt_ready[1], 1)
                act.wait_ge(max_ready, b + 1)
                if i is not None:
                    act.wait_ge(at_done_lag, b)
                act.activation(P[:, u, 0:KEYS], flat[:, 0:KEYS], ACT.Exp, bias=nmx[:, :], accum_out=l[:, 0:1])
                act.activation(P[:, u, KEYS:KEYS + DS], sN[:, :], ACT.Exp, bias=nmx[:, :],
                               accum_out=l[:, 1:2]).then_inc(exp_done, 1)
            requests(act, unit)
            act.wait_ge(o_ready, DB + 1)
            act.activation(so[:, :, :], oS[:, :, :], ACT.Square).then_inc(o_squared, 1)
            act.wait_ge(o_meaned, 1)
            mean = m.ps[:, 0, 0:HEADS * NS].rearrange("p (h t) -> p h t", h=HEADS)
            act.activation(ro[:, :, :], mean, ACT.Ln, bias=m.eps[:, :]).then_inc(o_read, 1)
            act.wait_ge(o_read, 1)
            act.activation(ro[:, :, :], ro[:, :, :], ACT.Exp, scale=-0.5).then_inc(ro_ready, 1)

        @block.vector
        def _(dve):
            setup = Steps(dve, setup_step)
            dve.wait_ge(iota_done, 6)
            setup(dve.tensor_scalar(tq[:, :], pr[:, :], DS - 1, None, ALU.bitwise_and))
            setup(dve.scalar_tensor_tensor(pat[:, :], pat1[:, :], m.coef[:, 1:2], pat0[:, :], ALU.mult, ALU.add))
            setup.wait()
            setup(dve.tensor_copy(tqf[:, :], tq[:, :]))
            setup.wait()
            setup(dve.tensor_scalar(cmask[:, :], tk[:, :], tqf[:, :], NEG, ALU.is_gt, ALU.mult))
            setup.wait()
            dve.sem_inc(o_ready, 1)
            dve.sem_inc(at_ready, 1)
            dve.sem_inc(at_done_lag, 1)
            step = Steps(dve, dve_step)

            def unit(b, u, i):
                if not isinstance(b, int) or b >= 2:
                    dve.wait_ge(scored, b - 1)
                dve.tensor_copy(kb[:, u, :, :], m.kS[:, :, bass.ds(b * DS, DS)])
                dve.tensor_copy(qb[:, u, :, :], m.qbd[:, :, bass.ds(b, 1), :].squeeze(2)).then_inc(qb_ready, 1)
                for g in range(NPG):
                    for h in (0, 2):
                        dve.wait_ge(kt_done, b * 16 + g * 4 + h + 1)
                        dve.tensor_copy(KT[:, g % 2, h, :], m.ps[:, 4, :]).then_inc(kt_ready[0], 1)
                dve.wait_ge(scored, b + 1)
                step(dve.tensor_tensor(sN[:, :], S_NEW, cmask[:, :], ALU.add))
                step(dve.tensor_reduce(mx[:, 0:1], flat[:, 0:KEYS], AX.X, ALU.max))
                step.wait()
                step(dve.tensor_reduce(mx[:, 1:2], sN[:, :], AX.X, ALU.max))
                step.wait()
                dve.tensor_reduce(nmx[:, :], mx[:, :], AX.X, ALU.max, negate=True).then_inc(max_ready, 1)
                if i is not None:
                    collect(b - 1)
                dve.wait_ge(exp_done, b + 1)
                step(dve.tensor_tensor(r[:, :], l[:, 0:1], l[:, 1:2], ALU.add))
                step.wait()
                step(dve.reciprocal(r[:, :], r[:, :]))
                step.wait()
                dve.tensor_scalar(C[:, u, :], pat[:, :], r[:, :], None, ALU.mult).then_inc(c_ready, 1)

            def collect(b):
                dve.wait_ge(at_done, b + 1)
                step(dve.tensor_copy(AT[:, :], m.ps[:, 7, :]))
                dve.tensor_copy(ATn[:, :], AT_NEW).then_inc(at_ready, 1)
                dve.sem_inc(at_done_lag, 1)
                dve.wait_ge(av_done, b + 1)
                dve.tensor_copy(oS[:, :, bass.ds(b * DS, DS)], OT.rearrange("p (h t) -> p h t", h=HEADS)).then_inc(o_ready, 1)
            unit(0, 0, None)
            with dve.Fori(0, DB // 2 - 1) as i:
                step.begin(i, 12)
                unit(i * 2 + 1, 1, i)
                unit(i * 2 + 2, 0, i)
                step.end(DB // 2 - 1)
            unit(DB - 1, 1, DB // 2 - 1)
            collect(DB - 1)
            dve.wait_ge(ro_ready, 1)
            dve.scalar_tensor_tensor(m.mixT[:, 0:HEADS, SEQ:TOK], oS[:, :, :], m.subw[:, :], ro[:, :, :],
                                     ALU.mult, ALU.mult)


def mix_phase(nc, a, m):
    NR = NG + NE
    with ExitStack() as ctx:
        sb, sem = scope(nc, ctx)
        wo = sb("m_wo", [128, KD, D])
        wr = sb("m_wr", [128, KD, NR])
        br = sb("m_br", [128, NR])
        xb = sb("m_xb", [128, 2, D])
        hs = sb("m_hs", [128, 2, D])
        ss = sb("m_ss", [128, 2])
        LG = sb("m_LG", [128, TILES, NR])
        place = sb("m_place", [128, TILES, EG])
        gm, gz, tm, v1, v2, w1, w2 = (sb(f"m_{n}", [128, TILES]) for n in ("gm", "gz", "tm", "v1", "v2", "w1", "w2"))
        t4, ohg, oh1, oh2, es, ge = (sb(f"m_{n}", [128, TILES, EG]) for n in ("t4", "ohg", "oh1", "oh2", "es", "ge"))
        t16 = sb("m_t16", [128, TILES, NG, EG])
        wo_in = [sem("m_wo_in0"), sem("m_wo_in1")]
        wr_in = sem("m_wr_in")
        x_in = [sem("m_x_in0"), sem("m_x_in1")]
        mixed, h_ready, squared, hs_ready, transposed, evacuated, routed, logits = (sem(f"m_{n}") for n in (
            "mixed", "h_ready", "squared", "hs_ready", "transposed", "evacuated", "routed", "logits"))
        act_step, dve_step, pool_step = sem("m_act_step"), sem("m_dve_step"), sem("m_pool_step")
        shifted, exp_done, v_diff, exp2_done = (sem(f"m_{n}") for n in ("shifted", "exp_done", "v_diff", "exp2_done"))
        block = ctx.enter_context(nc.Block())
        wo_d = a.w_out[0, :, :].rearrange("(k p) n -> p k n", p=128)
        xp = a.x_prompt[0, :, :].rearrange("(t p) d -> t p d", p=128)
        wrg = a.w_router_grp[0, :, :].rearrange("(k p) n -> p k n", p=128)
        wre = a.w_router_exp[0, :, :].rearrange("(k p) n -> p k n", p=128)

        @block.sync
        def _(sp):
            for t in range(TILES):
                u, n = t % 2, rows(t)
                if t >= 2:
                    sp.wait_ge(h_ready, 2 * (t - 1))
                src = xp[t, :, :] if t < NT else a.x_sample.rearrange("b t d -> (b t) d")
                sp.dma_start(xb[0:n, u, :], src).then_inc(x_in[u], 16)
                if t == 0:
                    for n in range(2):
                        sp.dma_start(wo[:, :, n * 512:n * 512 + 512], wo_d[:, :, n * 512:n * 512 + 512]).then_inc(wo_in[n], 16)
                    with nc.allow_non_contiguous_dma("small router weights"):
                        sp.dma_start(wr[:, :, 0:NG], wrg).then_inc(wr_in, 16)
                        sp.dma_start(wr[:, :, NG:NR], wre).then_inc(wr_in, 16)
                        sp.dma_start(br[:, 0:NG], a.b_router_grp[0, :].partition_broadcast(128)).then_inc(wr_in, 16)
                        sp.dma_start(br[:, NG:NR], a.b_router_exp[0, :].partition_broadcast(128)).then_inc(wr_in, 16)

        @block.gpsimd
        def _(pool):
            pool.memset(LG[:, :, :], 0.0).then_inc(pool_step, 1)
            for e in range(EG):
                pool.memset(place[:, :, e:e + 1], float(EG - e)).then_inc(pool_step, 1)

        @block.tensor
        def _(pe):
            def project(t):
                u, n = t % 2, rows(t)
                for b in range(2):
                    if t == 0:
                        pe.wait_ge(wo_in[b], 16)
                    if t >= 2:
                        pe.wait_ge(h_ready, 2 * (t - 2) + b + 1)
                    for k in range(KD):
                        ins = pe.matmul(m.ps[0:n, 2 * u + b, :], m.mixT[:, k, cols(t)], wo[:, k, b * 512:b * 512 + 512],
                                        start=(k == 0), stop=(k == KD - 1))
                    ins.then_inc(mixed, 1)

            def route(t):
                u, n = t % 2, rows(t)
                pe.wait_ge(hs_ready, t + 1)
                for b in range(2):
                    if t >= 1:
                        pe.wait_ge(evacuated, 2 * (t - 1) + b + 1)
                    for c in range(4):
                        k = 4 * b + c
                        ins = pe.transpose(m.ps[:, 4 + b, c * 128:c * 128 + n], hs[0:n, u, k * 128:k * 128 + 128],
                                           m.ident[0:n, 0:n])
                    ins.then_inc(transposed, 1)
                pe.wait_ge(evacuated, 2 * t + 2)
                if t == 0:
                    pe.wait_ge(wr_in, 64)
                if t >= 2:
                    pe.wait_ge(logits, t - 1)
                for k in range(KD):
                    ins = pe.matmul(m.ps[0:n, 6 + u, 0:NR], m.xT[:, k, cols(t)], wr[:, k, :],
                                    start=(k == 0), stop=(k == KD - 1))
                ins.then_inc(routed, 1)
            project(0)
            for t in range(TILES):
                if t + 1 < TILES:
                    project(t + 1)
                route(t)

        @block.scalar
        def _(act):
            load_ln_exp(nc, act)
            step = Steps(act, act_step)
            for t in range(TILES):
                u, n = t % 2, rows(t)
                act.wait_ge(h_ready, 2 * t + 2)
                if t >= 2:
                    act.wait_ge(transposed, 2 * (t - 1))
                step(act.activation(hs[0:n, u, :], m.Y[0:n, t, :], ACT.Square, accum_out=ss[0:n, u:u + 1]))
                step.wait()
                step(act.activation(ss[0:n, u:u + 1], ss[0:n, u:u + 1], ACT.Ln, scale=1.0 / D, bias=m.eps[0:n, :]))
                step.wait()
                step(act.activation(ss[0:n, u:u + 1], ss[0:n, u:u + 1], ACT.Exp, scale=-0.5))
                step.wait()
                act.activation(hs[0:n, u, :], m.Y[0:n, t, :], ACT.Copy, scale=ss[0:n, u:u + 1]).then_inc(hs_ready, 1)
            act.wait_ge(shifted, 1)
            act.activation(t4[:, :, :], t4[:, :, :], ACT.Exp).then_inc(exp_done, 1)
            act.wait_ge(v_diff, 1)
            act.activation(w2[:, :], w2[:, :], ACT.Exp).then_inc(exp2_done, 1)

        @block.vector
        def _(dve):
            step = Steps(dve, dve_step)

            def add_x(t):
                u, n = t % 2, rows(t)
                dve.wait_ge(x_in[u], (t // 2 + 1) * 16)
                for b in range(2):
                    dve.wait_ge(mixed, 2 * t + b + 1)
                    c = slice(b * 512, b * 512 + 512)
                    dve.tensor_tensor(m.Y[0:n, t, c], m.ps[0:n, 2 * u + b, :], xb[0:n, u, c], ALU.add).then_inc(h_ready, 1)

            dve.wait_ge(pool_step, 1 + EG)
            add_x(0)
            for t in range(TILES):
                u, n = t % 2, rows(t)
                if t + 1 < TILES:
                    add_x(t + 1)
                for b in range(2):
                    dve.wait_ge(transposed, 2 * t + b + 1)
                    i = m.ps[:, 4 + b, :].rearrange("p (c n) -> p c n", c=4)[:, :, 0:n]
                    wn = m.n2w[:, 4 * b:4 * b + 4].unsqueeze(2).to_broadcast([128, 4, n])
                    dve.tensor_tensor(m.xT[:, 4 * b:4 * b + 4, cols(t)], i, wn, ALU.mult).then_inc(evacuated, 1)
                dve.wait_ge(routed, t + 1)
                if t == 0:
                    dve.wait_ge(wr_in, 64)
                dve.tensor_tensor(LG[0:n, t, :], m.ps[0:n, 6 + u, 0:NR], br[0:n, :], ALU.add).then_inc(logits, 1)
            dve.wait_ge(logits, TILES)
            wide = lambda x: x[:, :].unsqueeze(2).to_broadcast([128, TILES, EG])

            def do(ins):
                step(ins)
                step.wait()

            def first_max(oh, x, mx):
                do(dve.tensor_reduce(mx[:, :], x, AX.X, ALU.max))
                do(dve.tensor_tensor(oh[:, :, :], x, wide(mx), ALU.is_equal))
                do(dve.tensor_tensor(oh[:, :, :], oh[:, :, :], place[:, :, :], ALU.mult))
                do(dve.tensor_reduce(tm[:, :], oh[:, :, :], AX.X, ALU.max))
                do(dve.tensor_tensor(oh[:, :, :], place[:, :, :], wide(tm), ALU.is_equal))
            G = LG[:, :, 0:NG]
            first_max(ohg, G, gm)
            do(dve.tensor_tensor(t4[:, :, :], G, wide(gm), ALU.subtract))
            dve.sem_inc(shifted, 1)
            dve.wait_ge(exp_done, 1)
            do(dve.tensor_reduce(gz[:, :], t4[:, :, :], AX.X, ALU.add))
            do(dve.reciprocal(gz[:, :], gz[:, :]))
            E4 = LG[:, :, NG:NR].rearrange("p t (g e) -> p t g e", g=NG)
            do(dve.tensor_tensor(t16[:, :, :, :], E4, ohg[:, :, :].unsqueeze(3).to_broadcast([128, TILES, NG, EG]), ALU.mult))
            do(dve.tensor_reduce(es[:, :, :], t16[:, :, :, :].rearrange("p t g e -> p t e g"), AX.X, ALU.add))
            first_max(oh1, es[:, :, :], v1)
            do(dve.scalar_tensor_tensor(es[:, :, :], oh1[:, :, :], -BIG, es[:, :, :], ALU.mult, ALU.add))
            first_max(oh2, es[:, :, :], v2)
            do(dve.tensor_tensor(w2[:, :], v2[:, :], v1[:, :], ALU.subtract))
            dve.sem_inc(v_diff, 1)
            dve.wait_ge(exp2_done, 1)
            do(dve.tensor_scalar(w1[:, :], w2[:, :], 1.0, None, ALU.add))
            do(dve.reciprocal(w1[:, :], w1[:, :]))
            do(dve.tensor_tensor(w1[:, :], w1[:, :], gz[:, :], ALU.mult))
            do(dve.tensor_tensor(w2[:, :], w2[:, :], w1[:, :], ALU.mult))
            do(dve.tensor_tensor(oh1[:, :, :], oh1[:, :, :], wide(w1), ALU.mult))
            do(dve.tensor_tensor(oh2[:, :, :], oh2[:, :, :], wide(w2), ALU.mult))
            do(dve.tensor_tensor(ge[:, :, :], oh1[:, :, :], oh2[:, :, :], ALU.add))
            do(dve.tensor_tensor(m.gates[:, :, :].rearrange("p t (g e) -> p t g e", g=NG),
                                 ge[:, :, :].unsqueeze(2).to_broadcast([128, TILES, NG, EG]),
                                 ohg[:, :, :].unsqueeze(3).to_broadcast([128, TILES, NG, EG]), ALU.mult))


def moe_phase(nc, a, out, m):
    FC = FF // 128
    with ExitStack() as ctx:
        sb, sem = scope(nc, ctx)
        wg = sb("e_wg", [128, 2, KD, FF])
        wu = sb("e_wu", [128, 2, KD, FF])
        wd = sb("e_wd", [128, 2, FC, D])
        sg = sb("e_sg", [128, 512])
        hT = sb("e_hT", [128, FC, TOK])
        w_in = [sem("e_w_in0"), sem("e_w_in1")]
        up_done, silu_done, h_ready, down_done, added, stored = (sem(f"e_{n}") for n in (
            "up_done", "silu_done", "h_ready", "down_done", "added", "stored"))
        block = ctx.enter_context(nc.Block())
        wg_d = a.w_gate[0, :, :, :].rearrange("e (k p) f -> e p k f", p=128)
        wu_d = a.w_up[0, :, :, :].rearrange("e (k p) f -> e p k f", p=128)
        wd_d = a.w_down[0, :, :, :].rearrange("e (k p) n -> e p k n", p=128)
        NU = FC * len(GROUPS)

        @block.sync
        def _(sp):
            def load(e, u):
                sp.dma_start(wg[:, u, :, :], wg_d[e, :, :, :]).then_inc(w_in[u], 16)
                sp.dma_start(wu[:, u, :, :], wu_d[e, :, :, :]).then_inc(w_in[u], 16)
                sp.dma_start(wd[:, u, :, :], wd_d[e, :, :, :]).then_inc(w_in[u], 16)
            load(0, 0)
            load(1, 1)
            with sp.Fori(1, NE // 2) as i:
                for u in range(2):
                    sp.wait_ge(down_done, (i * 2 + u - 1) * TILES * 2)
                    load(i * 2 + u, u)
            sp.wait_ge(added, NE * TILES * 2 + 4)
            sp.dma_start(out.y_prompt[0, :, :].rearrange("(t p) d -> p t d", p=128), m.Y[:, 0:NT, :]).then_inc(stored, 16)
            sp.dma_start(out.y_sample.rearrange("b t d -> (b t) d"), m.Y[0:NS, NT, :]).then_inc(stored, 16)
            sp.wait_ge(stored, 32)

        @block.tensor
        def _(pe):
            with pe.Fori(0, NE // 2) as i:
                for u in range(2):
                    e = i * 2 + u
                    pe.wait_ge(w_in[u], i * 48 + 48)
                    for n in range(NU):
                        f, (c0, w0) = n // 3, GROUPS[n % 3]
                        pe.wait_ge(h_ready, e * NU + n + 1)
                        for w, b in ((wg, 2 * (n % 2)), (wu, 2 * (n % 2) + 1)):
                            for k in range(KD):
                                ins = pe.matmul(m.ps[:, b, 0:w0], w[:, u, k, f * 128:f * 128 + 128],
                                                m.xT[:, k, c0:c0 + w0], start=(k == 0), stop=(k == KD - 1))
                            ins.then_inc(up_done, 1)
                    pe.wait_ge(h_ready, e * NU + NU + 2)
                    for t in range(TILES):
                        for b in range(2):
                            pe.wait_ge(added, e * 2 * TILES + (2 * t + b + 1 if t else 4))
                            for f in range(FC):
                                ins = pe.matmul(m.ps[0:rows(t), 4 + 2 * (t % 2) + b, :], hT[:, f, cols(t)],
                                                wd[:, u, f, b * 512:b * 512 + 512], start=(f == 0), stop=(f == FC - 1))
                            ins.then_inc(down_done, 1)

        @block.scalar
        def _(act):
            with act.Fori(0, NE // 2) as i:
                for u in range(2):
                    e = i * 2 + u
                    for n in range(NU):
                        w0 = GROUPS[n % 3][1]
                        act.wait_ge(up_done, e * 2 * NU + 2 * n + 1)
                        act.wait_ge(h_ready, e * NU + n + 2)
                        act.activation(sg[:, 0:w0], m.ps[:, 2 * (n % 2), 0:w0], ACT.Silu).then_inc(silu_done, 1)

        @block.vector
        def _(dve):
            dve.sem_inc(h_ready, 2)
            dve.sem_inc(added, 4)
            with dve.Fori(0, NE // 2) as i:
                for u in range(2):
                    e = i * 2 + u
                    for n in range(NU):
                        f, (c0, w0) = n // 3, GROUPS[n % 3]
                        dve.wait_ge(silu_done, e * NU + n + 1)
                        dve.wait_ge(up_done, e * 2 * NU + 2 * n + 2)
                        dve.tensor_tensor(hT[:, f, c0:c0 + w0], sg[:, 0:w0], m.ps[:, 2 * (n % 2) + 1, 0:w0],
                                          ALU.mult).then_inc(h_ready, 1)
                    for t in range(TILES):
                        for b in range(2):
                            dve.wait_ge(down_done, e * 2 * TILES + 2 * t + b + 1)
                            y = m.Y[0:rows(t), t, b * 512:b * 512 + 512]
                            dve.scalar_tensor_tensor(y, m.ps[0:rows(t), 4 + 2 * (t % 2) + b, :],
                                                     m.gates[0:rows(t), t, bass.ds(e, 1)], y, ALU.mult, ALU.add).then_inc(added, 1)


_INS = ["x_prompt", "x_sample", "cache_k", "cache_v", "state_hgrn", "page_table", "norm1_w", "w_in", "q_norm_w",
        "k_norm_w", "lambda_q1", "lambda_k1", "lambda_q2", "lambda_k2", "subln_w", "hg_lb", "hg_norm_w", "w_out",
        "norm2_w", "w_router_grp", "b_router_grp", "w_router_exp", "b_router_exp", "w_gate", "w_up", "w_down"]
_OUTS = [("y_prompt", (1, SEQ, D)), ("y_sample", (DB, DS, D)), ("k_prompt", (1, 1, SEQ, HEADS, 128)),
         ("v_prompt", (1, 1, SEQ, HEADS, 128)), ("hgrn_prompt", (1, 1, HEADS, 128, 128)),
         ("k_sample", (1, DB, DS, HEADS, 128)), ("v_sample", (1, DB, DS, HEADS, 128)),
         ("hgrn_sample", (1, DB, HEADS, 128, 128))]


def kernel(**inputs):
    import numpy as _np
    import concourse.bacc as _bacc
    from concourse.bass_utils import run_bass_kernel_spmd as _run

    nc = _bacc.Bacc("TRN2", target_bir_lowering=False, num_devices=1)
    arrays, a, out = {}, Named(), Named()
    for name in _INS:
        x = _np.ascontiguousarray(inputs[name])
        arrays[f"in_{name}"] = x
        a.__dict__[name] = nc.dram_tensor(f"in_{name}", x.shape, mybir.dt.from_np(x.dtype), kind="ExternalInput").ap()
    for name, shape in _OUTS:
        out.__dict__[name] = nc.dram_tensor(f"out_{name}", shape, F32, kind="ExternalOutput").ap()
    build(nc, a, out)
    r = _run(nc, [arrays], core_ids=[0])
    return tuple(r.results[0][f"out_{name}"] for name, _ in _OUTS)
```

```python
from contextlib import ExitStack


import concourse.bass as bass
from concourse import mybir

F32 = mybir.dt.float32
I32 = mybir.dt.int32
U8 = mybir.dt.uint8
ALU = mybir.AluOpType
ACT = mybir.ActivationFunctionType
AX = mybir.AxisListType

D = 1024
KD = D // 128
SEQ = 1024
NT = SEQ // 128
DB, DS = 8, 8
NS = DB * DS
TOK = SEQ + NS
TILES = NT + 1
GROUPS = [(0, 384), (384, 384), (768, 320)]
HEADS = 4
PAGE = 128
PAGES = 16
PG = 4
NPG = PAGES // PG
NE, NG, EG = 16, 4, 4
FF = 256
TOP = 2
SLOTS = (TOP * 1088 - NE) // 128 + NE
RING = 3
LEVELS = 7
SAMPLE_LEVELS = 3
EPS = 1e-6
NEG = -1e30
LAM_INIT = 0.2
BIG = 3e38
LN_EXP_SET = 6


class Named:
    pass


class Steps:

    def __init__(self, eng, sem):
        self.eng, self.sem, self.n, self.turn, self.per = eng, sem, 0, 0, 0

    def __call__(self, ins):
        ins.then_inc(self.sem, 1)
        self.n += 1

    def wait(self):
        self.eng.wait_ge(self.sem, self.turn * self.per + self.n)

    def begin(self, turn, per):
        self.turn, self.per, self.start = turn, per, self.n

    def end(self, turns):
        assert self.n - self.start == self.per, (self.n - self.start, self.per)
        self.n = self.start + turns * self.per
        self.turn, self.per = 0, 0


def rows(t):
    return 128 if t < NT else NS


def cols(t):
    return slice(t * 128, t * 128 + rows(t))


def build(nc, a, out):
    with ExitStack() as ctx:
        m = Named()
        sb = lambda n, s, dt=F32: ctx.enter_context(nc.sbuf_tensor(n, s, dt))
        m.ident = sb("ident", [128, 128])
        m.ones = sb("ones", [128, 128])
        m.halves = sb("halves", [128, 128])
        m.causal = sb("causal", [128, 128])
        m.eps = sb("eps", [128, 1])
        m.n1w = sb("n1w", [128, KD])
        m.n2w = sb("n2w", [128, KD])
        m.qw = sb("qw", [128, 1])
        m.kw = sb("kw", [128, 1])
        m.subw = sb("subw", [128, 1])
        m.hgw = sb("hgw", [128, 1])
        m.coef = sb("coef", [128, 2])
        m.lb = sb("lb", [128, HEADS])
        m.lb1 = sb("lb1", [128, HEADS])
        m.mixT = sb("mixT", [128, KD, TOK])
        m.xT = sb("xT", [128, KD, TOK])
        m.qbd = sb("qbd", [128, HEADS, DB, 32])
        m.kS = sb("kS", [128, HEADS, NS])
        m.hn_rows = nc.dram_tensor("hn_rows", (TOK, D), F32, kind="Internal").ap()
        m.slot_rows = nc.dram_tensor("slot_rows", (SLOTS * 128, 1), F32, kind="Internal").ap()
        m.expert_rows = nc.dram_tensor("expert_rows", (SLOTS * 128, D), F32, kind="Internal").ap()
        m.ps = ctx.enter_context(nc.psum_tensor("ps", [128, 8, 512], F32))
        norm_phase(nc, a, m)
        attention_phase(nc, a, out, m)
        hgrn_phase(nc, a, out, m)
        decode_phase(nc, a, out, m)
        with ExitStack() as late:
            m.Y = late.enter_context(nc.sbuf_tensor("Y", [128, TILES, D], F32))
            sb = lambda n, s, dt=F32: late.enter_context(nc.sbuf_tensor(n, s, dt))
            m.w1 = sb("w1", [128, TILES])
            m.w2 = sb("w2", [128, TILES])
            m.pos1 = sb("pos1", [128, TILES], I32)
            m.pos2 = sb("pos2", [128, TILES], I32)
            m.slot_tok = sb("slot_tok", [128, SLOTS], I32)
            m.tile_expert = sb("tile_expert", [1, SLOTS], I32)
            m.tile_ring = sb("tile_ring", [1, SLOTS], I32)
            m.cum = sb("cum", [1, NE], I32)
            mix_phase(nc, a, m)
            moe_phase(nc, a, out, m)


def scope(nc, ctx):
    sb = lambda n, s, dt=F32: ctx.enter_context(nc.sbuf_tensor(n, s, dt))
    made = []

    def sem(n):
        made.append(ctx.enter_context(nc.semaphore(n)))
        return made[-1]
    sem.made = made
    return sb, sem


def load_ln_exp(nc, act):
    act.add_instruction(mybir.InstLoadActFuncSet(name=nc.get_next_instruction_name(), engine=mybir.EngineType.Activation,
                                                 act_func_set_id=LN_EXP_SET, ins=[], outs=[]))


def column(v, n):
    return v.rearrange("(p o) -> p o", o=1)


def norm_phase(nc, a, m):
    with ExitStack() as ctx:
        sb, sem = scope(nc, ctx)
        xb = sb("n_xb", [128, 2, D])
        junk = sb("n_junk", [128, D])
        xs = sb("n_xs", [128, 2, D])
        ss = sb("n_ss", [128, 2])
        rs = sb("n_rs", [128, 2])
        lam = sb("n_lam", [128, 4, 64])
        prod = sb("n_prod", [128, 2, 64])
        dots = sb("n_dots", [128, 2])
        hb = sb("n_hb", [128, 2, HEADS])
        hm = sb("n_hm", [128, HEADS])
        hs = sb("n_hs", [128, HEADS])
        x_in = [sem("n_x_in0"), sem("n_x_in1")]
        w_in = sem("n_w_in")
        xs_ready = sem("n_xs_ready")
        act_step = sem("n_act_step")
        dve_step = sem("n_dve_step")
        pool_step = sem("n_pool_step")
        transposed = sem("n_transposed")
        evacuated = sem("n_evacuated")
        small = sem("n_small")
        small_exp = sem("n_small_exp")
        m.old_sems = sem.made
        block = ctx.enter_context(nc.Block())
        xp = a.x_prompt[0, :, :].rearrange("(t p) d -> t p d", p=128)
        SMALL = [(m.n1w[:, :], a.norm1_w[0, :].rearrange("(c p) -> p c", p=128)),
                 (m.n2w[:, :], a.norm2_w[0, :].rearrange("(c p) -> p c", p=128)),
                 (m.qw[0:64, :], column(a.q_norm_w[0, :], 64)),
                 (m.qw[64:128, :], column(a.q_norm_w[0, :], 64)),
                 (m.kw[0:64, :], column(a.k_norm_w[0, :], 64)),
                 (m.kw[64:128, :], column(a.k_norm_w[0, :], 64)),
                 (m.subw[:, :], column(a.subln_w[0, :], 128)),
                 (m.hgw[:, :], column(a.hg_norm_w[0, :], 128)),
                 (hb[:, :, :], a.hg_lb.rearrange("l (h p) -> p l h", p=128))]
        SMALL += [(lam[:, n, :], v[0, :].partition_broadcast(128)) for n, v in
                  enumerate((a.lambda_q1, a.lambda_k1, a.lambda_q2, a.lambda_k2))]

        @block.gpsimd
        def _(pool):
            step = Steps(pool, pool_step)
            for t, v in ((m.ident, 0.0), (m.ones, 1.0 / 128), (m.halves, 0.0), (m.causal, 0.0), (m.eps, EPS)):
                step(pool.memset(t[:, :], v))
            step(pool.memset(m.coef[:, 0:1], 1.0))
            step(pool.memset(m.qbd[:, :, :, :], 0.0))
            step.wait()
            step(pool.affine_select(out=m.ident[:, :], in_=m.ident[:, :], compare_op=ALU.not_equal, fill=1.0,
                                    base=0, pattern=[[-1, 128]], channel_multiplier=1))
            step(pool.affine_select(out=m.causal[:, :], in_=m.causal[:, :], compare_op=ALU.is_ge, fill=NEG,
                                    base=0, pattern=[[-1, 128]], channel_multiplier=1))
            step.wait()
            step(pool.memset(m.halves[0:64, 0:64], 1.0 / 64))
            step.wait()
            step(pool.memset(m.halves[64:128, 64:128], 1.0 / 64))
            step.wait()
        POOL_ALL = 11

        @block.sync
        def _(sp):
            def load(t, u, free):
                if free is not None:
                    sp.wait_ge(xs_ready, free)
                n = 128 if not isinstance(t, int) or t < NT else NS
                src = xp[t, :, :] if n == 128 else a.x_sample.rearrange("b t d -> (b t) d")
                sp.dma_start(xb[0:n, u, :], src).then_inc(x_in[u], 16)
            load(0, 0, None)
            load(1, 1, None)
            with nc.allow_non_contiguous_dma("small weight vectors"):
                for dst, src in SMALL:
                    sp.dma_start(dst, src).then_inc(w_in, 16)
            with sp.Fori(1, NT // 2) as j:
                for u in range(2):
                    load(j * 2 + u, u, j * 2 + u - 1)
            load(NT, 0, NT - 1)

        @block.scalar
        def _(act):
            step = Steps(act, act_step)

            def scale_tile(t, u, n, turn):
                act.wait_ge(x_in[u], turn * 16 + 16)
                step(act.activation(junk[0:n, :], xb[0:n, u, :], ACT.Square, accum_out=ss[0:n, u:u + 1]))
                step.wait()
                step(act.activation(rs[0:n, u:u + 1], ss[0:n, u:u + 1], ACT.Ln, scale=1.0 / D, bias=m.eps[0:n, :]))
                step.wait()
                step(act.activation(rs[0:n, u:u + 1], rs[0:n, u:u + 1], ACT.Exp, scale=-0.5))
                step.wait()
                if not isinstance(t, int) or t >= 2:
                    act.wait_ge(transposed, (t - 1) * 2)
                act.activation(xs[0:n, u, :], xb[0:n, u, :], ACT.Copy, scale=rs[0:n, u:u + 1]).then_inc(xs_ready, 1)
            load_ln_exp(nc, act)
            act.wait_ge(pool_step, POOL_ALL)
            for u in range(2):
                scale_tile(u, u, 128, 0)
            with act.Fori(1, NT // 2) as j:
                step.begin(j - 1, 6)
                for u in range(2):
                    scale_tile(j * 2 + u, u, 128, j)
                step.end(NT // 2 - 1)
            scale_tile(NT, 0, NS, NT // 2)
            act.wait_ge(small, 1)
            act.activation(dots[:, :], dots[:, :], ACT.Exp).then_inc(small_exp, 1)
            act.activation(hb[:, :, :], hb[:, :, :], ACT.Exp).then_inc(small_exp, 1)

        @block.tensor
        def _(pe):
            pe.wait_ge(pool_step, POOL_ALL)

            def transpose_tile(t, u, n):
                pe.wait_ge(xs_ready, t + 1)
                for b in range(2):
                    if not isinstance(t, int) or t >= 2:
                        pe.wait_ge(evacuated, (t - 2) * 2 + b + 1)
                    for c in range(4):
                        k = b * 4 + c
                        last = pe.transpose(m.ps[:, 2 * u + b, c * 128:c * 128 + n],
                                            xs[0:n, u, k * 128:(k + 1) * 128], m.ident[0:n, 0:n])
                    last.then_inc(transposed, 1)
            for u in range(2):
                transpose_tile(u, u, 128)
            with pe.Fori(1, NT // 2) as j:
                for u in range(2):
                    transpose_tile(j * 2 + u, u, 128)
            transpose_tile(NT, 0, NS)

        @block.vector
        def _(dve):
            step = Steps(dve, dve_step)
            dve.wait_ge(w_in, 16 * len(SMALL))
            dve.wait_ge(pool_step, POOL_ALL)
            for n in range(2):
                step(dve.tensor_tensor(prod[:, n, :], lam[:, 2 * n, :], lam[:, 2 * n + 1, :], ALU.mult))
            step(dve.tensor_scalar(m.qw[:, :], m.qw[:, :], 0.125, None, ALU.mult))
            step(dve.tensor_scalar(m.subw[:, :], m.subw[:, :], 1.0 - LAM_INIT, None, ALU.mult))
            step(dve.tensor_tensor(hm[:, :], hb[:, 0, :], hb[:, 1, :], ALU.max))
            step.wait()
            step(dve.tensor_reduce(dots[:, :], prod[:, :, :], AX.X, ALU.add))
            for n in range(2):
                step(dve.tensor_tensor(hb[:, n, :], hb[:, n, :], hm[:, :], ALU.subtract))
            step.wait()
            dve.sem_inc(small, 1)

            def evacuate(t, u, n):
                for b in range(2):
                    dve.wait_ge(transposed, t * 2 + b + 1)
                    o = m.xT[:, 4 * b:4 * b + 4, bass.ds(t * 128, n)]
                    i = m.ps[:, 2 * u + b, :].rearrange("p (c n) -> p c n", c=4)[:, :, 0:n]
                    w = m.n1w[:, 4 * b:4 * b + 4].unsqueeze(2).to_broadcast([128, 4, n])
                    dve.tensor_tensor(o, i, w, ALU.mult).then_inc(evacuated, 1)
            with dve.Fori(0, NT // 2) as j:
                for u in range(2):
                    evacuate(j * 2 + u, u, 128)
            evacuate(NT, 0, NS)
            dve.wait_ge(small_exp, 2)
            step(dve.tensor_tensor(prod[:, 0, 0:1], dots[:, 1:2], dots[:, 0:1], ALU.subtract))
            step(dve.tensor_tensor(hs[:, :], hb[:, 0, :], hb[:, 1, :], ALU.add))
            step.wait()
            step(dve.tensor_scalar(m.coef[:, 1:2], prod[:, 0, 0:1], LAM_INIT, None, ALU.subtract))
            step(dve.reciprocal(hm[:, :], hs[:, :]))
            step.wait()
            step(dve.tensor_tensor(m.lb[:, :], hb[:, 0, :], hm[:, :], ALU.mult))
            step.wait()
            step(dve.tensor_scalar(m.lb1[:, :], m.lb[:, :], -1.0, 1.0, ALU.mult, ALU.add))
            step.wait()


def attention_phase(nc, a, out, m):
    w_in_d = a.w_in[0, :, :].rearrange("(k p) c -> p k c", p=128)
    with ExitStack() as ctx:
        sb, sem = scope(nc, ctx)
        wq, wk, wv = (sb(f"a_{n}", [128, KD, 128]) for n in ("wq", "wk", "wv"))
        zq, zk, sq, sk, rq, rk, qT, kT = (sb(f"a_{n}", [128, TOK]) for n in
                                         ("zq", "zk", "sq", "sk", "rq", "rk", "qT", "kT"))
        v = sb("a_v", [128, TILES, 128])
        kt = sb("a_kt", [128, TILES, 128])
        P = sb("a_P", [128, 2, SEQ])
        A = sb("a_A", [128, SEQ])
        AT = sb("a_AT", [128, SEQ])
        oT = sb("a_oT", [128, SEQ])
        so = sb("a_so", [128, SEQ])
        ro = sb("a_ro", [128, SEQ])
        nmx = sb("a_nmx", [128, 2])
        l = sb("a_l", [128, 2])
        r = sb("a_r", [128, 2])
        w_in = [sem(f"a_w_in{n}") for n in "qkv"]
        projected = [sem(f"a_projected_{n}") for n in "qkv"]
        v8_done = sem("a_v8_projected")
        squared = [sem("a_squared_q"), sem("a_squared_k")]
        meaned = [sem("a_meaned_q"), sem("a_meaned_k")]
        ms_read = [sem("a_ms_read_q"), sem("a_ms_read_k")]
        r_ready = [sem("a_rq_ready"), sem("a_rk_ready")]
        q_ready, k_ready, v_ready = sem("a_q_ready"), sem("a_k_ready"), sem("a_v_ready")
        kt_done, kt_ready = sem("a_kt_done"), sem("a_kt_ready")
        stored = sem("a_stored")
        saved = sem("a_saved")
        scored, max_ready, exp_done = sem("a_scored"), sem("a_max_ready"), sem("a_exp_done")
        a_ready, at_done, at_ready, av_done = sem("a_a_ready"), sem("a_at_done"), sem("a_at_ready"), sem("a_av_done")
        o_squared, o_meaned, o_read, ro_ready = (sem(n) for n in ("a_o_squared", "a_o_meaned", "a_o_read", "a_ro_ready"))
        head_done = sem("a_head_done")
        act_step, dve_step = sem("a_act_step"), sem("a_dve_step")
        old_sems, m.old_sems = m.old_sems, sem.made
        block = ctx.enter_context(nc.Block())
        flat = m.ps[:, :, :].rearrange("p b n -> p (b n)")

        @block.sync
        def _(sp):
            kp = out.k_prompt[0, 0, :, :, :].rearrange("(t p) h e -> h p t e", p=128)
            vp = out.v_prompt[0, 0, :, :, :].rearrange("(t p) h e -> h p t e", p=128)
            ks = out.k_sample[0, :, :, :, :].rearrange("b t h e -> h (b t) e")
            vs = out.v_sample[0, :, :, :, :].rearrange("b t h e -> h (b t) e")
            sp.sem_inc(stored, 1)
            with sp.Fori(0, HEADS) as h:
                for n, w in enumerate((wq, wk, wv)):
                    sp.wait_ge(projected[n] if n < 2 else v8_done, h + 1)
                    sp.dma_start(w[:, :, :], w_in_d[:, :, bass.ds(h * 128 + n * 512, 128)]).then_inc(w_in[n], 16)
                sp.wait_ge(v_ready, h + 1)
                sp.dma_start(vp[h, :, :, :], v[:, 0:NT, :]).then_inc(stored, 16)
                sp.dma_start(vs[h, :, :], v[0:NS, NT, :]).then_inc(stored, 16)
                sp.wait_ge(kt_ready, h + 1)
                sp.dma_start(kp[h, :, :, :], kt[:, 0:NT, :]).then_inc(stored, 16)
                sp.dma_start(ks[h, :, :], kt[0:NS, NT, :]).then_inc(stored, 16)
            sp.wait_ge(stored, 64 * HEADS + 1)

        @block.gpsimd
        def _(pool):
            for s in old_sems:
                pool.sem_clear(s)
            pool.sem_inc(saved, 1)
            with pool.Fori(0, HEADS) as h:
                pool.wait_ge(q_ready, h + 1)
                for mm in range(2):
                    o = m.qbd[64 * mm:64 * mm + 64, h, :, 8 * mm:8 * mm + 8]
                    i = qT[64 * mm:64 * mm + 64, SEQ:TOK].rearrange("p (b t) -> p b t", b=DB)
                    pool.tensor_copy(o, i).then_inc(saved, 1)
                    pool.wait_ge(saved, h * 3 + mm + 1 + 1)
                pool.wait_ge(k_ready, h + 1)
                pool.tensor_copy(m.kS[:, h, :], kT[:, SEQ:TOK]).then_inc(saved, 1)
                pool.wait_ge(saved, h * 3 + 3 + 1)

        @block.tensor
        def _(pe):
            def project(n, w, banks):
                for (c0, w0), b in zip(GROUPS, banks):
                    for k in range(KD):
                        last = pe.matmul(m.ps[:, b, 0:w0], w[:, k, :], m.xT[:, k, c0:c0 + w0],
                                         start=(k == 0), stop=(k == KD - 1))
                last.then_inc(projected[n], 1)

            def project_v(t, b, o):
                n = rows(t)
                for k in range(KD):
                    last = pe.matmul(m.ps[0:n, b, o:o + 128], m.xT[:, k, cols(t)], wv[:, k, :],
                                     start=(k == 0), stop=(k == KD - 1))
                return last

            def mean(n, s, banks):
                for (c0, w0), b in zip(GROUPS, banks):
                    last = pe.matmul(m.ps[:, b, 0:w0], m.halves[:, :], s[:, c0:c0 + w0], start=True, stop=True)
                last.then_inc(meaned[n], 1)

            for s in (*projected, v8_done, at_done):
                pe.sem_inc(s, 1)
            with pe.Fori(0, HEADS) as h:
                pe.wait_ge(w_in[0], h * 16 + 16)
                pe.wait_ge(o_read, h + 1)
                project(0, wq, (0, 1, 2))
                pe.wait_ge(w_in[1], h * 16 + 16)
                project(1, wk, (3, 4, 5))
                pe.wait_ge(squared[0], h + 1)
                mean(0, sq, (0, 1, 2))
                pe.wait_ge(w_in[2], h * 16 + 16)
                for t in range(NT):
                    last = project_v(t, 6 + t // 4, t % 4 * 128)
                last.then_inc(projected[2], 1)
                pe.wait_ge(squared[1], h + 1)
                mean(1, sk, (3, 4, 5))
                pe.wait_ge(ms_read[0], h + 1)
                project_v(NT, 0, 0).then_inc(v8_done, 1)
                pe.wait_ge(k_ready, h + 1)
                for t in range(TILES):
                    last = pe.transpose(m.ps[0:rows(t), 3 + t // 4, t % 4 * 128:t % 4 * 128 + 128],
                                        kT[:, cols(t)], m.ident[:, :])
                last.then_inc(kt_done, 1)
                pe.wait_ge(kt_ready, h + 1)

                def score(i):
                    L = (i + 1) * 128
                    for mm in range(2):
                        if i:
                            pe.wait_ge(exp_done, h * 16 + 2 * i - 1 + mm)
                        for c in range(0, L, 512):
                            w0 = min(512, L - c)
                            last = pe.matmul(m.ps[:, 2 * mm + c // 512, 0:w0],
                                             qT[64 * mm:64 * mm + 64, i * 128:i * 128 + 128],
                                             kT[64 * mm:64 * mm + 64, c:c + w0], start=True, stop=True)
                        last.then_inc(scored, 1)
                score(0)
                for i in range(NT):
                    if i + 1 < NT:
                        score(i + 1)
                    pe.wait_ge(a_ready, h * NT + i + 1)
                    if i:
                        pe.wait_ge(at_ready, h * NT + i)
                    for j in range(i + 1):
                        last = pe.transpose(flat[:, 2048 + j * 128:2048 + j * 128 + 128],
                                            A[:, j * 128:j * 128 + 128], m.ident[:, :])
                    last.then_inc(at_done, 1)
                    pe.wait_ge(at_ready, h * NT + i + 1)
                    for j in range(i + 1):
                        last = pe.matmul(flat[:, 3072 + i * 128:3072 + i * 128 + 128], v[:, j, :],
                                         AT[:, j * 128:j * 128 + 128], start=(j == 0), stop=(j == i))
                    last.then_inc(av_done, 1)
                pe.wait_ge(o_squared, h + 1)
                for g in range(2):
                    last = pe.matmul(m.ps[:, g, :], m.ones[:, :], so[:, g * 512:g * 512 + 512], start=True, stop=True)
                last.then_inc(o_meaned, 1)

        @block.scalar
        def _(act):
            step = Steps(act, act_step)
            act.sem_inc(o_read, 1)
            load_ln_exp(nc, act)
            with act.Fori(0, HEADS) as h:
                step.begin(h, 2)
                for n, (z, s, banks) in enumerate(((zq, sq, (0, 1, 2)), (zk, sk, (3, 4, 5)))):
                    act.wait_ge(projected[n], h + 1 + 1)
                    for (c0, w0), b in zip(GROUPS, banks):
                        act.activation(z[:, c0:c0 + w0], m.ps[:, b, 0:w0], ACT.Copy)
                        last = act.activation(s[:, c0:c0 + w0], m.ps[:, b, 0:w0], ACT.Square)
                    last.then_inc(squared[n], 1)
                for n, (rr, banks) in enumerate(((rq, (0, 1, 2)), (rk, (3, 4, 5)))):
                    act.wait_ge(meaned[n], h + 1)
                    for (c0, w0), b in zip(GROUPS, banks):
                        last = act.activation(rr[:, c0:c0 + w0], m.ps[:, b, 0:w0], ACT.Ln, bias=m.eps[:, :])
                    last.then_inc(ms_read[n], 1)
                    act.wait_ge(ms_read[n], h + 1)
                    act.activation(rr[:, :], rr[:, :], ACT.Exp, scale=-0.5).then_inc(r_ready[n], 1)

                def exps(i):
                    L = (i + 1) * 128
                    for mm in range(2):
                        act.wait_ge(max_ready, h * 16 + 2 * i + mm + 1)
                        act.activation(P[:, mm, 0:L], flat[:, 1024 * mm:1024 * mm + L], ACT.Exp,
                                       bias=nmx[:, mm:mm + 1], accum_out=l[:, mm:mm + 1]).then_inc(exp_done, 1)
                exps(0)
                for i in range(NT):
                    act.wait_ge(at_done, h * NT + i + 1 + 1)
                    L = (i + 1) * 128
                    act.activation(AT[:, 0:L], flat[:, 2048:2048 + L], ACT.Copy).then_inc(at_ready, 1)
                    if i + 1 < NT:
                        exps(i + 1)
                act.wait_ge(av_done, h * NT + NT)
                act.wait_ge(head_done, h + 1)
                for g in range(2):
                    step(act.activation(oT[:, g * 512:g * 512 + 512], m.ps[:, 6 + g, :], ACT.Copy))
                    last = act.activation(so[:, g * 512:g * 512 + 512], m.ps[:, 6 + g, :], ACT.Square)
                last.then_inc(o_squared, 1)
                act.wait_ge(o_meaned, h + 1)
                for g in range(2):
                    last = act.activation(ro[:, g * 512:g * 512 + 512], m.ps[:, g, :], ACT.Ln, bias=m.eps[:, :])
                last.then_inc(o_read, 1)
                act.wait_ge(o_read, h + 1 + 1)
                act.activation(ro[:, :], ro[:, :], ACT.Exp, scale=-0.5).then_inc(ro_ready, 1)
                step.end(HEADS)

        @block.vector
        def _(dve):
            step = Steps(dve, dve_step)
            dve.sem_inc(head_done, 1)
            with dve.Fori(0, HEADS) as h:
                step.begin(h, 44)
                dve.wait_ge(r_ready[0], h + 1)
                dve.wait_ge(saved, h * 3 + 1)
                dve.scalar_tensor_tensor(qT[:, :], zq[:, :], m.qw[:, :], rq[:, :], ALU.mult, ALU.mult).then_inc(q_ready, 1)
                dve.wait_ge(projected[2], h + 1 + 1)
                dve.wait_ge(stored, h * 64 + 1)
                for g in range(2):
                    step(dve.tensor_copy(v[:, 4 * g:4 * g + 4, :], m.ps[:, 6 + g, :].rearrange("p (t e) -> p t e", t=4)))
                dve.wait_ge(r_ready[1], h + 1)
                dve.scalar_tensor_tensor(kT[:, :], zk[:, :], m.kw[:, :], rk[:, :], ALU.mult, ALU.mult).then_inc(k_ready, 1)
                dve.wait_ge(v8_done, h + 1 + 1)
                dve.tensor_copy(v[0:NS, NT, :], m.ps[0:NS, 0, 0:128]).then_inc(v_ready, 1)
                dve.wait_ge(kt_done, h + 1)
                for g in range(2):
                    step(dve.tensor_copy(kt[:, 4 * g:4 * g + 4, :], m.ps[:, 3 + g, :].rearrange("p (t e) -> p t e", t=4)))
                dve.tensor_copy(kt[0:NS, NT, :], m.ps[0:NS, 5, 0:128]).then_inc(kt_ready, 1)

                def maxes(i):
                    L = (i + 1) * 128
                    for mm in range(2):
                        dve.wait_ge(scored, h * 16 + 2 * i + mm + 1)
                        d = flat[:, 1024 * mm + L - 128:1024 * mm + L]
                        step(dve.tensor_tensor(d, d, m.causal[:, :], ALU.add))
                        step.wait()
                        dve.tensor_reduce(nmx[:, mm:mm + 1], flat[:, 1024 * mm:1024 * mm + L], AX.X, ALU.max,
                                          negate=True).then_inc(max_ready, 1)
                maxes(0)
                for i in range(NT):
                    L = (i + 1) * 128
                    dve.wait_ge(exp_done, h * 16 + 2 * i + 2)
                    step(dve.reciprocal(r[:, :], l[:, :]))
                    step.wait()
                    step(dve.tensor_tensor(r[:, :], r[:, :], m.coef[:, :], ALU.mult))
                    step.wait()
                    dve.wait_ge(at_done, h * NT + i + 1)
                    step(dve.tensor_scalar(A[:, 0:L], P[:, 0, 0:L], r[:, 0:1], None, ALU.mult))
                    step.wait()
                    dve.scalar_tensor_tensor(A[:, 0:L], P[:, 1, 0:L], r[:, 1:2], A[:, 0:L],
                                             ALU.mult, ALU.add).then_inc(a_ready, 1)
                    if i + 1 < NT:
                        maxes(i + 1)
                dve.wait_ge(ro_ready, h + 1)
                dve.scalar_tensor_tensor(m.mixT[:, h, 0:SEQ], oT[:, :], m.subw[:, :], ro[:, :],
                                         ALU.mult, ALU.mult).then_inc(head_done, 1)
                step.end(HEADS)


def hgrn_phase(nc, a, out, m):
    w_in_d = a.w_in[0, :, :].rearrange("(k p) c -> p k c", p=128)
    NL = LEVELS + 1
    SL = list(range(SAMPLE_LEVELS)) + [LEVELS]
    ORDER = ("f", "q", "v", "g")
    FIRST = {"q": 1536, "f": 2048, "v": 2560, "g": 3072}
    with ExitStack() as ctx:
        sb, sem = scope(nc, ctx)
        w = {n: sb(f"h_w{n}", [128, KD, 128]) for n in ORDER}
        si = sb("h_si", [128, 128], I32)
        ti = sb("h_ti", [128, 128], I32)
        xi = sb("h_xi", [128, 128], I32)
        sh = sb("h_sh", [128, 128], I32)
        gt = sb("h_gt", [128, 128], I32)
        mask = sb("h_mask", [128, NL, 128], U8)
        bmask = sb("h_bmask", [NS, DB])
        keep = sb("h_keep", [128, TOK])
        sg, q, g, f, kk, lf, b, eb, qe, kd, oT, so, ro = (sb(f"h_{n}", [128, TOK]) for n in (
            "sg", "q", "g", "f", "kk", "lf", "b", "eb", "qe", "kd", "oT", "so", "ro"))
        E = sb("h_E", [128, 2, TOK])
        X = sb("h_X", [128, 2, TOK])
        AT = sb("h_AT", [128, TILES, 128])
        v = sb("h_v", [128, TILES, 128])
        ket = sb("h_ket", [128, TILES, 128])
        eB = sb("h_eB", [128, NT + DB])
        S = sb("h_S", [128, NT + 1, 128])
        Ss = sb("h_Ss", [128, DB, 128])
        Sn = sb("h_Sn", [128, DB, 128])
        vblk = sb("h_vblk", [NS, DB, 128])
        w_in = {n: sem(f"h_w_in_{n}") for n in ORDER}
        projected = {n: sem(f"h_projected_{n}") for n in ORDER}
        v8_done = sem("h_v8_done")
        sig = {n: sem(f"h_sigmoid_{n}") for n in ("f", "q", "g")}
        s_in, stored = sem("h_s_in"), sem("h_stored")
        f_ready, lf_ready, b_ready, q_ready, g_ready, v_ready, v8_ready = (sem(f"h_{n}_ready") for n in (
            "f", "lf", "b", "q", "g", "v", "v8"))
        sub_done, exp_done, x_ready, level_done, level_read = (sem(f"h_{n}") for n in (
            "sub_done", "exp_done", "x_ready", "level_done", "level_read"))
        kd_sub, kd_exp, eb_ready, ke_ready, qe_ready = (sem(f"h_{n}") for n in (
            "kd_sub", "kd_exp", "eb_ready", "ke_ready", "qe_ready"))
        ket_done, ket_ready, u_done, us_done, s_ready = (sem(f"h_{n}") for n in (
            "ket_done", "ket_ready", "u_done", "us_done", "s_ready"))
        at_zero, o_done, o_squared, o_meaned, o_read, ro_ready, head_done = (sem(f"h_{n}") for n in (
            "at_zero", "o_done", "o_squared", "o_meaned", "o_read", "ro_ready", "head_done"))
        gate, gate_pool = sem("h_gate"), sem("h_gate_pool")
        mixed = sem("h_mixed")
        iota_done, setup_step, dve_step = sem("h_iota_done"), sem("h_setup_step"), sem("h_dve_step")
        old_sems, m.old_sems = m.old_sems, sem.made
        block = ctx.enter_context(nc.Block())
        flat = m.ps[:, :, :].rearrange("p b n -> p (b n)")

        def halves(t, lv):
            c = 1 << lv
            wd = TOK if lv < SAMPLE_LEVELS else SEQ
            x = t[:, 0:wd].rearrange("p (n two c) -> p n two c", two=2, c=c)
            n = wd // (2 * c)
            return x[:, :, 0, :], x[:, :, 1, :], x[:, :, 0, c - 1:c].to_broadcast([128, n, c])

        @block.sync
        def _(sp):
            state = a.state_hgrn[0, :, :, :, :].rearrange("b h k v -> h k b v")
            new = out.hgrn_sample[0, :, :, :, :].rearrange("b h k v -> h k b v")
            sp.sem_inc(stored, 1)
            with sp.Fori(0, HEADS) as h:
                for n in ORDER:
                    sp.wait_ge(v8_done if n == "v" else projected[n], h + 1)
                    sp.dma_start(w[n][:, :, :], w_in_d[:, :, bass.ds(h * 128 + FIRST[n], 128)]).then_inc(w_in[n], 16)
                sp.wait_ge(head_done, h + 1)
                sp.dma_start(Ss[:, :, :], state[h, :, :, :]).then_inc(s_in, 16)
                sp.wait_ge(s_ready, h * 2 + 2)
                sp.dma_start(out.hgrn_prompt[0, 0, h, :, :], S[:, NT, :]).then_inc(stored, 16)
                sp.dma_start(new[h, :, :, :], Sn[:, :, :]).then_inc(stored, 16)
            sp.wait_ge(stored, 32 * HEADS + 1)

        @block.gpsimd
        def _(pool):
            for s in old_sems:
                pool.sem_clear(s)
            pool.iota(si[:, :], [[0, 128]], base=0, channel_multiplier=1).then_inc(iota_done, 1)
            pool.iota(ti[:, :], [[1, 128]], base=0, channel_multiplier=0).then_inc(iota_done, 1)
            pool.memset(S[:, 0, :], 0.0).then_inc(iota_done, 1)
            pool.memset(keep[:, :], 1.0).then_inc(iota_done, 1)
            pool.wait_ge(iota_done, 4)
            pool.memset(keep[:, 0:SEQ].rearrange("p (n c) -> p n c", c=128)[:, :, 0:1], 0.0).then_inc(iota_done, 1)
            pool.memset(keep[:, SEQ:TOK].rearrange("p (n c) -> p n c", c=DS)[:, :, 0:1], 0.0).then_inc(iota_done, 1)
            with pool.Fori(0, HEADS) as h:
                pool.wait_ge(o_done, h + 1)
                pool.sem_inc(gate_pool, 1)
                pool.memset(AT[:, :, :], 0.0).then_inc(at_zero, 1)
                pool.wait_ge(kd_exp, h + 1)
                pool.tensor_tensor(kd[:, :], kd[:, :], kk[:, :], ALU.mult).then_inc(ke_ready, 1)
                pool.wait_ge(q_ready, h + 1)
                pool.wait_ge(eb_ready, h + 1)
                pool.tensor_tensor(qe[:, :], eb[:, :], q[:, :], ALU.mult).then_inc(qe_ready, 1)
                for lv in range(LEVELS):
                    u = lv % 2
                    pool.wait_ge(exp_done, h * LEVELS + lv + 1)
                    if lv >= 2:
                        pool.wait_ge(level_done, h * NL + lv - 1)
                    ke, _, _ = halves(kk, lv)
                    _, qo, _ = halves(q, lv)
                    ee, eo, _ = halves(E[:, u, :], lv)
                    xe, xo, _ = halves(X[:, u, :], lv)
                    pool.tensor_tensor(xe, ee, ke, ALU.mult)
                    pool.tensor_tensor(xo, eo, qo, ALU.mult).then_inc(x_ready, 1)

        @block.tensor
        def _(pe):
            def project(n, banks):
                for (c0, w0), bk in zip(GROUPS, banks):
                    for k in range(KD):
                        last = pe.matmul(m.ps[:, bk, 0:w0], w[n][:, k, :], m.xT[:, k, c0:c0 + w0],
                                         start=(k == 0), stop=(k == KD - 1))
                last.then_inc(projected[n], 1)

            def project_v(t, bk, o):
                for k in range(KD):
                    last = pe.matmul(m.ps[0:rows(t), bk, o:o + 128], m.xT[:, k, cols(t)], w["v"][:, k, :],
                                     start=(k == 0), stop=(k == KD - 1))
                return last

            for s in (*projected.values(), v8_done, o_done):
                pe.sem_inc(s, 1)
            with pe.Fori(0, HEADS) as h:
                pe.wait_ge(o_read, h + 1)
                pe.wait_ge(w_in["f"], h * 16 + 16)
                project("f", (0, 1, 2))
                pe.wait_ge(w_in["q"], h * 16 + 16)
                project("q", (3, 4, 5))
                pe.wait_ge(w_in["v"], h * 16 + 16)
                for t in range(NT):
                    last = project_v(t, 6 + t // 4, t % 4 * 128)
                last.then_inc(projected["v"], 1)
                pe.wait_ge(w_in["g"], h * 16 + 16)
                pe.wait_ge(sig["f"], h + 1)
                project("g", (0, 1, 2))
                pe.wait_ge(q_ready, h + 1)
                project_v(NT, 3, 0).then_inc(v8_done, 1)
                pe.wait_ge(ke_ready, h + 1)
                pe.wait_ge(v_ready, h + 1)
                for t in range(TILES):
                    last = pe.transpose(flat[0:rows(t), (3072 + t * 128 if t < NT else 2560):(3200 + t * 128 if t < NT else 2688)],
                                        kd[:, cols(t)], m.ident[:, :])
                last.then_inc(ket_done, 1)
                pe.wait_ge(g_ready, h + 1)
                pe.wait_ge(v8_ready, h + 1)
                pe.wait_ge(ket_ready, h + 1)
                for t in range(NT):
                    last = pe.matmul(flat[:, 3072 + t * 128:3200 + t * 128], ket[:, t, :], v[:, t, :], start=True, stop=True)
                last.then_inc(u_done, 1)
                for lv in range(NL):
                    u = lv % 2
                    if lv < LEVELS:
                        pe.wait_ge(x_ready, h * LEVELS + lv + 1)
                        left = right = X[:, u, :]
                    else:
                        left, right = kk, q
                    if lv >= 2:
                        pe.wait_ge(level_read, h * NL + lv - 1)
                    for t in range(NT):
                        last = pe.matmul(flat[:, 1024 * u + t * 128:1024 * u + t * 128 + 128],
                                         left[:, cols(t)], right[:, cols(t)], start=True, stop=True)
                    if lv in SL:
                        last = pe.matmul(m.ps[0:NS, 4 + u, 0:NS], left[:, cols(NT)], right[:, cols(NT)], start=True, stop=True)
                    last.then_inc(level_done, 1)
                pe.wait_ge(level_read, h * NL + NL)
                for n in range(2):
                    last = pe.matmul(m.ps[:, 4 + n, :], ket[0:NS, NT, :],
                                     vblk[:, 4 * n:4 * n + 4, :].rearrange("p b e -> p (b e)"), start=True, stop=True)
                last.then_inc(us_done, 1)
                pe.wait_ge(s_ready, h * 2 + 1)
                pe.wait_ge(s_in, h * 16 + 16)
                for t in range(NT):
                    o = flat[:, t * 128:t * 128 + 128]
                    pe.matmul(o, S[:, t, :], qe[:, cols(t)], start=True, stop=False)
                    pe.matmul(o, v[:, t, :], AT[:, t, :], start=False, stop=True)
                for n in range(DB):
                    pe.matmul(m.ps[:, 2, n * DS:n * DS + DS], Ss[:, n, :], qe[:, SEQ + n * DS:SEQ + n * DS + DS],
                              start=(n == 0), stop=False, skip_group_check=True)
                last = pe.matmul(m.ps[:, 2, 0:NS], v[0:NS, NT, :], AT[0:NS, NT, 0:NS], start=False, stop=True,
                                 skip_group_check=True)
                last.then_inc(o_done, 1)
                pe.wait_ge(o_squared, h + 1)
                for o, s0, n0 in ((3 * 512, 0, 512), (6 * 512, 512, 512), (7 * 512, 1024, NS)):
                    last = pe.matmul(flat[:, o:o + n0], m.ones[:, :], so[:, s0:s0 + n0], start=True, stop=True)
                last.then_inc(o_meaned, 1)

        @block.scalar
        def _(act):
            OG = ((0, 0, 512), (1, 512, 512), (2, 1024, NS))
            act.sem_inc(o_read, 1)
            with act.Fori(0, HEADS) as h:
                for n, banks in (("f", (0, 1, 2)), ("q", (3, 4, 5)), ("g", (0, 1, 2))):
                    act.wait_ge(projected[n], h + 1 + 1)
                    if n == "g":
                        act.wait_ge(mixed, h + 1)
                    dst = {"f": f, "q": q, "g": g}[n]
                    for (c0, w0), bk in zip(GROUPS, banks):
                        last = act.activation(dst[:, c0:c0 + w0], m.ps[:, bk, 0:w0], ACT.Sigmoid)
                    last.then_inc(sig[n], 1)
                load_ln_exp(nc, act)
                act.wait_ge(f_ready, h + 1)
                act.activation(lf[:, :], f[:, :], ACT.Ln).then_inc(lf_ready, 1)
                act.wait_ge(b_ready, h + 1)
                bp = b[:, 0:SEQ].rearrange("p (n c) -> p n c", c=128)[:, :, 127:128]
                bs = b[:, SEQ:TOK].rearrange("p (n c) -> p n c", c=DS)[:, :, DS - 1:DS]
                act.activation(eB[:, 0:NT].unsqueeze(2), bp, ACT.Exp)
                act.activation(eB[:, NT:NT + DB].unsqueeze(2), bs, ACT.Exp)
                act.activation(eb[:, :], b[:, :], ACT.Exp).then_inc(eb_ready, 1)
                act.wait_ge(kd_sub, h + 1)
                act.activation(kd[:, :], kd[:, :], ACT.Exp).then_inc(kd_exp, 1)
                for lv in range(LEVELS):
                    wd = TOK if lv < SAMPLE_LEVELS else SEQ
                    act.wait_ge(sub_done, h * LEVELS + lv + 1)
                    act.activation(E[:, lv % 2, 0:wd], E[:, lv % 2, 0:wd], ACT.Exp).then_inc(exp_done, 1)
                act.wait_ge(o_done, h + 1 + 1)
                act.wait_ge(head_done, h + 1)
                for bk, s0, n0 in OG:
                    act.activation(oT[:, s0:s0 + n0], m.ps[:, bk, 0:n0], ACT.Copy)
                    last = act.activation(so[:, s0:s0 + n0], m.ps[:, bk, 0:n0], ACT.Square)
                last.then_inc(o_squared, 1)
                act.wait_ge(o_meaned, h + 1)
                for bk, (_, s0, n0) in zip((3, 6, 7), OG):
                    last = act.activation(ro[:, s0:s0 + n0], m.ps[:, bk, 0:n0], ACT.Ln, bias=m.eps[:, :])
                last.then_inc(o_read, 1)
                act.wait_ge(o_read, h + 1 + 1)
                act.activation(ro[:, :], ro[:, :], ACT.Exp, scale=-0.5).then_inc(ro_ready, 1)

        @block.vector
        def _(dve):
            setup = Steps(dve, setup_step)
            dve.wait_ge(iota_done, 6)
            setup(dve.tensor_tensor(xi[:, :], si[:, :], ti[:, :], ALU.bitwise_xor))
            setup(dve.tensor_tensor(gt[:, :], ti[:, :], si[:, :], ALU.is_gt))
            setup(dve.tensor_tensor(mask[:, LEVELS, :], ti[:, :], si[:, :], ALU.is_equal))
            setup.wait()
            setup(dve.tensor_scalar(sh[:, :], si[:, :], 3, None, ALU.logical_shift_right))
            setup.wait()
            setup(dve.tensor_tensor(bmask[:, :], sh[0:NS, 0:DB], ti[0:NS, 0:DB], ALU.is_equal))
            setup.wait()
            for lv in range(LEVELS):
                setup(dve.tensor_scalar(sh[:, :], xi[:, :], lv, None, ALU.logical_shift_right))
                setup.wait()
                setup(dve.scalar_tensor_tensor(mask[:, lv, :], sh[:, :], 1, gt[:, :], ALU.is_equal, ALU.mult))
                setup.wait()
            step = Steps(dve, dve_step)
            dve.sem_inc(head_done, 1)
            dve.sem_inc(mixed, 1)
            with dve.Fori(0, HEADS) as h:
                step.begin(h, 19)
                dve.wait_ge(sig["f"], h + 1)
                step(dve.tensor_scalar(f[:, :], f[:, :], m.lb1[:, bass.ds(h, 1)], m.lb[:, bass.ds(h, 1)], ALU.mult, ALU.add))
                step.wait()
                dve.sem_inc(f_ready, 1)
                step(dve.tensor_scalar(kk[:, :], f[:, :], -1.0, 1.0, ALU.mult, ALU.add))
                dve.wait_ge(lf_ready, h + 1)
                dve.tensor_tensor_scan(b[:, :], keep[:, :], lf[:, :], 0.0, ALU.mult, ALU.add).then_inc(b_ready, 1)
                dve.wait_ge(b_ready, h + 1)
                for c0, c1, c in ((0, SEQ, 128), (SEQ, TOK, DS)):
                    bv = b[:, c0:c1].rearrange("p (n c) -> p n c", c=c)
                    kv = kd[:, c0:c1].rearrange("p (n c) -> p n c", c=c)
                    last = dve.tensor_tensor(kv, bv[:, :, c - 1:c].to_broadcast([128, (c1 - c0) // c, c]), bv, ALU.subtract)
                last.then_inc(kd_sub, 1)

                def subs(lv):
                    if lv >= 2:
                        dve.wait_ge(x_ready, h * LEVELS + lv - 1)
                    be, bo, br = halves(b, lv)
                    ee, eo, _ = halves(E[:, lv % 2, :], lv)
                    dve.tensor_tensor(ee, br, be, ALU.subtract)
                    dve.tensor_tensor(eo, bo, br, ALU.subtract).then_inc(sub_done, 1)

                def collect(lv):
                    dve.wait_ge(level_done, h * NL + lv + 1)
                    if lv:
                        dve.wait_ge(level_read, h * NL + lv)
                    dve.sem_inc(gate, 1)
                    u = lv % 2
                    mk = mask[:, lv, :].unsqueeze(1).to_broadcast([128, 4, 128])
                    for g2 in range(2):
                        last = dve.copy_predicated(AT[:, 4 * g2:4 * g2 + 4, :], mk,
                                                   m.ps[:, 2 * u + g2, :].rearrange("p (t n) -> p t n", t=4))
                    if lv in SL:
                        last = dve.copy_predicated(AT[0:NS, NT, 0:NS], mask[0:NS, lv, 0:NS], m.ps[0:NS, 4 + u, 0:NS])
                    last.then_inc(level_read, 1)

                subs(0)
                subs(1)
                dve.wait_ge(sig["q"], h + 1)
                for (c0, w0), bk in zip(GROUPS, (3, 4, 5)):
                    last = dve.tensor_tensor(q[:, c0:c0 + w0], q[:, c0:c0 + w0], m.ps[:, bk, 0:w0], ALU.mult)
                last.then_inc(q_ready, 1)
                dve.wait_ge(projected["v"], h + 1 + 1)
                for n in range(2):
                    last = dve.tensor_copy(v[:, 4 * n:4 * n + 4, :], m.ps[:, 6 + n, :].rearrange("p (t e) -> p t e", t=4))
                last.then_inc(v_ready, 1)
                dve.wait_ge(sig["g"], h + 1)
                for (c0, w0), bk in zip(GROUPS, (0, 1, 2)):
                    last = dve.tensor_tensor(g[:, c0:c0 + w0], g[:, c0:c0 + w0], m.ps[:, bk, 0:w0], ALU.mult)
                last.then_inc(g_ready, 1)
                dve.wait_ge(v8_done, h + 1 + 1)
                step(dve.tensor_copy(v[0:NS, NT, :], m.ps[0:NS, 3, 0:128]))
                step.wait()
                dve.tensor_tensor(vblk[:, :, :], v[0:NS, NT, :].unsqueeze(1).to_broadcast([NS, DB, 128]),
                                  bmask[:, :].unsqueeze(2).to_broadcast([NS, DB, 128]), ALU.mult).then_inc(v8_ready, 1)
                dve.wait_ge(ket_done, h + 1)
                for n in range(2):
                    dve.tensor_copy(ket[:, 4 * n:4 * n + 4, :], m.ps[:, 6 + n, :].rearrange("p (t e) -> p t e", t=4))
                dve.tensor_copy(ket[0:NS, NT, :], m.ps[0:NS, 5, 0:128]).then_inc(ket_ready, 1)
                dve.wait_ge(at_zero, h + 1)
                collect(0)
                subs(2)
                dve.wait_ge(eb_ready, h + 1)
                dve.wait_ge(u_done, h + 1)
                dve.wait_ge(stored, h * 32 + 1)
                for t in range(NT):
                    ins = dve.scalar_tensor_tensor(S[:, t + 1, :], S[:, t, :], eB[:, t:t + 1],
                                                   flat[:, 3072 + t * 128:3200 + t * 128], ALU.mult, ALU.add)
                    step(ins)
                    step.wait()
                dve.sem_inc(s_ready, 1)
                for lv in range(1, NL):
                    collect(lv)
                    if lv + 2 < LEVELS:
                        subs(lv + 2)
                dve.wait_ge(us_done, h + 1)
                dve.wait_ge(s_in, h * 16 + 16)
                for n in range(DB):
                    step(dve.scalar_tensor_tensor(Sn[:, n, :], Ss[:, n, :], eB[:, NT + n:NT + n + 1],
                                                  flat[:, 2048 + n * 128:2176 + n * 128], ALU.mult, ALU.add))
                step.wait()
                dve.sem_inc(s_ready, 1)
                dve.wait_ge(ro_ready, h + 1)
                dve.scalar_tensor_tensor(oT[:, :], oT[:, :], m.hgw[:, :], ro[:, :], ALU.mult, ALU.mult).then_inc(head_done, 1)
                dve.wait_ge(head_done, h + 1 + 1)
                dve.tensor_tensor(m.mixT[:, bass.ds(h + HEADS, 1), :].squeeze(1), oT[:, :], g[:, :], ALU.mult).then_inc(mixed, 1)
                step.end(HEADS)


def decode_phase(nc, a, out, m):
    KEYS = PAGES * PAGE
    with ExitStack() as ctx:
        sb, sem = scope(nc, ctx)
        pt = sb("d_pt", [1, DB * PAGES], I32)
        K = sb("d_K", [128, 2, PG, 512])
        V = sb("d_V", [128, 2, PAGES, 512])
        Vn = sb("d_Vn", [DS, 2, 512])
        sN = sb("d_sN", [128, DS])
        KT = sb("d_KT", [128, 2, HEADS, PG * PAGE])
        qb = sb("d_qb", [128, 2, HEADS, 32])
        kb = sb("d_kb", [128, 2, HEADS, DS])
        P = sb("d_P", [128, 2, KEYS + DS])
        PT = sb("d_PT", [128, 2, PG * 128])
        PTn = sb("d_PTn", [DS, 128])
        O = sb("d_O", [128, 512])
        pat0 = sb("d_pat0", [128, 32])
        pat1 = sb("d_pat1", [128, 32])
        pat = sb("d_pat", [128, 32])
        C = sb("d_C", [128, 2, 32])
        cmask = sb("d_cmask", [128, DS])
        pr = sb("d_pr", [128, 1], I32)
        tq = sb("d_tq", [128, 1], I32)
        tk = sb("d_tk", [128, DS], I32)
        tqf = sb("d_tqf", [128, 1])
        mx = sb("d_mx", [128, 2])
        nmx = sb("d_nmx", [128, 1])
        l = sb("d_l", [128, 2])
        r = sb("d_r", [128, 1])
        oS = sb("d_oS", [128, HEADS, NS])
        so = sb("d_so", [128, HEADS, NS])
        ro = sb("d_ro", [128, HEADS, NS])
        gate = sem("d_gate")
        pt_in = sem("d_pt_in")
        k_in = [sem("d_k_in0"), sem("d_k_in1")]
        v_in = [sem("d_v_in0"), sem("d_v_in1")]
        kt_done = sem("d_kt_done")
        kt_ready = [sem("d_kt_ready_even"), sem("d_kt_ready_odd")]
        qb_ready, scored, max_ready, exp_done, c_ready = (sem(f"d_{n}") for n in (
            "qb_ready", "scored", "max_ready", "exp_done", "c_ready"))
        pt_done, pt_ready, new_done, new_read = (sem(f"d_{n}") for n in ("pt_done", "pt_ready", "new_done", "new_read"))
        av_done, acc_ready, picked, o_ready = (sem(f"d_{n}") for n in ("av_done", "acc_ready", "picked", "o_ready"))
        o_squared, o_meaned, o_read, ro_ready = (sem(f"d_{n}") for n in ("o_squared", "o_meaned", "o_read", "ro_ready"))
        iota_done, setup_step, dve_step, act_step = (sem(f"d_{n}") for n in (
            "iota_done", "setup_step", "dve_step", "act_step"))
        block = ctx.enter_context(nc.Block())
        flat = m.ps[:, :, :].rearrange("p b n -> p (b n)")
        kc = a.cache_k[0, :, :, :, :].rearrange("n p h e -> n p (h e)")
        vc = a.cache_v[0, :, :, :, :].rearrange("n p h e -> n p (h e)")
        S_NEW, PT_NEW, OT = m.ps[:, 4, 0:DS], m.ps[0:DS, 4, 128:256], m.ps[:, 7, 0:HEADS * DS]
        VROUND = (PAGES + 1) * 16

        def requests(eng, unit):
            unit(0, 0, None)
            with eng.Fori(0, DB // 2 - 1) as i:
                unit(i * 2 + 1, 1, i)
                unit(i * 2 + 2, 0, i)
            unit(DB - 1, 1, DB // 2 - 1)

        @block.sync
        def _(sp):
            sp.dma_start(pt[:, :], a.page_table.rearrange("(o b) n -> o (b n)", o=1)).then_inc(pt_in, 16)
            sp.wait_ge(pt_in, 16)

            def page_numbers(b, g):
                _, pages = nc.values_load_multi_w_load_instructions(
                    pt[0:1, bass.ds(b * PAGES + g * PG, PG)], engines=[mybir.EngineType.SP], min_val=0,
                    max_val=a.cache_k.shape[1] - 1)
                return pages

            def load_keys(b, g, pages, early):
                if not early or b * NPG + g >= 2:
                    sp.wait_ge(kt_done, (b * NPG + g - 1) * HEADS)
                    sp.sem_inc(gate, 1)
                for j, page in enumerate(pages):
                    sp.dma_start(K[:, g % 2, j, :], kc[page, :, :]).then_inc(k_in[g % 2], 16)

            def load_values(u, g, pages):
                for j, page in enumerate(pages):
                    sp.dma_start(V[:, u, g * PG + j, :], vc[page, :, :]).then_inc(v_in[u], 16)

            def load(b, u, early):
                pages = [page_numbers(b, g) for g in range(2)]
                for g in range(2):
                    load_keys(b, g, pages[g], early)
                if not early:
                    sp.wait_ge(av_done, b - 1)
                    sp.sem_inc(gate, 1)
                for g in range(2):
                    load_values(u, g, pages[g])
                for g in range(2, NPG):
                    more = page_numbers(b, g)
                    load_keys(b, g, more, early)
                    load_values(u, g, more)
                sp.dma_start(Vn[:, u, :], out.v_sample[0, b, :, :, :].rearrange("t h e -> t (h e)")).then_inc(v_in[u], 16)
            load(0, 0, True)
            load(1, 1, True)
            with sp.Fori(1, DB // 2) as i:
                for u in range(2):
                    load(i * 2 + u, u, False)

        @block.gpsimd
        def _(pool):
            pool.memset(pat0[:, :], 0.0).then_inc(iota_done, 1)
            pool.memset(pat1[:, :], 0.0).then_inc(iota_done, 1)
            pool.iota(pr[:, :], [[0, 1]], base=0, channel_multiplier=1).then_inc(iota_done, 1)
            pool.iota(tk[:, :], [[1, DS]], base=0, channel_multiplier=0).then_inc(iota_done, 1)
            pool.wait_ge(iota_done, 4)
            for p, base in ((pat0, 0), (pat1, -DS)):
                v = p[:, :].rearrange("p (h t) -> p h t", h=HEADS)
                pool.affine_select(out=v, in_=v, compare_op=ALU.not_equal, fill=1.0, base=base,
                                   pattern=[[-32, HEADS], [-1, DS]], channel_multiplier=1).then_inc(iota_done, 1)

        @block.tensor
        def _(pe):
            def transpose_keys(b, g, h, first):
                if h == 0:
                    pe.wait_ge(k_in[g % 2], (b * 2 + g // 2 + 1) * PG * 16)
                if not (first and g == 0 and h < 2):
                    pe.wait_ge(kt_ready[h % 2], b * 8 + g * 2 + h // 2)
                if not first and g == 0 and h == 0:
                    pe.wait_ge(new_read, b)
                for j in range(PG):
                    ins = pe.transpose(m.ps[:, 4 + h % 2, j * 128:j * 128 + 128],
                                       K[:, g % 2, j, h * 128:h * 128 + 128], m.ident[:, :])
                ins.then_inc(kt_done, 1)

            def score(b, u, g, h):
                pe.wait_ge(kt_ready[h % 2], b * 8 + g * 2 + h // 2 + 1)
                return pe.matmul(m.ps[32 * h:32 * h + 32, g, :], qb[:, u, h, :], KT[:, g % 2, h, :],
                                 start=True, stop=True)

            def transpose_map(b, u, g):
                if g:
                    pe.wait_ge(pt_ready, b * NPG + g)
                else:
                    pe.wait_ge(exp_done, b + 1)
                    pe.wait_ge(o_ready, b + 1)
                for j in range(PG):
                    p = (g * PG + j) * 128
                    ins = pe.transpose(m.ps[:, 7, j * 128:j * 128 + 128], P[:, u, p:p + 128], m.ident[:, :])
                ins.then_inc(pt_done, 1)

            def values(b, u, g):
                pe.wait_ge(pt_ready, b * NPG + g + 1)
                for j in range(PG):
                    pe.matmul(m.ps[:, 6, :], PT[:, g % 2, j * 128:j * 128 + 128], V[:, u, g * PG + j, :],
                              start=(g == 0 and j == 0), stop=False)

            def new_values(b, u):
                pe.wait_ge(new_read, b + 2)
                pe.matmul(m.ps[:, 6, :], PTn[:, :], Vn[:, u, :], start=False, stop=True).then_inc(av_done, 1)

            def pick(b, u):
                pe.wait_ge(acc_ready, b + 1)
                pe.wait_ge(c_ready, b + 1)
                for h in range(HEADS):
                    ins = pe.matmul(m.ps[:, 7, h * DS:h * DS + DS], O[:, h * 128:h * 128 + 128],
                                    C[:, u, h * DS:h * DS + DS], start=True, stop=True)
                ins.then_inc(picked, 1)

            def unit(b, u, i):
                last = isinstance(b, int) and b == DB - 1
                pe.wait_ge(qb_ready, b + 1)
                if i is not None:
                    pe.wait_ge(exp_done, b)
                for g in range(1, NPG):
                    for h in range(HEADS):
                        transpose_keys(b, g, h, i is None)
                        score(b, u, g - 1, h)
                    if i is not None:
                        if g == 1:
                            pe.wait_ge(v_in[1 - u], i * VROUND + VROUND)
                        else:
                            values(b - 1, 1 - u, g - 2)
                        transpose_map(b - 1, 1 - u, g - 1)
                for h in range(HEADS):
                    score(b, u, NPG - 1, h)
                for h in range(HEADS):
                    ins = pe.matmul(m.ps[32 * h:32 * h + 32, 4, 0:DS], qb[:, u, h, :],
                                    kb[:, u, h, :], start=True, stop=True)
                ins.then_inc(scored, 1)
                if i is not None:
                    pe.transpose(PT_NEW, P[:, 1 - u, KEYS:KEYS + DS], m.ident[:, :]).then_inc(new_done, 1)
                    values(b - 1, 1 - u, 2)
                    transpose_map(b - 1, 1 - u, 3)
                if not last:
                    for h in range(2):
                        transpose_keys(b + 1, 0, h, False)
                if i is not None:
                    values(b - 1, 1 - u, 3)
                    new_values(b - 1, 1 - u)
                if not last:
                    for h in range(2, HEADS):
                        transpose_keys(b + 1, 0, h, False)
                if i is not None:
                    pick(b - 1, 1 - u)
            for h in range(HEADS):
                transpose_keys(0, 0, h, True)
            requests(pe, unit)
            pe.wait_ge(v_in[1], DB // 2 * VROUND)
            pe.wait_ge(new_read, DB)
            pe.wait_ge(exp_done, DB)
            pe.transpose(PT_NEW, P[:, 1, KEYS:KEYS + DS], m.ident[:, :]).then_inc(new_done, 1)
            for g in range(NPG):
                transpose_map(DB - 1, 1, g)
                values(DB - 1, 1, g)
            new_values(DB - 1, 1)
            pick(DB - 1, 1)
            pe.wait_ge(o_squared, 1)
            pe.matmul(m.ps[:, 0, 0:HEADS * NS], m.ones[:, :], so[:, :, :].rearrange("p h t -> p (h t)"),
                      start=True, stop=True).then_inc(o_meaned, 1)

        @block.scalar
        def _(act):
            load_ln_exp(nc, act)

            def keys(b, g):
                for h in (1, 3):
                    act.wait_ge(kt_done, b * 16 + g * 4 + h + 1)
                    act.activation(KT[:, g % 2, h, :], m.ps[:, 5, :], ACT.Copy).then_inc(kt_ready[1], 1)

            def map_out(b, g):
                act.wait_ge(pt_done, b * NPG + g + 1)
                act.activation(PT[:, g % 2, :], m.ps[:, 7, :], ACT.Copy).then_inc(pt_ready, 1)

            def unit(b, u, i):
                for g in range(1, NPG):
                    keys(b, g)
                    if i is not None and g >= 2:
                        map_out(b - 1, g - 1)
                act.wait_ge(max_ready, b + 1)
                act.activation(P[:, u, 0:KEYS], flat[:, 0:KEYS], ACT.Exp, bias=nmx[:, :], accum_out=l[:, 0:1])
                act.activation(P[:, u, KEYS:KEYS + DS], sN[:, :], ACT.Exp, bias=nmx[:, :],
                               accum_out=l[:, 1:2]).then_inc(exp_done, 1)
                if not (isinstance(b, int) and b == DB - 1):
                    keys(b + 1, 0)
            keys(0, 0)
            requests(act, unit)
            for g in (1, 2):
                map_out(DB - 1, g)
            act.wait_ge(o_ready, DB + 1)
            act.activation(so[:, :, :], oS[:, :, :], ACT.Square).then_inc(o_squared, 1)
            act.wait_ge(o_meaned, 1)
            mean = m.ps[:, 0, 0:HEADS * NS].rearrange("p (h t) -> p h t", h=HEADS)
            act.activation(ro[:, :, :], mean, ACT.Ln, bias=m.eps[:, :]).then_inc(o_read, 1)
            act.wait_ge(o_read, 1)
            act.activation(ro[:, :, :], ro[:, :, :], ACT.Exp, scale=-0.5).then_inc(ro_ready, 1)

        @block.vector
        def _(dve):
            setup = Steps(dve, setup_step)
            dve.wait_ge(iota_done, 6)
            setup(dve.tensor_scalar(tq[:, :], pr[:, :], DS - 1, None, ALU.bitwise_and))
            setup(dve.scalar_tensor_tensor(pat[:, :], pat1[:, :], m.coef[:, 1:2], pat0[:, :], ALU.mult, ALU.add))
            setup.wait()
            setup(dve.tensor_copy(tqf[:, :], tq[:, :]))
            setup.wait()
            setup(dve.tensor_scalar(cmask[:, :], tk[:, :], tqf[:, :], NEG, ALU.is_gt, ALU.mult))
            setup.wait()
            dve.sem_inc(o_ready, 1)
            step = Steps(dve, dve_step)

            def keys(b, g):
                for h in (0, 2):
                    dve.wait_ge(kt_done, b * 16 + g * 4 + h + 1)
                    dve.tensor_copy(KT[:, g % 2, h, :], m.ps[:, 4, :]).then_inc(kt_ready[0], 1)

            def queries(b, u):
                dve.tensor_copy(kb[:, u, :, :], m.kS[:, :, bass.ds(b * DS, DS)])
                dve.tensor_copy(qb[:, u, :, :], m.qbd[:, :, bass.ds(b, 1), :].squeeze(2)).then_inc(qb_ready, 1)

            def map_out(b, g):
                dve.wait_ge(pt_done, b * NPG + g + 1)
                dve.tensor_copy(PT[:, g % 2, :], m.ps[:, 7, :]).then_inc(pt_ready, 1)

            def new_map(b):
                dve.wait_ge(new_done, b + 1)
                dve.tensor_copy(PTn[:, :], PT_NEW).then_inc(new_read, 1)

            def collect(b):
                dve.wait_ge(av_done, b + 1)
                dve.tensor_copy(O[:, :], m.ps[:, 6, :]).then_inc(acc_ready, 1)

            def unit(b, u, i):
                last = isinstance(b, int) and b == DB - 1
                for g in range(1, NPG):
                    keys(b, g)
                    if i is not None and g == 1:
                        map_out(b - 1, 0)
                dve.wait_ge(scored, b + 1)
                if i is not None:
                    dve.wait_ge(new_done, b)
                step(dve.tensor_tensor(sN[:, :], S_NEW, cmask[:, :], ALU.add))
                if i is not None:
                    new_map(b - 1)
                step.wait()
                if i is None:
                    dve.sem_inc(new_read, 1)
                step(dve.tensor_reduce(mx[:, 0:1], flat[:, 0:KEYS], AX.X, ALU.max))
                step(dve.tensor_reduce(mx[:, 1:2], sN[:, :], AX.X, ALU.max))
                step.wait()
                dve.tensor_reduce(nmx[:, :], mx[:, :], AX.X, ALU.max, negate=True).then_inc(max_ready, 1)
                if i is not None:
                    map_out(b - 1, 3)
                if not last:
                    queries(b + 1, 1 - u)
                    keys(b + 1, 0)
                dve.wait_ge(exp_done, b + 1)
                step(dve.tensor_tensor(r[:, :], l[:, 0:1], l[:, 1:2], ALU.add))
                step.wait()
                step(dve.reciprocal(r[:, :], r[:, :]))
                step.wait()
                dve.tensor_scalar(C[:, u, :], pat[:, :], r[:, :], None, ALU.mult).then_inc(c_ready, 1)
                if i is not None:
                    collect(b - 1)
                    place(b - 1)

            def place(b):
                dve.wait_ge(picked, b + 1)
                dve.tensor_copy(oS[:, :, bass.ds(b * DS, DS)], OT.rearrange("p (h t) -> p h t", h=HEADS)).then_inc(o_ready, 1)
            queries(0, 0)
            keys(0, 0)
            unit(0, 0, None)
            with dve.Fori(0, DB // 2 - 1) as i:
                step.begin(i, 10)
                unit(i * 2 + 1, 1, i)
                unit(i * 2 + 2, 0, i)
                step.end(DB // 2 - 1)
            unit(DB - 1, 1, DB // 2 - 1)
            new_map(DB - 1)
            map_out(DB - 1, 0)
            map_out(DB - 1, 3)
            collect(DB - 1)
            place(DB - 1)
            dve.wait_ge(ro_ready, 1)
            dve.scalar_tensor_tensor(m.mixT[:, 0:HEADS, SEQ:TOK], oS[:, :, :], m.subw[:, :], ro[:, :, :],
                                     ALU.mult, ALU.mult)


def mix_phase(nc, a, m):
    NR = NG + NE
    with ExitStack() as ctx:
        sb, sem = scope(nc, ctx)
        wo = sb("m_wo", [128, KD, D])
        wr = sb("m_wr", [128, KD, NR])
        br = sb("m_br", [128, NR])
        xb = sb("m_xb", [128, 2, D])
        hs = sb("m_hs", [128, 2, D])
        ss = sb("m_ss", [128, 2])
        LG = sb("m_LG", [128, TILES, NR])
        place = sb("m_place", [128, TILES, EG])
        gm, gz, tm, v1, v2, w1, w2 = (sb(f"m_{n}", [128, TILES]) for n in ("gm", "gz", "tm", "v1", "v2", "w1", "w2"))
        t4, ohg, oh1, oh2, es, ge = (sb(f"m_{n}", [128, TILES, EG]) for n in ("t4", "ohg", "oh1", "oh2", "es", "ge"))
        t16 = sb("m_t16", [128, TILES, NG, EG])
        sel1, sel2, sel, pos = (sb(f"m_{n}", [128, TILES, NE]) for n in ("sel1", "sel2", "sel", "pos"))
        pre = sb("m_pre", [128, TILES + 1, NE])
        before = sb("m_before", [128, 128])
        valid = sb("m_valid", [128, TILES])
        tokf = sb("m_tokf", [128, TILES])
        zero = sb("m_zero", [SLOTS, 128])
        one16 = sb("m_one16", [128, NE])
        cnt, tl, cumf, base = (sb(f"m_{n}", [128, NE]) for n in ("cnt", "tl", "cumf", "base"))
        cnti, tli = sb("m_cnti", [128, NE], I32), sb("m_tli", [128, NE], I32)
        posf = sb("m_posf", [128, 2, TILES])
        tilef = sb("m_tilef", [1, SLOTS])
        over = sb("m_over", [1, SLOTS, NE])
        ef = sb("m_ef", [1, SLOTS])
        third = sb("m_third", [1, SLOTS], I32)
        rows_t = sb("m_rows_t", [SLOTS, 128])
        wo_in = [sem("m_wo_in0"), sem("m_wo_in1")]
        wr_in = sem("m_wr_in")
        x_in = [sem("m_x_in0"), sem("m_x_in1")]
        mixed, h_ready, squared, hs_ready, transposed, evacuated, routed, logits = (sem(f"m_{n}") for n in (
            "mixed", "h_ready", "squared", "hs_ready", "transposed", "evacuated", "routed", "logits"))
        act_step, dve_step, pool_step = sem("m_act_step"), sem("m_dve_step"), sem("m_pool_step")
        shifted, exp_done, v_diff, exp2_done = (sem(f"m_{n}") for n in ("shifted", "exp_done", "v_diff", "exp2_done"))
        hn_stored = [sem("m_hn_stored0"), sem("m_hn_stored1")]
        zeroed, scattered, rows_in = (sem(f"m_{n}") for n in ("zeroed", "scattered", "rows_in"))
        sel_ready, counted, pos_ready, rows_done = (sem(f"m_{n}") for n in ("sel_ready", "counted", "pos_ready", "rows_done"))
        block = ctx.enter_context(nc.Block())
        wo_d = a.w_out[0, :, :].rearrange("(k p) n -> p k n", p=128)
        xp = a.x_prompt[0, :, :].rearrange("(t p) d -> t p d", p=128)
        wrg = a.w_router_grp[0, :, :].rearrange("(k p) n -> p k n", p=128)
        wre = a.w_router_exp[0, :, :].rearrange("(k p) n -> p k n", p=128)

        @block.sync
        def _(sp):
            def store(t):
                sp.wait_ge(hs_ready, t + 1)
                sp.dma_start(m.hn_rows[t * 128:t * 128 + rows(t), :], hs[0:rows(t), t % 2, :]).then_inc(hn_stored[t % 2], 16)

            for t in range(TILES):
                if t >= 2:
                    store(t - 2)
                u, n = t % 2, rows(t)
                if t >= 2:
                    sp.wait_ge(h_ready, 2 * (t - 1))
                src = xp[t, :, :] if t < NT else a.x_sample.rearrange("b t d -> (b t) d")
                sp.dma_start(xb[0:n, u, :], src).then_inc(x_in[u], 16)
                if t == 0:
                    for n in range(2):
                        sp.dma_start(wo[:, :, n * 512:n * 512 + 512], wo_d[:, :, n * 512:n * 512 + 512]).then_inc(wo_in[n], 16)
                    with nc.allow_non_contiguous_dma("small router weights"):
                        sp.dma_start(wr[:, :, 0:NG], wrg).then_inc(wr_in, 16)
                        sp.dma_start(wr[:, :, NG:NR], wre).then_inc(wr_in, 16)
                        sp.dma_start(br[:, 0:NG], a.b_router_grp[0, :].partition_broadcast(128)).then_inc(wr_in, 16)
                        sp.dma_start(br[:, NG:NR], a.b_router_exp[0, :].partition_broadcast(128)).then_inc(wr_in, 16)

            store(TILES - 2)
            store(TILES - 1)
            sp.wait_ge(scattered, 16 * 2 * TILES)
            sp.dma_start(rows_t[:, :], m.slot_rows.rearrange("(i p) o -> i (p o)", p=128)).then_inc(rows_in, 16)
            sp.wait_ge(hn_stored[0], 16 * (TILES // 2 + 1))
            sp.wait_ge(hn_stored[1], 16 * (TILES // 2))

        @block.gpsimd
        def _(pool):
            step = Steps(pool, pool_step)

            def do(ins):
                step(ins)
                step.wait()
            do(pool.memset(LG[:, :, :], 0.0))
            for e in range(EG):
                do(pool.memset(place[:, :, e:e + 1], float(EG - e)))
            do(pool.memset(before[:, :], 0.0))
            do(pool.affine_select(out=before[:, :], in_=before[:, :], compare_op=ALU.is_ge, fill=1.0,
                                  base=0, pattern=[[-1, 128]], channel_multiplier=1))
            do(pool.memset(valid[:, :], 1.0))
            do(pool.memset(valid[NS:128, NT:TILES], 0.0))
            do(pool.memset(pre[:, 0, :], 0.0))
            do(pool.memset(one16[:, :], 1.0))
            do(pool.memset(zero[:, :], 0.0))
            pool.dma_start(m.slot_rows.rearrange("(i p) o -> i (p o)", p=128), zero[:, :]).then_inc(zeroed, 16)
            do(pool.iota(tokf[:, :], [[128, TILES]], base=0, channel_multiplier=1, allow_small_or_imprecise_dtypes=True))
            do(pool.iota(tilef[:, :], [[1, SLOTS]], base=0, channel_multiplier=0, allow_small_or_imprecise_dtypes=True))
            pool.wait_ge(zeroed, 16)
            pool.wait_ge(pos_ready, 1)
            for p in (m.pos1, m.pos2):
                for t in range(TILES):
                    n = rows(t)
                    pool.indirect_dma_start(m.slot_rows, bass.IndirectOffsetOnAxis(ap=p[0:n, t:t + 1], axis=0),
                                            tokf[0:n, t:t + 1], None).then_inc(scattered, 16)
            pool.wait_ge(scattered, 16 * 2 * TILES)

        POOL_ALL = EG + 10

        @block.tensor
        def _(pe):
            def project(t):
                u, n = t % 2, rows(t)
                for b in range(2):
                    if t == 0:
                        pe.wait_ge(wo_in[b], 16)
                    if t >= 2:
                        pe.wait_ge(h_ready, 2 * (t - 2) + b + 1)
                    for k in range(KD):
                        ins = pe.matmul(m.ps[0:n, 2 * u + b, :], m.mixT[:, k, cols(t)], wo[:, k, b * 512:b * 512 + 512],
                                        start=(k == 0), stop=(k == KD - 1))
                    ins.then_inc(mixed, 1)

            def route(t):
                u, n = t % 2, rows(t)
                pe.wait_ge(hs_ready, t + 1)
                for b in range(2):
                    if t >= 1:
                        pe.wait_ge(evacuated, 2 * (t - 1) + b + 1)
                    for c in range(4):
                        k = 4 * b + c
                        ins = pe.transpose(m.ps[:, 4 + b, c * 128:c * 128 + n], hs[0:n, u, k * 128:k * 128 + 128],
                                           m.ident[0:n, 0:n])
                    ins.then_inc(transposed, 1)
                pe.wait_ge(evacuated, 2 * t + 2)
                if t == 0:
                    pe.wait_ge(wr_in, 64)
                if t >= 2:
                    pe.wait_ge(logits, t - 1)
                for k in range(KD):
                    ins = pe.matmul(m.ps[0:n, 6 + u, 0:NR], m.xT[:, k, cols(t)], wr[:, k, :],
                                    start=(k == 0), stop=(k == KD - 1))
                ins.then_inc(routed, 1)
            def count():
                pe.wait_ge(sel_ready, 1)
                s = sel[:, :, :].rearrange("p t e -> p (t e)")
                pe.matmul(m.ps[:, 0, 0:TILES * NE], before[:, :], s, start=True, stop=True)
                pe.matmul(m.ps[:, 1, 0:TILES * NE], m.ones[:, :], s, start=True, stop=True).then_inc(counted, 1)

            def turn_rows():
                pe.wait_ge(rows_in, 16)
                pe.transpose(m.ps[:, 2, 0:SLOTS], rows_t[:, :], m.ident[0:SLOTS, 0:SLOTS]).then_inc(rows_done, 1)
            project(0)
            for t in range(TILES):
                if t + 1 < TILES:
                    project(t + 1)
                route(t)
            count()
            turn_rows()

        @block.scalar
        def _(act):
            load_ln_exp(nc, act)
            step = Steps(act, act_step)
            for t in range(TILES):
                u, n = t % 2, rows(t)
                act.wait_ge(h_ready, 2 * t + 2)
                if t >= 2:
                    act.wait_ge(transposed, 2 * (t - 1))
                    act.wait_ge(hn_stored[u], 16 * (t // 2))
                step(act.activation(hs[0:n, u, :], m.Y[0:n, t, :], ACT.Square, accum_out=ss[0:n, u:u + 1]))
                step.wait()
                step(act.activation(ss[0:n, u:u + 1], ss[0:n, u:u + 1], ACT.Ln, scale=1.0 / D, bias=m.eps[0:n, :]))
                step.wait()
                step(act.activation(ss[0:n, u:u + 1], ss[0:n, u:u + 1], ACT.Exp, scale=-0.5))
                step.wait()
                act.activation(hs[0:n, u, :], m.Y[0:n, t, :], ACT.Copy, scale=ss[0:n, u:u + 1]).then_inc(hs_ready, 1)
            act.wait_ge(shifted, 1)
            act.activation(t4[:, :, :], t4[:, :, :], ACT.Exp).then_inc(exp_done, 1)
            act.wait_ge(v_diff, 1)
            act.activation(w2[:, :], w2[:, :], ACT.Exp).then_inc(exp2_done, 1)

        @block.vector
        def _(dve):
            step = Steps(dve, dve_step)

            def add_x(t):
                u, n = t % 2, rows(t)
                dve.wait_ge(x_in[u], (t // 2 + 1) * 16)
                for b in range(2):
                    dve.wait_ge(mixed, 2 * t + b + 1)
                    c = slice(b * 512, b * 512 + 512)
                    dve.tensor_tensor(m.Y[0:n, t, c], m.ps[0:n, 2 * u + b, :], xb[0:n, u, c], ALU.add).then_inc(h_ready, 1)

            dve.wait_ge(pool_step, POOL_ALL)
            add_x(0)
            for t in range(TILES):
                u, n = t % 2, rows(t)
                if t + 1 < TILES:
                    add_x(t + 1)
                for b in range(2):
                    dve.wait_ge(transposed, 2 * t + b + 1)
                    i = m.ps[:, 4 + b, :].rearrange("p (c n) -> p c n", c=4)[:, :, 0:n]
                    wn = m.n2w[:, 4 * b:4 * b + 4].unsqueeze(2).to_broadcast([128, 4, n])
                    dve.tensor_tensor(m.xT[:, 4 * b:4 * b + 4, cols(t)], i, wn, ALU.mult).then_inc(evacuated, 1)
                dve.wait_ge(routed, t + 1)
                if t == 0:
                    dve.wait_ge(wr_in, 64)
                dve.tensor_tensor(LG[0:n, t, :], m.ps[0:n, 6 + u, 0:NR], br[0:n, :], ALU.add).then_inc(logits, 1)
            dve.wait_ge(logits, TILES)
            wide = lambda x: x[:, :].unsqueeze(2).to_broadcast([128, TILES, EG])

            def do(ins):
                step(ins)
                step.wait()

            def first_max(oh, x, mx):
                do(dve.tensor_reduce(mx[:, :], x, AX.X, ALU.max))
                do(dve.tensor_tensor(oh[:, :, :], x, wide(mx), ALU.is_equal))
                do(dve.tensor_tensor(oh[:, :, :], oh[:, :, :], place[:, :, :], ALU.mult))
                do(dve.tensor_reduce(tm[:, :], oh[:, :, :], AX.X, ALU.max))
                do(dve.tensor_tensor(oh[:, :, :], place[:, :, :], wide(tm), ALU.is_equal))
            G = LG[:, :, 0:NG]
            first_max(ohg, G, gm)
            do(dve.tensor_tensor(t4[:, :, :], G, wide(gm), ALU.subtract))
            dve.sem_inc(shifted, 1)
            dve.wait_ge(exp_done, 1)
            do(dve.tensor_reduce(gz[:, :], t4[:, :, :], AX.X, ALU.add))
            do(dve.reciprocal(gz[:, :], gz[:, :]))
            E4 = LG[:, :, NG:NR].rearrange("p t (g e) -> p t g e", g=NG)
            do(dve.tensor_tensor(t16[:, :, :, :], E4, ohg[:, :, :].unsqueeze(3).to_broadcast([128, TILES, NG, EG]), ALU.mult))
            do(dve.tensor_reduce(es[:, :, :], t16[:, :, :, :].rearrange("p t g e -> p t e g"), AX.X, ALU.add))
            first_max(oh1, es[:, :, :], v1)
            do(dve.scalar_tensor_tensor(es[:, :, :], oh1[:, :, :], -BIG, es[:, :, :], ALU.mult, ALU.add))
            first_max(oh2, es[:, :, :], v2)
            do(dve.tensor_tensor(w2[:, :], v2[:, :], v1[:, :], ALU.subtract))
            dve.sem_inc(v_diff, 1)
            dve.wait_ge(exp2_done, 1)
            do(dve.tensor_scalar(w1[:, :], w2[:, :], 1.0, None, ALU.add))
            do(dve.reciprocal(w1[:, :], w1[:, :]))
            do(dve.tensor_tensor(m.w1[:, :], w1[:, :], gz[:, :], ALU.mult))
            do(dve.tensor_tensor(m.w2[:, :], w2[:, :], m.w1[:, :], ALU.mult))

            ohg4 = ohg[:, :, :].unsqueeze(3).to_broadcast([128, TILES, NG, EG])
            for s, oh in ((sel1, oh1), (sel2, oh2)):
                do(dve.tensor_tensor(s[:, :, :].rearrange("p t (g e) -> p t g e", g=NG), ohg4,
                                     oh[:, :, :].unsqueeze(2).to_broadcast([128, TILES, NG, EG]), ALU.mult))
            do(dve.tensor_tensor(sel[:, :, :], sel1[:, :, :], sel2[:, :, :], ALU.add))
            do(dve.tensor_tensor(sel[:, :, :], sel[:, :, :], valid[:, :].unsqueeze(2).to_broadcast([128, TILES, NE]), ALU.mult))
            dve.sem_inc(sel_ready, 1)
            dve.wait_ge(counted, 1)
            for t in range(TILES):
                do(dve.scalar_tensor_tensor(pre[:, t + 1, :], m.ps[:, 1, t * NE:t * NE + NE], 128.0, pre[:, t, :],
                                            ALU.mult, ALU.add))
            do(dve.tensor_scalar(cnti[:, :], pre[:, TILES, :], 127.0, None, ALU.add))
            do(dve.tensor_scalar(tli[:, :], cnti[:, :], 7, None, ALU.logical_shift_right))
            do(dve.tensor_copy(tl[:, :], tli[:, :]))
            do(dve.tensor_tensor_scan(cumf[:, :], one16[:, :], tl[:, :], 0.0, ALU.mult, ALU.add))
            do(dve.tensor_tensor(base[:, :], cumf[:, :], tl[:, :], ALU.subtract))
            do(dve.tensor_scalar(base[:, :], base[:, :], 128.0, None, ALU.mult))
            do(dve.tensor_tensor(pos[:, :, :], m.ps[:, 0, 0:TILES * NE].rearrange("p (t e) -> p t e", e=NE),
                                 pre[:, 0:TILES, :], ALU.add))
            do(dve.tensor_tensor(pos[:, :, :], pos[:, :, :], base[:, :].unsqueeze(1).to_broadcast([128, TILES, NE]), ALU.add))
            for n, (s, p) in enumerate(((sel1, m.pos1), (sel2, m.pos2))):
                do(dve.tensor_tensor(s[:, :, :], s[:, :, :], pos[:, :, :], ALU.mult))
                do(dve.tensor_reduce(posf[:, n, :], s[:, :, :], AX.X, ALU.add))
                do(dve.tensor_copy(p[:, :], posf[:, n, :]))
            dve.sem_inc(pos_ready, 1)
            do(dve.tensor_copy(m.cum[:, :], cumf[0:1, :]))
            do(dve.tensor_tensor(over[:, :, :], tilef[:, :].unsqueeze(2).to_broadcast([1, SLOTS, NE]),
                                 cumf[0:1, :].unsqueeze(1).to_broadcast([1, SLOTS, NE]), ALU.is_ge))
            do(dve.tensor_reduce(ef[:, :], over[:, :, :], AX.X, ALU.add))
            do(dve.tensor_scalar(ef[:, :], ef[:, :], float(NE - 1), None, ALU.min))
            do(dve.tensor_copy(m.tile_expert[:, :], ef[:, :]))
            do(dve.tensor_scalar(third[:, :], ef[:, :], 11.0, None, ALU.mult))
            do(dve.tensor_scalar(third[:, :], third[:, :], 5, None, ALU.logical_shift_right))
            do(dve.scalar_tensor_tensor(m.tile_ring[:, :], third[:, :], -3.0, ef[:, :], ALU.mult, ALU.add))
            dve.wait_ge(rows_done, 1)
            do(dve.tensor_copy(m.slot_tok[:, :], m.ps[:, 2, 0:SLOTS]))


def moe_phase(nc, a, out, m):
    FC = FF // 128
    EW = KD * 2 * FF
    with ExitStack() as ctx:
        sb, sem = scope(nc, ctx)
        ring = sb("e_ring", [128, RING * (EW + FC * D)])
        up_w = ring[:, 0:RING * EW].rearrange("p (r k f) -> p r k f", r=RING, k=KD)
        down_w = ring[:, RING * EW:].rearrange("p (r f n) -> p (r f) n", r=RING, f=FC)
        up_k = ring[:, 0:RING * EW].rearrange("p (r f) -> p r f", f=2 * FF)
        spare = m.xT[:, :, :].rearrange("p k t -> p (k t)")
        xg = spare[:, 0:2 * D].rearrange("p (u d) -> p u d", u=2)
        xgT = spare[:, 2 * D:4 * D].rearrange("p (u k n) -> p u k n", u=2, k=KD)
        oE = spare[:, 4 * D:6 * D].rearrange("p (u d) -> p u d", u=2)
        hid = sb("e_hid", [128, 2, FF])
        sg = sb("e_sg", [128, 2, FF])
        hT = sb("e_hT", [128, 2, FF])
        idx = sb("e_idx", [128, 2], I32)
        back = m.mixT[:, :, :].rearrange("p k t -> p (k t)")[:, 0:8 * D].rearrange("p (s j d) -> p s j d", s=4, j=TOP)
        w_in = [sem(f"e_w_in{r}") for r in range(RING)]
        w_ready, tile_done = sem("e_w_ready"), sem("e_tile_done")
        idx_ready, x_in, x_turned, xt_ready = sem("e_idx_ready"), [sem("e_x_in0"), sem("e_x_in1")], sem("e_x_turned"), sem("e_xt_ready")
        up_done, silu_done, hid_ready, h_turned, ht_ready = (sem(f"e_{n}") for n in (
            "up_done", "silu_done", "hid_ready", "h_turned", "ht_ready"))
        down_done, o_left, o_right = sem("e_down_done"), sem("e_o_left"), sem("e_o_right")
        o_stored = [sem("e_o_stored0"), sem("e_o_stored1")]
        back_in = [sem(f"e_back_in{s}") for s in range(4)]
        act_gate, pool_gate = sem("e_act_gate"), sem("e_pool_gate")
        added1, added, y_stored = sem("e_added1"), sem("e_added"), sem("e_y_stored")
        block = ctx.enter_context(nc.Block())
        wg_d = a.w_gate[0, :, :, :].rearrange("e (k p) f -> e p k f", p=128)
        wu_d = a.w_up[0, :, :, :].rearrange("e (k p) f -> e p k f", p=128)
        wd_d = a.w_down[0, :, :, :].rearrange("e (k p) n -> e p k n", p=128)
        orow = m.expert_rows.rearrange("(i p) d -> i p d", p=128)

        @block.sync
        def _(sp):
            def load(e, r):
                sp.dma_start(up_w[:, r, :, 0:FF], wg_d[e, :, :, :]).then_inc(w_in[r], 16)
                sp.dma_start(up_w[:, r, :, FF:2 * FF], wu_d[e, :, :, :]).then_inc(w_in[r], 16)
                sp.dma_start(down_w[:, FC * r:FC * r + FC, :], wd_d[e, :, :, :]).then_inc(w_in[r], 16)

            def landed(r, turn):
                sp.wait_ge(w_in[r], turn * 48 + 48)
                sp.sem_inc(w_ready, 1)

            def replace(e, r, turn):
                tiles = sp.value_load(m.cum[0:1, bass.ds(e - RING, 1)], min_val=0, max_val=SLOTS)
                sp.wait_ge(tile_done, tiles + 1)
                load(e, r)
                landed((r - 1) % RING, turn if r else turn - 1)
            for r in range(RING):
                load(r, r)
            landed(0, 0)
            landed(1, 0)
            with sp.Fori(1, NE // RING) as j:
                for r in range(RING):
                    replace(j * RING + r, r, j)
            replace(NE - 1, 0, NE // RING)
            landed(0, NE // RING)

        @block.gpsimd
        def _(pool):
            def gather(i, u, turn):
                if turn is not None:
                    pool.wait_ge(x_in[u], turn * 16)
                    pool.wait_ge(x_turned, i - 1)
                pool.tensor_copy(idx[:, u:u + 1], m.slot_tok[:, bass.ds(i, 1)]).then_inc(idx_ready, 1)
                pool.wait_ge(idx_ready, i + 1)
                pool.sem_inc(pool_gate, 1)
                pool.indirect_dma_start(xg[:, u, :], None, m.hn_rows,
                                        bass.IndirectOffsetOnAxis(ap=idx[:, u:u + 1], axis=0)).then_inc(x_in[u], 16)
            gather(0, 0, None)
            gather(1, 1, None)
            with pool.Fori(1, SLOTS // 2) as j:
                for u in range(2):
                    gather(j * 2 + u, u, j)
            for u in range(2):
                pool.wait_ge(o_stored[u], SLOTS // 2 * 16)
            for t in range(TILES):
                n, s = rows(t), t % 4
                if t >= 4:
                    pool.wait_ge(added, t - 3)
                for j, p in enumerate((m.pos1, m.pos2)):
                    pool.indirect_dma_start(back[0:n, s, j, :], None, m.expert_rows,
                                            bass.IndirectOffsetOnAxis(ap=p[0:n, t:t + 1], axis=0)).then_inc(back_in[s], 16)

        @block.tensor
        def _(pe):
            def turn_x(i, u, turn):
                pe.wait_ge(x_in[u], turn * 16 + 16)
                if not (isinstance(i, int) and i == 0):
                    pe.wait_ge(xt_ready, i)
                for k in range(KD):
                    ins = pe.transpose(m.ps[:, k // 4, k % 4 * 128:k % 4 * 128 + 128],
                                       xg[:, u, k * 128:k * 128 + 128], m.ident[:, :])
                ins.then_inc(x_turned, 1)

            def expert_of(i):
                e = pe.value_load(m.tile_expert[0:1, bass.ds(i, 1)], min_val=0, max_val=NE - 1)
                r = pe.value_load(m.tile_ring[0:1, bass.ds(i, 1)], min_val=0, max_val=RING - 1)
                return e, r

            def up(i, u):
                e, r = expert_of(i)
                pe.wait_ge(xt_ready, i + 1)
                pe.wait_ge(w_ready, e + 1)
                for k in range(KD):
                    ins = pe.matmul(m.ps[:, 2 + u, :], xgT[:, u, k, :], up_k[:, bass.ds(r * KD + k, 1), :].squeeze(1),
                                    start=(k == 0), stop=(k == KD - 1))
                ins.then_inc(up_done, 1)

            def down(i, u):
                r = pe.value_load(m.tile_ring[0:1, bass.ds(i, 1)], min_val=0, max_val=RING - 1)
                pe.wait_ge(hid_ready, i + 1)
                for f in range(FC):
                    ins = pe.transpose(m.ps[:, 4 + u, f * 128:f * 128 + 128], hid[:, u, f * 128:f * 128 + 128], m.ident[:, :])
                ins.then_inc(h_turned, 1)
                pe.wait_ge(ht_ready, i + 1)
                if not (isinstance(i, int) and i == 0):
                    pe.wait_ge(o_left, i)
                    pe.wait_ge(o_right, i)
                for b in range(2):
                    for f in range(FC):
                        ins = pe.matmul(m.ps[:, 6 + b, :], hT[:, u, f * 128:f * 128 + 128],
                                        down_w[:, bass.ds(r * FC + f, 1), b * 512:b * 512 + 512].squeeze(1),
                                        start=(f == 0), stop=(f == FC - 1))
                    ins.then_inc(tile_done if b else down_done, 1)

            pe.sem_inc(tile_done, 1)
            turn_x(0, 0, 0)
            turn_x(1, 1, 0)
            up(0, 0)
            up(1, 1)
            turn_x(2, 0, 1)
            down(0, 0)
            with pe.Fori(1, SLOTS // 2 - 1) as j:
                turn_x(j * 2 + 1, 1, j)
                up(j * 2, 0)
                down(j * 2 - 1, 1)
                turn_x(j * 2 + 2, 0, j + 1)
                up(j * 2 + 1, 1)
                down(j * 2, 0)
            turn_x(SLOTS - 1, 1, SLOTS // 2 - 1)
            up(SLOTS - 2, 0)
            down(SLOTS - 3, 1)
            up(SLOTS - 1, 1)
            down(SLOTS - 2, 0)
            down(SLOTS - 1, 1)

        @block.scalar
        def _(act):
            def silu(i, u):
                act.wait_ge(up_done, i + 1)
                act.activation(sg[:, u, :], m.ps[:, 2 + u, 0:FF], ACT.Silu).then_inc(silu_done, 1)

            def rest(i, u, turn):
                act.wait_ge(h_turned, i + 1)
                act.activation(hT[:, u, :], m.ps[:, 4 + u, 0:FF], ACT.Copy).then_inc(ht_ready, 1)
                act.wait_ge(down_done, i + 1)
                if not (isinstance(turn, int) and turn == 0):
                    act.wait_ge(o_stored[u], turn * 16)
                act.activation(oE[:, u, 0:512], m.ps[:, 6, :], ACT.Copy).then_inc(o_left, 1)
                act.wait_ge(o_left, i + 1)
                act.wait_ge(o_right, i + 1)
                act.sem_inc(act_gate, 1)
                act.dma_start(orow[i, :, :], oE[:, u, :]).then_inc(o_stored[u], 16)
            silu(0, 0)
            silu(1, 1)
            rest(0, 0, 0)
            silu(2, 0)
            rest(1, 1, 0)
            silu(3, 1)
            rest(2, 0, 1)
            with act.Fori(2, SLOTS // 2) as j:
                silu(j * 2, 0)
                rest(j * 2 - 1, 1, j - 1)
                silu(j * 2 + 1, 1)
                rest(j * 2, 0, j)
            rest(SLOTS - 1, 1, SLOTS // 2 - 1)

            for t in range(TILES):
                act.wait_ge(added, t + 1)
                dst = out.y_prompt[0, t * 128:t * 128 + 128, :] if t < NT else out.y_sample.rearrange("b t d -> (b t) d")
                act.dma_start(dst, m.Y[0:rows(t), t, :]).then_inc(y_stored, 16)
            act.wait_ge(y_stored, 16 * TILES)

        @block.vector
        def _(dve):
            def turn(i, u):
                for b in range(2):
                    if b == 0:
                        dve.wait_ge(x_turned, i + 1)
                    p = m.ps[:, b, :].rearrange("p (c n) -> p c n", c=4)
                    wn = m.n2w[:, 4 * b:4 * b + 4].unsqueeze(2).to_broadcast([128, 4, 128])
                    ins = dve.tensor_tensor(xgT[:, u, 4 * b:4 * b + 4, :], p, wn, ALU.mult)
                ins.then_inc(xt_ready, 1)

            def hidden(i, u):
                dve.wait_ge(silu_done, i + 1)
                dve.tensor_tensor(hid[:, u, :], sg[:, u, :], m.ps[:, 2 + u, FF:2 * FF], ALU.mult).then_inc(hid_ready, 1)

            def right(i, u, turn_):
                dve.wait_ge(tile_done, i + 2)
                if not (isinstance(turn_, int) and turn_ == 0):
                    dve.wait_ge(o_stored[u], turn_ * 16)
                dve.tensor_copy(oE[:, u, 512:1024], m.ps[:, 7, :]).then_inc(o_right, 1)
            turn(0, 0)
            turn(1, 1)
            hidden(0, 0)
            hidden(1, 1)
            turn(2, 0)
            right(0, 0, 0)
            turn(3, 1)
            hidden(2, 0)
            right(1, 1, 0)
            turn(4, 0)
            hidden(3, 1)
            right(2, 0, 1)
            with dve.Fori(2, SLOTS // 2 - 1) as j:
                turn(j * 2 + 1, 1)
                hidden(j * 2, 0)
                right(j * 2 - 1, 1, j - 1)
                turn(j * 2 + 2, 0)
                hidden(j * 2 + 1, 1)
                right(j * 2, 0, j)
            turn(SLOTS - 1, 1)
            hidden(SLOTS - 2, 0)
            right(SLOTS - 3, 1, SLOTS // 2 - 2)
            hidden(SLOTS - 1, 1)
            right(SLOTS - 2, 0, SLOTS // 2 - 1)
            right(SLOTS - 1, 1, SLOTS // 2 - 1)
            for t in range(TILES):
                n, s = rows(t), t % 4
                dve.wait_ge(back_in[s], (t // 4 + 1) * 32)
                y = m.Y[0:n, t, :]
                dve.scalar_tensor_tensor(y, back[0:n, s, 0, :], m.w1[0:n, t:t + 1], y, ALU.mult, ALU.add).then_inc(added1, 1)
                dve.wait_ge(added1, t + 1)
                dve.scalar_tensor_tensor(y, back[0:n, s, 1, :], m.w2[0:n, t:t + 1], y, ALU.mult, ALU.add).then_inc(added, 1)


_INS = ["x_prompt", "x_sample", "cache_k", "cache_v", "state_hgrn", "page_table", "norm1_w", "w_in", "q_norm_w",
        "k_norm_w", "lambda_q1", "lambda_k1", "lambda_q2", "lambda_k2", "subln_w", "hg_lb", "hg_norm_w", "w_out",
        "norm2_w", "w_router_grp", "b_router_grp", "w_router_exp", "b_router_exp", "w_gate", "w_up", "w_down"]
_OUTS = [("y_prompt", (1, SEQ, D)), ("y_sample", (DB, DS, D)), ("k_prompt", (1, 1, SEQ, HEADS, 128)),
         ("v_prompt", (1, 1, SEQ, HEADS, 128)), ("hgrn_prompt", (1, 1, HEADS, 128, 128)),
         ("k_sample", (1, DB, DS, HEADS, 128)), ("v_sample", (1, DB, DS, HEADS, 128)),
         ("hgrn_sample", (1, DB, HEADS, 128, 128))]


def kernel(**inputs):
    import numpy as _np
    import concourse.bacc as _bacc
    from concourse.bass_utils import run_bass_kernel_spmd as _run

    nc = _bacc.Bacc("TRN2", target_bir_lowering=False, num_devices=1)
    arrays, a, out = {}, Named(), Named()
    for name in _INS:
        x = _np.ascontiguousarray(inputs[name])
        arrays[f"in_{name}"] = x
        a.__dict__[name] = nc.dram_tensor(f"in_{name}", x.shape, mybir.dt.from_np(x.dtype), kind="ExternalInput").ap()
    for name, shape in _OUTS:
        out.__dict__[name] = nc.dram_tensor(f"out_{name}", shape, F32, kind="ExternalOutput").ap()
    build(nc, a, out)
    r = _run(nc, [arrays], core_ids=[0])
    return tuple(r.results[0][f"out_{name}"] for name, _ in _OUTS)
```

```python
from contextlib import ExitStack


import concourse.bass as bass
from concourse import mybir

F32 = mybir.dt.float32
F32R = mybir.dt.float32r
I32 = mybir.dt.int32
U8 = mybir.dt.uint8
ALU = mybir.AluOpType
ACT = mybir.ActivationFunctionType
AX = mybir.AxisListType

D = 1024
KD = D // 128
SEQ = 1024
NT = SEQ // 128
DB, DS = 8, 8
NS = DB * DS
TOK = SEQ + NS
TILES = NT + 1
GROUPS = [(0, 384), (384, 384), (768, 320)]
HEADS = 4
PAGE = 128
PAGES = 16
PG = 4
NPG = PAGES // PG
NE, NG, EG = 16, 4, 4
FF = 256
TOP = 2
SLOTS = (TOP * 1088 - NE) // 128 + NE
RING = 3
LEVELS = 7
SAMPLE_LEVELS = 3
EPS = 1e-6
NEG = -1e30
LAM_INIT = 0.2
BIG = 3e38
LN_EXP_SET = 6


class Named:
    pass


class Steps:

    def __init__(self, eng, sem):
        self.eng, self.sem, self.n, self.turn, self.per = eng, sem, 0, 0, 0

    def __call__(self, ins):
        ins.then_inc(self.sem, 1)
        self.n += 1

    def wait(self):
        self.eng.wait_ge(self.sem, self.turn * self.per + self.n)

    def begin(self, turn, per):
        self.turn, self.per, self.start = turn, per, self.n

    def end(self, turns):
        assert self.n - self.start == self.per, (self.n - self.start, self.per)
        self.n = self.start + turns * self.per
        self.turn, self.per = 0, 0


def rows(t):
    return 128 if t < NT else NS


def cols(t):
    return slice(t * 128, t * 128 + rows(t))


def build(nc, a, out):
    with ExitStack() as ctx:
        m = Named()
        sb = lambda n, s, dt=F32: ctx.enter_context(nc.sbuf_tensor(n, s, dt))
        m.ident = sb("ident", [128, 128])
        m.ones = sb("ones", [128, 128])
        m.halves = sb("halves", [128, 128])
        m.causal = sb("causal", [128, 128])
        m.eps = sb("eps", [128, 1])
        m.n1w = sb("n1w", [128, KD])
        m.n2w = sb("n2w", [128, KD])
        m.qw = sb("qw", [128, 1])
        m.kw = sb("kw", [128, 1])
        m.subw = sb("subw", [128, 1])
        m.hgw = sb("hgw", [128, 1])
        m.coef = sb("coef", [128, 2])
        m.lb = sb("lb", [128, HEADS])
        m.lb1 = sb("lb1", [128, HEADS])
        m.mixT = sb("mixT", [128, KD, TOK])
        m.qbd = sb("qbd", [128, HEADS, DB, 32])
        m.kS = sb("kS", [128, HEADS, NS])
        m.hn_rows = nc.dram_tensor("hn_rows", (TOK, D), F32, kind="Internal").ap()
        m.slot_rows = nc.dram_tensor("slot_rows", (SLOTS * 128, 1), F32, kind="Internal").ap()
        m.expert_rows = nc.dram_tensor("expert_rows", (SLOTS * 128, D), F32, kind="Internal").ap()
        m.zT = nc.dram_tensor("zT", (3, HEADS, 128, TOK), F32, kind="Internal").ap()
        m.zi = nc.dram_tensor("zi", (HEADS, TOK, 128), F32, kind="Internal").ap()
        m.ps = ctx.enter_context(nc.psum_tensor("ps", [128, 8, 512], F32))
        m.z_stored, m.v_stored = (ctx.enter_context(nc.semaphore(n)) for n in ("z_stored", "v_stored"))
        with ExitStack() as early:
            m.xh = early.enter_context(nc.sbuf_tensor("xh", [128, KD, TOK], F32R))
            m.xl = early.enter_context(nc.sbuf_tensor("xl", [128, KD, TOK], F32R))
            norm_phase(nc, a, m)
            proj_phase(nc, a, out, m)
            attention_phase(nc, a, out, m)
        hgrn_phase(nc, a, out, m)
        decode_phase(nc, a, out, m)
        with ExitStack() as late:
            m.Y = late.enter_context(nc.sbuf_tensor("Y", [128, TILES, D], F32))
            sb = lambda n, s, dt=F32: late.enter_context(nc.sbuf_tensor(n, s, dt))
            m.w1 = sb("w1", [128, TILES])
            m.w2 = sb("w2", [128, TILES])
            m.pos1 = sb("pos1", [128, TILES], I32)
            m.pos2 = sb("pos2", [128, TILES], I32)
            m.slot_tok = sb("slot_tok", [128, SLOTS], I32)
            m.tile_expert = sb("tile_expert", [1, SLOTS], I32)
            m.tile_ring = sb("tile_ring", [1, SLOTS], I32)
            m.cum = sb("cum", [1, NE], I32)
            mix_phase(nc, a, m)
            moe_phase(nc, a, out, m)


def scope(nc, ctx):
    sb = lambda n, s, dt=F32: ctx.enter_context(nc.sbuf_tensor(n, s, dt))
    made = []

    def sem(n):
        made.append(ctx.enter_context(nc.semaphore(n)))
        return made[-1]
    sem.made = made
    return sb, sem


def load_ln_exp(nc, act):
    act.add_instruction(mybir.InstLoadActFuncSet(name=nc.get_next_instruction_name(), engine=mybir.EngineType.Activation,
                                                 act_func_set_id=LN_EXP_SET, ins=[], outs=[]))


def column(v, n):
    return v.rearrange("(p o) -> p o", o=1)


def norm_phase(nc, a, m):
    with ExitStack() as ctx:
        sb, sem = scope(nc, ctx)
        xb = sb("n_xb", [128, 2, D])
        junk = sb("n_junk", [128, D])
        xs = sb("n_xs", [128, 2, D])
        xt = sb("n_xt", [128, 2, KD, 128])
        ss = sb("n_ss", [128, 2])
        rs = sb("n_rs", [128, 2])
        lam = sb("n_lam", [128, 4, 64])
        prod = sb("n_prod", [128, 2, 64])
        dots = sb("n_dots", [128, 2])
        hb = sb("n_hb", [128, 2, HEADS])
        hm = sb("n_hm", [128, HEADS])
        hs = sb("n_hs", [128, HEADS])
        x_in = [sem("n_x_in0"), sem("n_x_in1")]
        w_in = sem("n_w_in")
        xs_ready = sem("n_xs_ready")
        act_step = sem("n_act_step")
        dve_step = sem("n_dve_step")
        pool_step = sem("n_pool_step")
        transposed = sem("n_transposed")
        evacuated = sem("n_evacuated")
        rounded, split = sem("n_rounded"), sem("n_split")
        small = sem("n_small")
        small_exp = sem("n_small_exp")
        m.old_sems = sem.made
        block = ctx.enter_context(nc.Block())
        xp = a.x_prompt[0, :, :].rearrange("(t p) d -> t p d", p=128)
        SMALL = [(m.n1w[:, :], a.norm1_w[0, :].rearrange("(c p) -> p c", p=128)),
                 (m.n2w[:, :], a.norm2_w[0, :].rearrange("(c p) -> p c", p=128)),
                 (m.qw[0:64, :], column(a.q_norm_w[0, :], 64)),
                 (m.qw[64:128, :], column(a.q_norm_w[0, :], 64)),
                 (m.kw[0:64, :], column(a.k_norm_w[0, :], 64)),
                 (m.kw[64:128, :], column(a.k_norm_w[0, :], 64)),
                 (m.subw[:, :], column(a.subln_w[0, :], 128)),
                 (m.hgw[:, :], column(a.hg_norm_w[0, :], 128)),
                 (hb[:, :, :], a.hg_lb.rearrange("l (h p) -> p l h", p=128))]
        SMALL += [(lam[:, n, :], v[0, :].partition_broadcast(128)) for n, v in
                  enumerate((a.lambda_q1, a.lambda_k1, a.lambda_q2, a.lambda_k2))]

        @block.gpsimd
        def _(pool):
            step = Steps(pool, pool_step)
            for t, v in ((m.ident, 0.0), (m.ones, 1.0 / 128), (m.halves, 0.0), (m.causal, 0.0), (m.eps, EPS)):
                step(pool.memset(t[:, :], v))
            step(pool.memset(m.coef[:, 0:1], 1.0))
            step(pool.memset(m.qbd[:, :, :, :], 0.0))
            step.wait()
            step(pool.affine_select(out=m.ident[:, :], in_=m.ident[:, :], compare_op=ALU.not_equal, fill=1.0,
                                    base=0, pattern=[[-1, 128]], channel_multiplier=1))
            step(pool.affine_select(out=m.causal[:, :], in_=m.causal[:, :], compare_op=ALU.is_ge, fill=NEG,
                                    base=0, pattern=[[-1, 128]], channel_multiplier=1))
            step.wait()
            step(pool.memset(m.halves[0:64, 0:64], 1.0 / 64))
            step.wait()
            step(pool.memset(m.halves[64:128, 64:128], 1.0 / 64))
            step.wait()
            pool.sem_inc(split, 2)

            def rest(t, u, n):
                pool.wait_ge(rounded, t + 1)
                tok = bass.ds(t * 128, n)
                pool.tensor_tensor(m.xl[:, :, tok], xt[:, u, :, 0:n], m.xh[:, :, tok], ALU.subtract).then_inc(split, 1)
            with pool.Fori(0, NT // 2) as j:
                for u in range(2):
                    rest(j * 2 + u, u, 128)
            rest(NT, 0, NS)
            pool.wait_ge(split, TILES + 2)
        POOL_ALL = 11

        @block.sync
        def _(sp):
            def load(t, u, free):
                if free is not None:
                    sp.wait_ge(xs_ready, free)
                n = 128 if not isinstance(t, int) or t < NT else NS
                src = xp[t, :, :] if n == 128 else a.x_sample.rearrange("b t d -> (b t) d")
                sp.dma_start(xb[0:n, u, :], src).then_inc(x_in[u], 16)
            load(0, 0, None)
            load(1, 1, None)
            with nc.allow_non_contiguous_dma("small weight vectors"):
                for dst, src in SMALL:
                    sp.dma_start(dst, src).then_inc(w_in, 16)
            with sp.Fori(1, NT // 2) as j:
                for u in range(2):
                    load(j * 2 + u, u, j * 2 + u - 1)
            load(NT, 0, NT - 1)

        @block.scalar
        def _(act):
            step = Steps(act, act_step)

            def scale_tile(t, u, n, turn):
                act.wait_ge(x_in[u], turn * 16 + 16)
                step(act.activation(junk[0:n, :], xb[0:n, u, :], ACT.Square, accum_out=ss[0:n, u:u + 1]))
                step.wait()
                step(act.activation(rs[0:n, u:u + 1], ss[0:n, u:u + 1], ACT.Ln, scale=1.0 / D, bias=m.eps[0:n, :]))
                step.wait()
                step(act.activation(rs[0:n, u:u + 1], rs[0:n, u:u + 1], ACT.Exp, scale=-0.5))
                step.wait()
                if not isinstance(t, int) or t >= 2:
                    act.wait_ge(transposed, (t - 1) * 2)
                act.activation(xs[0:n, u, :], xb[0:n, u, :], ACT.Copy, scale=rs[0:n, u:u + 1]).then_inc(xs_ready, 1)
            load_ln_exp(nc, act)
            act.wait_ge(pool_step, POOL_ALL)
            for u in range(2):
                scale_tile(u, u, 128, 0)
            with act.Fori(1, NT // 2) as j:
                step.begin(j - 1, 6)
                for u in range(2):
                    scale_tile(j * 2 + u, u, 128, j)
                step.end(NT // 2 - 1)
            scale_tile(NT, 0, NS, NT // 2)
            act.wait_ge(small, 1)
            act.activation(dots[:, :], dots[:, :], ACT.Exp).then_inc(small_exp, 1)
            act.activation(hb[:, :, :], hb[:, :, :], ACT.Exp).then_inc(small_exp, 1)

        @block.tensor
        def _(pe):
            pe.wait_ge(pool_step, POOL_ALL)

            def transpose_tile(t, u, n):
                pe.wait_ge(xs_ready, t + 1)
                for b in range(2):
                    if not isinstance(t, int) or t >= 2:
                        pe.wait_ge(evacuated, (t - 2) * 2 + b + 1)
                    for c in range(4):
                        k = b * 4 + c
                        last = pe.transpose(m.ps[:, 2 * u + b, c * 128:c * 128 + n],
                                            xs[0:n, u, k * 128:(k + 1) * 128], m.ident[0:n, 0:n])
                    last.then_inc(transposed, 1)
            for u in range(2):
                transpose_tile(u, u, 128)
            with pe.Fori(1, NT // 2) as j:
                for u in range(2):
                    transpose_tile(j * 2 + u, u, 128)
            transpose_tile(NT, 0, NS)

        @block.vector
        def _(dve):
            step = Steps(dve, dve_step)
            dve.wait_ge(w_in, 16 * len(SMALL))
            dve.wait_ge(pool_step, POOL_ALL)
            for n in range(2):
                step(dve.tensor_tensor(prod[:, n, :], lam[:, 2 * n, :], lam[:, 2 * n + 1, :], ALU.mult))
            step(dve.tensor_scalar(m.qw[:, :], m.qw[:, :], 0.125, None, ALU.mult))
            step(dve.tensor_scalar(m.subw[:, :], m.subw[:, :], 1.0 - LAM_INIT, None, ALU.mult))
            step(dve.tensor_tensor(hm[:, :], hb[:, 0, :], hb[:, 1, :], ALU.max))
            step.wait()
            step(dve.tensor_reduce(dots[:, :], prod[:, :, :], AX.X, ALU.add))
            for n in range(2):
                step(dve.tensor_tensor(hb[:, n, :], hb[:, n, :], hm[:, :], ALU.subtract))
            step.wait()
            dve.sem_inc(small, 1)

            def evacuate(t, u, n):
                dve.wait_ge(split, t + 1)
                for b in range(2):
                    dve.wait_ge(transposed, t * 2 + b + 1)
                    i = m.ps[:, 2 * u + b, :].rearrange("p (c n) -> p c n", c=4)[:, :, 0:n]
                    w = m.n1w[:, 4 * b:4 * b + 4].unsqueeze(2).to_broadcast([128, 4, n])
                    dve.tensor_tensor(xt[:, u, 4 * b:4 * b + 4, 0:n], i, w, ALU.mult).then_inc(evacuated, 1)
                dve.wait_ge(evacuated, t * 2 + 2)
                dve.tensor_copy(m.xh[:, :, bass.ds(t * 128, n)], xt[:, u, :, 0:n]).then_inc(rounded, 1)
            with dve.Fori(0, NT // 2) as j:
                for u in range(2):
                    evacuate(j * 2 + u, u, 128)
            evacuate(NT, 0, NS)
            dve.wait_ge(small_exp, 2)
            step(dve.tensor_tensor(prod[:, 0, 0:1], dots[:, 1:2], dots[:, 0:1], ALU.subtract))
            step(dve.tensor_tensor(hs[:, :], hb[:, 0, :], hb[:, 1, :], ALU.add))
            step.wait()
            step(dve.tensor_scalar(m.coef[:, 1:2], prod[:, 0, 0:1], LAM_INIT, None, ALU.subtract))
            step(dve.reciprocal(hm[:, :], hs[:, :]))
            step.wait()
            step(dve.tensor_tensor(m.lb[:, :], hb[:, 0, :], hm[:, :], ALU.mult))
            step.wait()
            step(dve.tensor_scalar(m.lb1[:, :], m.lb[:, :], -1.0, 1.0, ALU.mult, ALU.add))
            step.wait()


def proj_phase(nc, a, out, m):
    w_in_d = a.w_in[0, :, :].rearrange("(k p) c -> p k c", p=128)
    FIRST = (0, 512)
    FIRST_V = (1024, 2560)
    NC = len(FIRST)
    with ExitStack() as ctx:
        sb, sem = scope(nc, ctx)
        w = sb("p_w", [128, 2, KD, 128])
        wh, wl = sb("p_wh", [128, 2, KD, 128], F32R), sb("p_wl", [128, 2, KD, 128], F32R)
        wv = sb("p_wv", [128, KD, 256])
        wvh, wvl = sb("p_wvh", [128, KD, 256], F32R), sb("p_wvl", [128, KD, 256], F32R)
        vs = sb("p_vs", [128, TILES, 256])
        w_in = [sem("p_w_in0"), sem("p_w_in1")]
        wv_in = sem("p_wv_in")
        w_ready, z_done, z_read = sem("p_w_ready"), sem("p_z_done"), sem("p_z_read")
        w_rounded = sem("p_w_rounded")
        wv_rounded, wv_ready = sem("p_wv_rounded"), sem("p_wv_ready")
        v_done, v_read = sem("p_v_done"), sem("p_v_read")
        v_stored = m.v_stored
        v_left = sem("p_v_left")
        gate, sp_gate = sem("p_gate"), sem("p_sp_gate")
        old_sems, m.old_sems = m.old_sems, sem.made
        block = ctx.enter_context(nc.Block())

        @block.sync
        def _(sp):
            with sp.Fori(0, HEADS) as t:
                for n in range(NC):
                    sp.wait_ge(w_ready, t * NC + n + 1)
                    sp.sem_inc(sp_gate, 1)
                    sp.dma_start(w[:, n, :, :], w_in_d[:, :, bass.ds(t * 128 + FIRST[n], 128)]).then_inc(w_in[n], 16)
                    if n == 1:
                        sp.wait_ge(wv_ready, t + 1)
                        sp.sem_inc(sp_gate, 1)
                        for j, c in enumerate(FIRST_V):
                            sp.dma_start(wv[:, :, j * 128:j * 128 + 128], w_in_d[:, :, bass.ds(t * 128 + c, 128)]).then_inc(wv_in, 16)

        @block.gpsimd
        def _(pool):
            for s in old_sems:
                pool.sem_clear(s)
            vp = out.v_prompt[0, 0, :, :, :].rearrange("(t p) h e -> h p t e", p=128)
            vsm = out.v_sample[0, :, :, :, :].rearrange("b t h e -> h (b t) e")
            zi = m.zi[:, 0:SEQ, :].rearrange("h (t p) e -> h p t e", p=128)
            pool.sem_inc(v_left, 1)
            with pool.Fori(0, HEADS) as t:
                pool.wait_ge(v_read, t * TILES + TILES + 2)
                pool.sem_inc(gate, 1)
                pool.dma_start(vp[t, :, :, :], vs[:, 0:NT, 0:128]).then_inc(v_stored, 16)
                pool.dma_start(vsm[t, :, :], vs[0:NS, NT, 0:128]).then_inc(v_stored, 16)
                pool.dma_start(zi[t, :, :, :], vs[:, 0:NT, 128:256]).then_inc(v_stored, 16)
                pool.dma_start(m.zi[t, SEQ:TOK, :], vs[0:NS, NT, 128:256]).then_inc(v_stored, 16)
                pool.wait_ge(v_stored, t * 64 + 64)
                pool.sem_inc(v_left, 1)

        @block.tensor
        def _(pe):
            def project(t, n):
                u = n
                pe.wait_ge(w_ready, t * NC + n + 3)
                pe.wait_ge(z_read, t * NC + n + 1)
                for k in range(KD):
                    for i, (left, right) in enumerate(((wh, m.xh), (wh, m.xl), (wl, m.xh))):
                        for g, (c0, w0) in enumerate(GROUPS):
                            ins = pe.matmul(m.ps[:, 3 * u + g, 0:w0], left[:, u, k, :], right[:, k, c0:c0 + w0],
                                            start=(k == 0 and i == 0), stop=(k == KD - 1 and i == 2))
                ins.then_inc(z_done, 1)

            def project_v(t, j):
                pe.wait_ge(v_read, t * TILES + j + (2 if j == 0 else 1))
                for k in range(KD):
                    for i, (left, right) in enumerate(((m.xh, wvh), (m.xh, wvl), (m.xl, wvh))):
                        ins = pe.matmul(m.ps[0:rows(j), 6 + j % 2, 0:256], left[:, k, cols(j)], right[:, k, :],
                                        start=(k == 0 and i == 0), stop=(k == KD - 1 and i == 2))
                ins.then_inc(v_done, 1)
            pe.sem_inc(z_done, 2)
            pe.sem_inc(v_done, 1)
            with pe.Fori(0, HEADS) as t:
                for n in range(NC):
                    project(t, n)
                pe.wait_ge(wv_ready, t + 1 + 1)
                for j in range(TILES):
                    project_v(t, j)

        @block.scalar
        def _(act):
            def round_w(t, n):
                act.wait_ge(w_in[n], t * 16 + 16)
                act.wait_ge(z_done, t * NC + n + 1)
                act.activation(wh[:, n, :, :], w[:, n, :, :], ACT.Copy).then_inc(w_rounded, 1)

            def read(t, n):
                act.wait_ge(z_done, t * NC + n + 3)
                for g, (c0, w0) in enumerate(GROUPS):
                    dst = m.mixT[:, bass.ds(t + HEADS * n, 1), c0:c0 + w0].squeeze(1)
                    ins = act.activation(dst, m.ps[:, 3 * n + g, 0:w0], ACT.Copy)
                ins.then_inc(z_read, 1)
            act.sem_inc(z_read, 2)
            with act.Fori(0, HEADS) as t:
                round_w(t, 0)
                round_w(t, 1)
                act.wait_ge(wv_in, t * 32 + 32)
                act.wait_ge(v_done, t * TILES + 1)
                act.activation(wvh[:, :, :], wv[:, :, :], ACT.Copy).then_inc(wv_rounded, 1)
                for n in range(NC):
                    read(t, n)

        @block.vector
        def _(dve):
            def rest_of_w(t, n):
                dve.wait_ge(w_rounded, t * NC + n + 1)
                dve.tensor_tensor(wl[:, n, :, :], w[:, n, :, :], wh[:, n, :, :], ALU.subtract).then_inc(w_ready, 1)
            dve.sem_inc(w_ready, 2)
            dve.sem_inc(wv_ready, 1)
            dve.sem_inc(v_read, 2)
            with dve.Fori(0, HEADS) as t:
                rest_of_w(t, 0)
                rest_of_w(t, 1)
                dve.wait_ge(wv_rounded, t + 1)
                dve.tensor_tensor(wvl[:, :, :], wv[:, :, :], wvh[:, :, :], ALU.subtract).then_inc(wv_ready, 1)
                dve.wait_ge(v_left, t + 1)
                for j in range(TILES):
                    dve.wait_ge(v_done, t * TILES + j + 2)
                    dve.tensor_copy(vs[0:rows(j), j, :], m.ps[0:rows(j), 6 + j % 2, 0:256]).then_inc(v_read, 1)


def attention_phase(nc, a, out, m):
    w_in_d = a.w_in[0, :, :].rearrange("(k p) c -> p k c", p=128)
    FIRST = (1536, 2048, 3072)
    NZ, UNITS = len(FIRST), len(FIRST) * len(GROUPS)
    with ExitStack() as ctx:
        sb, sem = scope(nc, ctx)
        sq, sk, rq, rk, qT, kT = (sb(f"a_{n}", [128, TOK]) for n in ("sq", "sk", "rq", "rk", "qT", "kT"))
        v = sb("a_v", [128, NT, 128])
        kt = sb("a_kt", [128, TILES, 128])
        P = sb("a_P", [128, 2, SEQ])
        A = sb("a_A", [128, SEQ])
        AT = sb("a_AT", [128, SEQ])
        oT = sb("a_oT", [128, SEQ])
        so = sb("a_so", [128, SEQ])
        ro = sb("a_ro", [128, SEQ])
        nmx = sb("a_nmx", [128, 2])
        l = sb("a_l", [128, 2])
        r = sb("a_r", [128, 2])
        w = sb("a_w", [128, KD, 128])
        wh, wl = sb("a_wh", [128, 2, KD, 128], F32R), sb("a_wl", [128, 2, KD, 128], F32R)
        zs = sb("a_zs", [128, TOK])
        w_in, w_rounded, w_ready = sem("a_w_in"), sem("a_w_rounded"), sem("a_w_ready")
        z_done, z_read, z_left = sem("a_z_done"), sem("a_z_read"), sem("a_z_left")
        pool_gate = sem("a_pool_gate")
        half_read = sem("a_half_read")
        v_in = sem("a_v_in")
        sp_gate = sem("a_sp_gate")
        squared = [sem("a_squared_q"), sem("a_squared_k")]
        meaned = [sem("a_meaned_q"), sem("a_meaned_k")]
        ms_read = [sem("a_ms_read_q"), sem("a_ms_read_k")]
        r_ready = [sem("a_rq_ready"), sem("a_rk_ready")]
        q_ready, k_ready = sem("a_q_ready"), sem("a_k_ready")
        kt_done, kt_ready = sem("a_kt_done"), sem("a_kt_ready")
        stored = sem("a_stored")
        saved = sem("a_saved")
        scored, max_ready, exp_done = sem("a_scored"), sem("a_max_ready"), sem("a_exp_done")
        a_ready, at_done, at_ready, av_done = sem("a_a_ready"), sem("a_at_done"), sem("a_at_ready"), sem("a_av_done")
        o_squared, o_meaned, o_read, ro_ready = (sem(n) for n in ("a_o_squared", "a_o_meaned", "a_o_read", "a_ro_ready"))
        head_done = sem("a_head_done")
        dve_step = sem("a_dve_step")
        old_sems, m.old_sems = m.old_sems, sem.made
        block = ctx.enter_context(nc.Block())
        flat = m.ps[:, :, :].rearrange("p b n -> p (b n)")

        @block.sync
        def _(sp):
            kp = out.k_prompt[0, 0, :, :, :].rearrange("(t p) h e -> h p t e", p=128)
            vp = out.v_prompt[0, 0, :, :, :].rearrange("(t p) h e -> h p t e", p=128)
            ks = out.k_sample[0, :, :, :, :].rearrange("b t h e -> h (b t) e")
            sp.sem_inc(stored, 1)
            with sp.Fori(0, HEADS) as h:
                def load_w(n):
                    sp.wait_ge(w_ready, h * NZ + n + 1)
                    sp.sem_inc(sp_gate, 1)
                    sp.dma_start(w[:, :, :], w_in_d[:, :, bass.ds(h * 128 + FIRST[n], 128)]).then_inc(w_in, 16)
                load_w(0)
                sp.wait_ge(o_squared, h + 1)
                sp.sem_inc(sp_gate, 1)
                sp.dma_start(v[:, :, :], vp[h, :, :, :]).then_inc(v_in, 16)
                load_w(1)
                sp.wait_ge(kt_ready, h + 1)
                sp.dma_start(kp[h, :, :, :], kt[:, 0:NT, :]).then_inc(stored, 16)
                sp.dma_start(ks[h, :, :], kt[0:NS, NT, :]).then_inc(stored, 16)
                load_w(2)
            sp.wait_ge(stored, 32 * HEADS + 1)

        @block.gpsimd
        def _(pool):
            for s in old_sems:
                pool.sem_clear(s)
            pool.sem_inc(saved, 1)
            pool.sem_inc(z_left, 1)
            with pool.Fori(0, HEADS) as h:
                pool.wait_ge(q_ready, h + 1)
                for mm in range(2):
                    o = m.qbd[64 * mm:64 * mm + 64, h, :, 8 * mm:8 * mm + 8]
                    i = qT[64 * mm:64 * mm + 64, SEQ:TOK].rearrange("p (b t) -> p b t", b=DB)
                    pool.tensor_copy(o, i).then_inc(saved, 1)
                    pool.wait_ge(saved, h * 3 + mm + 1 + 1)
                pool.wait_ge(k_ready, h + 1)
                pool.tensor_copy(m.kS[:, h, :], kT[:, SEQ:TOK]).then_inc(saved, 1)
                pool.wait_ge(saved, h * 3 + 3 + 1)
                for n in range(NZ):
                    pool.wait_ge(z_read, h * UNITS + 3 * n + 3 + 1)
                    pool.sem_inc(pool_gate, 1)
                    pool.dma_start(m.zT[n, h, :, :], zs[:, :]).then_inc(m.z_stored, 16)
                    pool.wait_ge(m.z_stored, h * NZ * 16 + n * 16 + 16)
                    pool.sem_inc(z_left, 1)

        @block.tensor
        def _(pe):
            def mean(n, s, banks):
                for (c0, w0), b in zip(GROUPS, banks):
                    last = pe.matmul(m.ps[:, b, 0:w0], m.halves[:, :], s[:, c0:c0 + w0], start=True, stop=True)
                last.then_inc(meaned[n], 1)

            def prepare(h):
                if not (isinstance(h, int) and h == 0):
                    pe.wait_ge(exp_done, h * 16)
                for n, sn in enumerate((sq, sk)):
                    pe.wait_ge(squared[n], h + 1)
                    mean(n, sn, (3 * n, 3 * n + 1, 3 * n + 2))

            def head(h, prepare_next):
                pe.wait_ge(k_ready, h + 1)
                for t in range(TILES):
                    last = pe.transpose(m.ps[0:rows(t), 3 + t // 4, t % 4 * 128:t % 4 * 128 + 128],
                                        kT[:, cols(t)], m.ident[:, :])
                last.then_inc(kt_done, 1)
                pe.wait_ge(kt_ready, h + 1)

                def project(q):
                    if q == 0:
                        pe.wait_ge(o_read, h + 1)
                    n, (c0, w0) = q // 3, GROUPS[q % 3]
                    if q % 3 == 0:
                        pe.wait_ge(w_ready, h * NZ + n + 1 + 1)
                    pe.wait_ge(z_read, h * UNITS + q + 1)
                    for k in range(KD):
                        for j, (left, right) in enumerate(((wh, m.xh), (wh, m.xl), (wl, m.xh))):
                            ins = pe.matmul(m.ps[:, 7, 0:w0], left[:, n % 2, k, :], right[:, k, c0:c0 + w0],
                                            start=(k == 0 and j == 0), stop=(k == KD - 1 and j == 2))
                    ins.then_inc(z_done, 1)

                def score(i):
                    L = (i + 1) * 128
                    for mm in range(2):
                        if i:
                            pe.wait_ge(exp_done, h * 16 + 2 * i - 1 + mm)
                        for c in range(0, L, 512):
                            w0 = min(512, L - c)
                            last = pe.matmul(m.ps[:, 2 * mm + c // 512, 0:w0],
                                             qT[64 * mm:64 * mm + 64, i * 128:i * 128 + 128],
                                             kT[64 * mm:64 * mm + 64, c:c + w0], start=True, stop=True)
                        last.then_inc(scored, 1)
                score(0)
                for i in range(NT):
                    if i + 1 < NT:
                        score(i + 1)
                    pe.wait_ge(a_ready, h * NT + i + 1)
                    if i:
                        pe.wait_ge(at_ready, h * NT + i)
                    for j in range(i + 1):
                        last = pe.transpose(flat[:, 2048 + j * 128:2048 + j * 128 + 128],
                                            A[:, j * 128:j * 128 + 128], m.ident[:, :])
                    last.then_inc(at_done, 1)
                    project(i)
                    pe.wait_ge(at_ready, h * NT + i + 1)
                    if i == 4:
                        pe.wait_ge(half_read, h + 1)
                    if i == 0:
                        pe.wait_ge(v_in, h * 16 + 16)
                    for j in range(i + 1):
                        last = pe.matmul(m.ps[:, 6, i % 4 * 128:i % 4 * 128 + 128], v[:, j, :],
                                         AT[:, j * 128:j * 128 + 128], start=(j == 0), stop=(j == i))
                    last.then_inc(av_done, 1)
                prepare_next()
                project(UNITS - 1)
                pe.wait_ge(o_squared, h + 1 + 1)
                pe.matmul(m.ps[:, 6, :], m.ones[:, :], so[:, 0:512], start=True, stop=True)
                pe.wait_ge(z_read, h * UNITS + UNITS + 1)
                pe.matmul(m.ps[:, 7, :], m.ones[:, :], so[:, 512:1024], start=True, stop=True).then_inc(o_meaned, 1)
            pe.sem_inc(at_done, 1)
            prepare(0)
            with pe.Fori(0, HEADS - 1) as h:
                head(h, lambda: prepare(h + 1))
            head(HEADS - 1, lambda: None)

        @block.scalar
        def _(act):
            act.sem_inc(o_read, 1)
            act.sem_inc(o_squared, 1)
            act.sem_inc(z_read, 1)
            load_ln_exp(nc, act)

            def squares(h):
                for n, s in enumerate((sq, sk)):
                    z = m.mixT[:, bass.ds(h + HEADS * n, 1), :].squeeze(1)
                    act.activation(s[:, :], z, ACT.Square).then_inc(squared[n], 1)

            def norms(h):
                for n, (rr, banks) in enumerate(((rq, (0, 1, 2)), (rk, (3, 4, 5)))):
                    act.wait_ge(meaned[n], h + 1)
                    for (c0, w0), b in zip(GROUPS, banks):
                        last = act.activation(rr[:, c0:c0 + w0], m.ps[:, b, 0:w0], ACT.Ln, bias=m.eps[:, :])
                    last.then_inc(ms_read[n], 1)
                    act.wait_ge(ms_read[n], h + 1)
                    act.activation(rr[:, :], rr[:, :], ACT.Exp, scale=-0.5).then_inc(r_ready[n], 1)

            def head(h, last):
                def round_w(n):
                    act.wait_ge(w_in, h * NZ * 16 + n * 16 + 16)
                    act.activation(wh[:, n % 2, :, :], w[:, :, :], ACT.Copy).then_inc(w_rounded, 1)

                def read_unit(q):
                    if q % 3 == 0:
                        act.wait_ge(z_left, h * NZ + q // 3 + 1)
                    c0, w0 = GROUPS[q % 3]
                    act.wait_ge(z_done, h * UNITS + q + 1)
                    act.activation(zs[:, c0:c0 + w0], m.ps[:, 7, 0:w0], ACT.Copy).then_inc(z_read, 1)

                def read_o(g):
                    act.wait_ge(av_done, h * NT + 4 * g + 4)
                    act.activation(oT[:, g * 512:g * 512 + 512], m.ps[:, 6, :], ACT.Copy)
                    return act.activation(so[:, g * 512:g * 512 + 512], m.ps[:, 6, :], ACT.Square)
                round_w(0)

                def exps(i):
                    L = (i + 1) * 128
                    for mm in range(2):
                        act.wait_ge(max_ready, h * 16 + 2 * i + mm + 1)
                        act.activation(P[:, mm, 0:L], flat[:, 1024 * mm:1024 * mm + L], ACT.Exp,
                                       bias=nmx[:, mm:mm + 1], accum_out=l[:, mm:mm + 1]).then_inc(exp_done, 1)
                exps(0)
                for i in range(NT):
                    act.wait_ge(at_done, h * NT + i + 1 + 1)
                    L = (i + 1) * 128
                    act.activation(AT[:, 0:L], flat[:, 2048:2048 + L], ACT.Copy).then_inc(at_ready, 1)
                    if i + 1 < NT:
                        exps(i + 1)
                    read_unit(i)
                    if i == 0:
                        round_w(1)
                    if i == 2:
                        round_w(2)
                    if i == 3:
                        act.wait_ge(head_done, h + 1)
                        read_o(0).then_inc(half_read, 1)
                if not last:
                    squares(h + 1)
                read_o(1).then_inc(o_squared, 1)
                read_unit(UNITS - 1)
                if not last:
                    norms(h + 1)
                act.wait_ge(o_meaned, h + 1)
                for g in range(2):
                    ins = act.activation(ro[:, g * 512:g * 512 + 512], m.ps[:, 6 + g, :], ACT.Ln, bias=m.eps[:, :])
                ins.then_inc(o_read, 1)
                act.wait_ge(o_read, h + 1 + 1)
                act.activation(ro[:, :], ro[:, :], ACT.Exp, scale=-0.5).then_inc(ro_ready, 1)
            squares(0)
            norms(0)
            with act.Fori(0, HEADS - 1) as h:
                head(h, False)
            head(HEADS - 1, True)

        @block.vector
        def _(dve):
            step = Steps(dve, dve_step)
            dve.sem_inc(head_done, 1)
            dve.sem_inc(w_ready, 1)

            def prepare(h):
                zq, zk = (m.mixT[:, bass.ds(h + HEADS * n, 1), :].squeeze(1) for n in range(2))
                dve.wait_ge(r_ready[0], h + 1)
                dve.wait_ge(saved, h * 3 + 1)
                dve.scalar_tensor_tensor(qT[:, :], zq, m.qw[:, :], rq[:, :], ALU.mult, ALU.mult).then_inc(q_ready, 1)
                dve.wait_ge(r_ready[1], h + 1)
                dve.scalar_tensor_tensor(kT[:, :], zk, m.kw[:, :], rk[:, :], ALU.mult, ALU.mult).then_inc(k_ready, 1)

            def head(h, prepare_next):
                dve.wait_ge(stored, h * 32 + 1)
                dve.wait_ge(kt_done, h + 1)
                for g in range(2):
                    step(dve.tensor_copy(kt[:, 4 * g:4 * g + 4, :], m.ps[:, 3 + g, :].rearrange("p (t e) -> p t e", t=4)))
                dve.tensor_copy(kt[0:NS, NT, :], m.ps[0:NS, 5, 0:128]).then_inc(kt_ready, 1)

                def maxes(i):
                    L = (i + 1) * 128
                    for mm in range(2):
                        dve.wait_ge(scored, h * 16 + 2 * i + mm + 1)
                        d = flat[:, 1024 * mm + L - 128:1024 * mm + L]
                        step(dve.tensor_tensor(d, d, m.causal[:, :], ALU.add))
                        step.wait()
                        dve.tensor_reduce(nmx[:, mm:mm + 1], flat[:, 1024 * mm:1024 * mm + L], AX.X, ALU.max,
                                          negate=True).then_inc(max_ready, 1)
                def rest_of_w(n):
                    dve.wait_ge(w_rounded, h * NZ + n + 1)
                    dve.tensor_tensor(wl[:, n % 2, :, :], w[:, :, :], wh[:, n % 2, :, :], ALU.subtract).then_inc(w_ready, 1)
                maxes(0)
                rest_of_w(0)
                for i in range(NT):
                    L = (i + 1) * 128
                    dve.wait_ge(exp_done, h * 16 + 2 * i + 2)
                    step(dve.reciprocal(r[:, :], l[:, :]))
                    step.wait()
                    step(dve.tensor_tensor(r[:, :], r[:, :], m.coef[:, :], ALU.mult))
                    step.wait()
                    dve.wait_ge(at_done, h * NT + i + 1)
                    step(dve.tensor_scalar(A[:, 0:L], P[:, 0, 0:L], r[:, 0:1], None, ALU.mult))
                    step.wait()
                    dve.scalar_tensor_tensor(A[:, 0:L], P[:, 1, 0:L], r[:, 1:2], A[:, 0:L],
                                             ALU.mult, ALU.add).then_inc(a_ready, 1)
                    if i + 1 < NT:
                        maxes(i + 1)
                    if i in (1, 3):
                        rest_of_w(1 + i // 2)
                prepare_next()
                dve.wait_ge(ro_ready, h + 1)
                dve.scalar_tensor_tensor(m.mixT[:, h, 0:SEQ], oT[:, :], m.subw[:, :], ro[:, :],
                                         ALU.mult, ALU.mult).then_inc(head_done, 1)
            prepare(0)
            with dve.Fori(0, HEADS - 1) as h:
                step.begin(h, 42)
                head(h, lambda: prepare(h + 1))
                step.end(HEADS - 1)
            head(HEADS - 1, lambda: None)


def hgrn_phase(nc, a, out, m):
    RL = 4
    NL = LEVELS + 1
    SL = list(range(SAMPLE_LEVELS)) + [LEVELS]
    ORDER = ("f", "q", "g")
    PLACE = {"q": 0, "f": 1, "g": 2}
    with ExitStack() as ctx:
        sb, sem = scope(nc, ctx)
        z = {n: sb(f"h_z{n}", [128, TOK]) for n in ORDER}
        si = sb("h_si", [128, 128], I32)
        ti = sb("h_ti", [128, 128], I32)
        xi = sb("h_xi", [128, 128], I32)
        sh = sb("h_sh", [128, 128], I32)
        gt = sb("h_gt", [128, 128], I32)
        mask = sb("h_mask", [128, NL, 128], U8)
        bmask = sb("h_bmask", [NS, DB])
        keep = sb("h_keep", [128, TOK])
        q, f, kk, lf, b, eb, qe, kd, oT, so, ro = (sb(f"h_{n}", [128, TOK]) for n in (
            "q", "f", "kk", "lf", "b", "eb", "qe", "kd", "oT", "so", "ro"))
        E = sb("h_E", [128, RL, TOK])
        X = sb("h_X", [128, RL, TOK])
        AT = sb("h_AT", [128, TILES, 128])
        v = sb("h_v", [128, TILES, 128])
        ket = sb("h_ket", [128, TILES, 128])
        eB = sb("h_eB", [128, NT + DB])
        S = sb("h_S", [128, NT + 1, 128])
        Ss = sb("h_Ss", [128, DB, 128])
        Sn = sb("h_Sn", [128, DB, 128])
        vblk = sb("h_vblk", [NS, DB, 128])
        z_in = {n: sem(f"h_z_in_{n}") for n in ORDER}
        v_in = sem("h_v_in")
        vblk_ready = sem("h_vblk_ready")
        sig = {n: sem(f"h_sigmoid_{n}") for n in ("f", "q", "g")}
        s_in, stored = sem("h_s_in"), sem("h_stored")
        f_ready, lf_ready, b_ready, q_ready, g_ready = (sem(f"h_{n}_ready") for n in ("f", "lf", "b", "q", "g"))
        sub_done, exp_done, x_ready, level_done, level_read = (sem(f"h_{n}") for n in (
            "sub_done", "exp_done", "x_ready", "level_done", "level_read"))
        kd_sub, kd_exp, eb_ready, ke_ready, qe_ready = (sem(f"h_{n}") for n in (
            "kd_sub", "kd_exp", "eb_ready", "ke_ready", "qe_ready"))
        ket_done, ket_ready, u_done, us_done, s_ready = (sem(f"h_{n}") for n in (
            "ket_done", "ket_ready", "u_done", "us_done", "s_ready"))
        at_zero, o_done, o_squared, o_meaned, o_read, ro_ready, head_done = (sem(f"h_{n}") for n in (
            "at_zero", "o_done", "o_squared", "o_meaned", "o_read", "ro_ready", "head_done"))
        sp_gate = sem("h_sp_gate")
        gate, gate_pool = sem("h_gate"), sem("h_gate_pool")
        iota_done, setup_step, dve_step = sem("h_iota_done"), sem("h_setup_step"), sem("h_dve_step")
        old_sems, m.old_sems = m.old_sems, sem.made
        block = ctx.enter_context(nc.Block())
        flat = m.ps[:, :, :].rearrange("p b n -> p (b n)")

        def heads(eng, prepare, head, steps=None, per=0):
            prepare(0)
            with eng.Fori(0, HEADS - 1) as h:
                if steps:
                    steps.begin(h, per)
                head(h, lambda: prepare(h + 1))
                if steps:
                    steps.end(HEADS - 1)
            head(HEADS - 1, lambda: None)

        def gate_of(h):
            return m.mixT[:, bass.ds(h + HEADS, 1), :].squeeze(1)

        def halves(t, lv):
            c = 1 << lv
            wd = TOK if lv < SAMPLE_LEVELS else SEQ
            x = t[:, 0:wd].rearrange("p (n two c) -> p n two c", two=2, c=c)
            n = wd // (2 * c)
            return x[:, :, 0, :], x[:, :, 1, :], x[:, :, 0, c - 1:c].to_broadcast([128, n, c])

        @block.sync
        def _(sp):
            state = a.state_hgrn[0, :, :, :, :].rearrange("b h k v -> h k b v")
            new = out.hgrn_sample[0, :, :, :, :].rearrange("b h k v -> h k b v")
            zi = m.zi[:, 0:SEQ, :].rearrange("h (t p) e -> h p t e", p=128)
            sp.sem_inc(stored, 1)

            def load_z(h):
                for n, used in (("f", sig["f"]), ("q", q_ready), ("g", g_ready)):
                    sp.wait_ge(used, h + 1)
                    sp.sem_inc(sp_gate, 1)
                    sp.dma_start(z[n][:, :], m.zT[PLACE[n], h, :, :]).then_inc(z_in[n], 16)

            def head(h, load_next_z):
                sp.wait_ge(o_done, h + 1)
                sp.sem_inc(sp_gate, 1)
                sp.dma_start(v[:, 0:NT, :], zi[h, :, :, :]).then_inc(v_in, 16)
                sp.dma_start(v[0:NS, NT, :], m.zi[h, SEQ:TOK, :]).then_inc(v_in, 16)
                sp.dma_start(Ss[:, :, :], state[h, :, :, :]).then_inc(s_in, 16)
                load_next_z()
                sp.wait_ge(s_ready, h * 2 + 2)
                sp.dma_start(out.hgrn_prompt[0, 0, h, :, :], S[:, NT, :]).then_inc(stored, 16)
                sp.dma_start(new[h, :, :, :], Sn[:, :, :]).then_inc(stored, 16)
            heads(sp, load_z, head)
            sp.wait_ge(stored, 32 * HEADS + 1)

        @block.gpsimd
        def _(pool):
            for s in old_sems:
                pool.sem_clear(s)
            pool.iota(si[:, :], [[0, 128]], base=0, channel_multiplier=1).then_inc(iota_done, 1)
            pool.iota(ti[:, :], [[1, 128]], base=0, channel_multiplier=0).then_inc(iota_done, 1)
            pool.memset(S[:, 0, :], 0.0).then_inc(iota_done, 1)
            pool.memset(keep[:, :], 1.0).then_inc(iota_done, 1)
            pool.wait_ge(iota_done, 4)
            pool.memset(keep[:, 0:SEQ].rearrange("p (n c) -> p n c", c=128)[:, :, 0:1], 0.0).then_inc(iota_done, 1)
            pool.memset(keep[:, SEQ:TOK].rearrange("p (n c) -> p n c", c=DS)[:, :, 0:1], 0.0).then_inc(iota_done, 1)

            def head(h, _):
                pool.wait_ge(kd_exp, h + 1)
                pool.tensor_tensor(kd[:, :], kd[:, :], kk[:, :], ALU.mult).then_inc(ke_ready, 1)
                pool.wait_ge(o_done, h + 1)
                pool.sem_inc(gate_pool, 1)
                pool.memset(AT[:, :, :], 0.0).then_inc(at_zero, 1)
                pool.wait_ge(q_ready, h + 1 + 1)
                for lv in range(LEVELS):
                    u = lv % RL
                    pool.wait_ge(exp_done, h * LEVELS + lv + 1)
                    if lv >= RL:
                        pool.wait_ge(level_done, h * NL + lv - RL + 1)
                    ke, _, _ = halves(kk, lv)
                    _, qo, _ = halves(q, lv)
                    ee, eo, _ = halves(E[:, u, :], lv)
                    xe, xo, _ = halves(X[:, u, :], lv)
                    pool.tensor_tensor(xe, ee, ke, ALU.mult)
                    pool.tensor_tensor(xo, eo, qo, ALU.mult).then_inc(x_ready, 1)
                    if lv == RL:
                        pool.wait_ge(eb_ready, h + 1)
                        pool.tensor_tensor(qe[:, :], eb[:, :], q[:, :], ALU.mult).then_inc(qe_ready, 1)
            with pool.Fori(0, HEADS) as h:
                head(h, None)

        @block.tensor
        def _(pe):
            pe.sem_inc(o_done, 1)
            with pe.Fori(0, HEADS) as h:
                pe.wait_ge(o_read, h + 1)
                pe.wait_ge(ke_ready, h + 1)
                for t in range(TILES):
                    last = pe.transpose(flat[0:rows(t), (3072 + t * 128 if t < NT else 2560):(3200 + t * 128 if t < NT else 2688)],
                                        kd[:, cols(t)], m.ident[:, :])
                last.then_inc(ket_done, 1)
                pe.wait_ge(ket_ready, h + 1)
                pe.wait_ge(v_in, h * 32 + 32)
                for t in range(NT):
                    last = pe.matmul(flat[:, 3072 + t * 128:3200 + t * 128], ket[:, t, :], v[:, t, :], start=True, stop=True)
                last.then_inc(u_done, 1)
                for lv in range(NL):
                    u = lv % 2
                    if lv < LEVELS:
                        pe.wait_ge(x_ready, h * LEVELS + lv + 1)
                        left = right = X[:, lv % RL, :]
                    else:
                        left, right = kk, q
                        pe.wait_ge(q_ready, h + 1 + 1)
                    if lv >= 2:
                        pe.wait_ge(level_read, h * NL + lv - 1)
                    for t in range(NT):
                        last = pe.matmul(flat[:, 1024 * u + t * 128:1024 * u + t * 128 + 128],
                                         left[:, cols(t)], right[:, cols(t)], start=True, stop=True)
                    if lv in SL:
                        last = pe.matmul(m.ps[0:NS, 4 + u, 0:NS], left[:, cols(NT)], right[:, cols(NT)], start=True, stop=True)
                    last.then_inc(level_done, 1)
                pe.wait_ge(level_read, h * NL + NL)
                pe.wait_ge(vblk_ready, h + 1)
                for n in range(2):
                    last = pe.matmul(m.ps[:, 4 + n, :], ket[0:NS, NT, :],
                                     vblk[:, 4 * n:4 * n + 4, :].rearrange("p b e -> p (b e)"), start=True, stop=True)
                last.then_inc(us_done, 1)
                pe.wait_ge(s_ready, h * 2 + 1)
                pe.wait_ge(s_in, h * 16 + 16)
                pe.wait_ge(qe_ready, h + 1)
                for t in range(NT):
                    o = flat[:, t * 128:t * 128 + 128]
                    pe.matmul(o, S[:, t, :], qe[:, cols(t)], start=True, stop=False)
                    pe.matmul(o, v[:, t, :], AT[:, t, :], start=False, stop=True)
                for n in range(DB):
                    pe.matmul(m.ps[:, 2, n * DS:n * DS + DS], Ss[:, n, :], qe[:, SEQ + n * DS:SEQ + n * DS + DS],
                              start=(n == 0), stop=False, skip_group_check=True)
                last = pe.matmul(m.ps[:, 2, 0:NS], v[0:NS, NT, :], AT[0:NS, NT, 0:NS], start=False, stop=True,
                                 skip_group_check=True)
                last.then_inc(o_done, 1)
                pe.wait_ge(o_squared, h + 1)
                for o, s0, n0 in ((3 * 512, 0, 512), (6 * 512, 512, 512), (7 * 512, 1024, NS)):
                    last = pe.matmul(flat[:, o:o + n0], m.ones[:, :], so[:, s0:s0 + n0], start=True, stop=True)
                last.then_inc(o_meaned, 1)

        @block.scalar
        def _(act):
            OG = ((0, 0, 512), (1, 512, 512), (2, 1024, NS))
            act.sem_inc(o_read, 1)
            act.sem_inc(sig["f"], 1)

            def open_gates(h):
                if not (isinstance(h, int) and h == 0):
                    act.wait_ge(level_done, h * NL)
                    act.wait_ge(qe_ready, h)
                for n, dst in (("f", f[:, :]), ("q", q[:, :]), ("g", gate_of(h))):
                    act.wait_ge(z_in[n], h * 16 + 16)
                    act.activation(dst, z[n][:, :], ACT.Sigmoid).then_inc(sig[n], 1)
                load_ln_exp(nc, act)
                act.wait_ge(f_ready, h + 1)
                act.activation(lf[:, :], f[:, :], ACT.Ln).then_inc(lf_ready, 1)

            def decays(h):
                act.wait_ge(b_ready, h + 1)
                bp = b[:, 0:SEQ].rearrange("p (n c) -> p n c", c=128)[:, :, 127:128]
                bs = b[:, SEQ:TOK].rearrange("p (n c) -> p n c", c=DS)[:, :, DS - 1:DS]
                act.activation(eB[:, 0:NT].unsqueeze(2), bp, ACT.Exp)
                act.activation(eB[:, NT:NT + DB].unsqueeze(2), bs, ACT.Exp)
                act.activation(eb[:, :], b[:, :], ACT.Exp).then_inc(eb_ready, 1)
                act.wait_ge(kd_sub, h + 1)
                act.activation(kd[:, :], kd[:, :], ACT.Exp).then_inc(kd_exp, 1)

            def head(h, last):
                for lv in range(LEVELS):
                    wd = TOK if lv < SAMPLE_LEVELS else SEQ
                    act.wait_ge(sub_done, h * LEVELS + lv + 1)
                    act.activation(E[:, lv % RL, 0:wd], E[:, lv % RL, 0:wd], ACT.Exp).then_inc(exp_done, 1)
                if not last:
                    open_gates(h + 1)
                act.wait_ge(o_done, h + 1 + 1)
                act.wait_ge(head_done, h + 1)
                for bk, s0, n0 in OG:
                    act.activation(oT[:, s0:s0 + n0], m.ps[:, bk, 0:n0], ACT.Copy)
                    ins = act.activation(so[:, s0:s0 + n0], m.ps[:, bk, 0:n0], ACT.Square)
                ins.then_inc(o_squared, 1)
                if not last:
                    decays(h + 1)
                act.wait_ge(o_meaned, h + 1)
                for bk, (_, s0, n0) in zip((3, 6, 7), OG):
                    ins = act.activation(ro[:, s0:s0 + n0], m.ps[:, bk, 0:n0], ACT.Ln, bias=m.eps[:, :])
                ins.then_inc(o_read, 1)
                act.wait_ge(o_read, h + 1 + 1)
                act.activation(ro[:, :], ro[:, :], ACT.Exp, scale=-0.5).then_inc(ro_ready, 1)
            open_gates(0)
            decays(0)
            with act.Fori(0, HEADS - 1) as h:
                head(h, False)
            head(HEADS - 1, True)

        @block.vector
        def _(dve):
            step = Steps(dve, dve_step)
            dve.sem_inc(head_done, 1)
            dve.sem_inc(q_ready, 1)
            dve.sem_inc(g_ready, 1)

            def subs(h, lv):
                if lv >= RL:
                    dve.wait_ge(x_ready, h * LEVELS + lv - RL + 1)
                be, bo, br = halves(b, lv)
                ee, eo, _ = halves(E[:, lv % RL, :], lv)
                dve.tensor_tensor(ee, br, be, ALU.subtract)
                dve.tensor_tensor(eo, bo, br, ALU.subtract).then_inc(sub_done, 1)

            def prepare(h):
                dve.wait_ge(sig["f"], h + 1 + 1)
                step(dve.tensor_scalar(f[:, :], f[:, :], m.lb1[:, bass.ds(h, 1)], m.lb[:, bass.ds(h, 1)], ALU.mult, ALU.add))
                step.wait()
                dve.sem_inc(f_ready, 1)
                step(dve.tensor_scalar(kk[:, :], f[:, :], -1.0, 1.0, ALU.mult, ALU.add))
                dve.wait_ge(sig["q"], h + 1)
                dve.tensor_tensor(q[:, :], q[:, :], z["q"][:, :], ALU.mult).then_inc(q_ready, 1)
                dve.wait_ge(lf_ready, h + 1)
                if isinstance(h, int):
                    dve.wait_ge(iota_done, 6)
                dve.tensor_tensor_scan(b[:, :], keep[:, :], lf[:, :], 0.0, ALU.mult, ALU.add).then_inc(b_ready, 1)
                dve.wait_ge(b_ready, h + 1)
                for c0, c1, c in ((0, SEQ, 128), (SEQ, TOK, DS)):
                    bv = b[:, c0:c1].rearrange("p (n c) -> p n c", c=c)
                    kv = kd[:, c0:c1].rearrange("p (n c) -> p n c", c=c)
                    last = dve.tensor_tensor(kv, bv[:, :, c - 1:c].to_broadcast([128, (c1 - c0) // c, c]), bv, ALU.subtract)
                last.then_inc(kd_sub, 1)
                for lv in range(RL):
                    subs(h, lv)
                dve.wait_ge(sig["g"], h + 1)
                dve.tensor_tensor(gate_of(h), gate_of(h), z["g"][:, :], ALU.mult).then_inc(g_ready, 1)

            def head(h, prepare_next):
                def collect(lv):
                    dve.wait_ge(level_done, h * NL + lv + 1)
                    if lv:
                        dve.wait_ge(level_read, h * NL + lv)
                    dve.sem_inc(gate, 1)
                    u = lv % 2
                    mk = mask[:, lv, :].unsqueeze(1).to_broadcast([128, 4, 128])
                    for g2 in range(2):
                        last = dve.copy_predicated(AT[:, 4 * g2:4 * g2 + 4, :], mk,
                                                   m.ps[:, 2 * u + g2, :].rearrange("p (t n) -> p t n", t=4))
                    if lv in SL:
                        last = dve.copy_predicated(AT[0:NS, NT, 0:NS], mask[0:NS, lv, 0:NS], m.ps[0:NS, 4 + u, 0:NS])
                    last.then_inc(level_read, 1)

                dve.wait_ge(v_in, h * 32 + 32)
                dve.tensor_tensor(vblk[:, :, :], v[0:NS, NT, :].unsqueeze(1).to_broadcast([NS, DB, 128]),
                                  bmask[:, :].unsqueeze(2).to_broadcast([NS, DB, 128]), ALU.mult).then_inc(vblk_ready, 1)
                dve.wait_ge(ket_done, h + 1)
                for n in range(2):
                    dve.tensor_copy(ket[:, 4 * n:4 * n + 4, :], m.ps[:, 6 + n, :].rearrange("p (t e) -> p t e", t=4))
                dve.tensor_copy(ket[0:NS, NT, :], m.ps[0:NS, 5, 0:128]).then_inc(ket_ready, 1)
                dve.wait_ge(at_zero, h + 1)
                collect(0)
                subs(h, RL)
                dve.wait_ge(eb_ready, h + 1)
                dve.wait_ge(u_done, h + 1)
                dve.wait_ge(stored, h * 32 + 1)
                for t in range(NT):
                    ins = dve.scalar_tensor_tensor(S[:, t + 1, :], S[:, t, :], eB[:, t:t + 1],
                                                   flat[:, 3072 + t * 128:3200 + t * 128], ALU.mult, ALU.add)
                    step(ins)
                    step.wait()
                dve.sem_inc(s_ready, 1)
                for lv in range(1, NL):
                    collect(lv)
                    if lv + RL < LEVELS:
                        subs(h, lv + RL)
                dve.wait_ge(us_done, h + 1)
                dve.wait_ge(s_in, h * 16 + 16)
                for n in range(DB):
                    step(dve.scalar_tensor_tensor(Sn[:, n, :], Ss[:, n, :], eB[:, NT + n:NT + n + 1],
                                                  flat[:, 2048 + n * 128:2176 + n * 128], ALU.mult, ALU.add))
                step.wait()
                dve.sem_inc(s_ready, 1)
                prepare_next()
                dve.wait_ge(ro_ready, h + 1)
                dve.scalar_tensor_tensor(oT[:, :], oT[:, :], m.hgw[:, :], ro[:, :], ALU.mult, ALU.mult).then_inc(head_done, 1)
                dve.wait_ge(head_done, h + 1 + 1)
                dve.wait_ge(g_ready, h + 1 + 1)
                dve.tensor_tensor(gate_of(h), oT[:, :], gate_of(h), ALU.mult)
            def masks():
                setup = Steps(dve, setup_step)
                setup(dve.tensor_tensor(xi[:, :], si[:, :], ti[:, :], ALU.bitwise_xor))
                setup(dve.tensor_tensor(gt[:, :], ti[:, :], si[:, :], ALU.is_gt))
                setup(dve.tensor_tensor(mask[:, LEVELS, :], ti[:, :], si[:, :], ALU.is_equal))
                setup.wait()
                setup(dve.tensor_scalar(sh[:, :], si[:, :], 3, None, ALU.logical_shift_right))
                setup.wait()
                setup(dve.tensor_tensor(bmask[:, :], sh[0:NS, 0:DB], ti[0:NS, 0:DB], ALU.is_equal))
                setup.wait()
                for lv in range(LEVELS):
                    setup(dve.tensor_scalar(sh[:, :], xi[:, :], lv, None, ALU.logical_shift_right))
                    setup.wait()
                    setup(dve.scalar_tensor_tensor(mask[:, lv, :], sh[:, :], 1, gt[:, :], ALU.is_equal, ALU.mult))
                    setup.wait()

            def prepare_first(h):
                prepare(h)
                if isinstance(h, int):
                    masks()
            heads(dve, prepare_first, head, step, 18)


def decode_phase(nc, a, out, m):
    KEYS = PAGES * PAGE
    with ExitStack() as ctx:
        sb, sem = scope(nc, ctx)
        pt = sb("d_pt", [1, DB * PAGES], I32)
        K = sb("d_K", [128, 2, PG, 512])
        V = sb("d_V", [128, 2, PAGES, 512])
        Vn = sb("d_Vn", [DS, 2, 512])
        sN = sb("d_sN", [128, DS])
        KT = sb("d_KT", [128, 2, HEADS, PG * PAGE])
        qb = sb("d_qb", [128, 2, HEADS, 32])
        kb = sb("d_kb", [128, 2, HEADS, DS])
        P = sb("d_P", [128, 2, KEYS + DS])
        PT = sb("d_PT", [128, 2, PG * 128])
        PTn = sb("d_PTn", [DS, 128])
        O = sb("d_O", [128, 512])
        pat0 = sb("d_pat0", [128, 32])
        pat1 = sb("d_pat1", [128, 32])
        pat = sb("d_pat", [128, 32])
        C = sb("d_C", [128, 2, 32])
        cmask = sb("d_cmask", [128, DS])
        pr = sb("d_pr", [128, 1], I32)
        tq = sb("d_tq", [128, 1], I32)
        tk = sb("d_tk", [128, DS], I32)
        tqf = sb("d_tqf", [128, 1])
        mx = sb("d_mx", [128, 2])
        nmx = sb("d_nmx", [128, 1])
        l = sb("d_l", [128, 2])
        r = sb("d_r", [128, 1])
        oS = sb("d_oS", [128, HEADS, NS])
        so = sb("d_so", [128, HEADS, NS])
        ro = sb("d_ro", [128, HEADS, NS])
        gate = sem("d_gate")
        pt_in = sem("d_pt_in")
        k_in = [sem("d_k_in0"), sem("d_k_in1")]
        v_in = [sem("d_v_in0"), sem("d_v_in1")]
        kt_done = sem("d_kt_done")
        kt_ready = [sem("d_kt_ready_even"), sem("d_kt_ready_odd")]
        qb_ready, scored, max_ready, exp_done, c_ready = (sem(f"d_{n}") for n in (
            "qb_ready", "scored", "max_ready", "exp_done", "c_ready"))
        pt_done, pt_ready, new_done, new_read = (sem(f"d_{n}") for n in ("pt_done", "pt_ready", "new_done", "new_read"))
        av_done, acc_ready, picked, o_ready = (sem(f"d_{n}") for n in ("av_done", "acc_ready", "picked", "o_ready"))
        o_squared, o_meaned, o_read, ro_ready = (sem(f"d_{n}") for n in ("o_squared", "o_meaned", "o_read", "ro_ready"))
        iota_done, setup_step, dve_step, act_step = (sem(f"d_{n}") for n in (
            "iota_done", "setup_step", "dve_step", "act_step"))
        block = ctx.enter_context(nc.Block())
        flat = m.ps[:, :, :].rearrange("p b n -> p (b n)")
        kc = a.cache_k[0, :, :, :, :].rearrange("n p h e -> n p (h e)")
        vc = a.cache_v[0, :, :, :, :].rearrange("n p h e -> n p (h e)")
        S_NEW, PT_NEW, OT = m.ps[:, 4, 0:DS], m.ps[0:DS, 4, 128:256], m.ps[:, 7, 0:HEADS * DS]
        VROUND = (PAGES + 1) * 16

        def requests(eng, unit):
            unit(0, 0, None)
            with eng.Fori(0, DB // 2 - 1) as i:
                unit(i * 2 + 1, 1, i)
                unit(i * 2 + 2, 0, i)
            unit(DB - 1, 1, DB // 2 - 1)

        @block.sync
        def _(sp):
            sp.dma_start(pt[:, :], a.page_table.rearrange("(o b) n -> o (b n)", o=1)).then_inc(pt_in, 16)
            sp.wait_ge(pt_in, 16)

            def page_numbers(b, g):
                _, pages = nc.values_load_multi_w_load_instructions(
                    pt[0:1, bass.ds(b * PAGES + g * PG, PG)], engines=[mybir.EngineType.SP], min_val=0,
                    max_val=a.cache_k.shape[1] - 1)
                return pages

            def load_keys(b, g, pages, early):
                if not early or b * NPG + g >= 2:
                    sp.wait_ge(kt_done, (b * NPG + g - 1) * HEADS)
                    sp.sem_inc(gate, 1)
                for j, page in enumerate(pages):
                    sp.dma_start(K[:, g % 2, j, :], kc[page, :, :]).then_inc(k_in[g % 2], 16)

            def load_values(u, g, pages):
                for j, page in enumerate(pages):
                    sp.dma_start(V[:, u, g * PG + j, :], vc[page, :, :]).then_inc(v_in[u], 16)

            def load(b, u, early):
                pages = []
                for g in range(2):
                    pages.append(page_numbers(b, g))
                    load_keys(b, g, pages[g], early)
                if not early:
                    sp.wait_ge(av_done, b - 1)
                    sp.sem_inc(gate, 1)
                for g in range(2):
                    load_values(u, g, pages[g])
                for g in range(2, NPG):
                    more = page_numbers(b, g)
                    load_keys(b, g, more, early)
                    load_values(u, g, more)
                sp.dma_start(Vn[:, u, :], out.v_sample[0, b, :, :, :].rearrange("t h e -> t (h e)")).then_inc(v_in[u], 16)
            load(0, 0, True)
            load(1, 1, True)
            with sp.Fori(1, DB // 2) as i:
                for u in range(2):
                    load(i * 2 + u, u, False)

        @block.gpsimd
        def _(pool):
            pool.memset(pat0[:, :], 0.0).then_inc(iota_done, 1)
            pool.memset(pat1[:, :], 0.0).then_inc(iota_done, 1)
            pool.iota(pr[:, :], [[0, 1]], base=0, channel_multiplier=1).then_inc(iota_done, 1)
            pool.iota(tk[:, :], [[1, DS]], base=0, channel_multiplier=0).then_inc(iota_done, 1)
            pool.wait_ge(iota_done, 4)
            for p, base in ((pat0, 0), (pat1, -DS)):
                v = p[:, :].rearrange("p (h t) -> p h t", h=HEADS)
                pool.affine_select(out=v, in_=v, compare_op=ALU.not_equal, fill=1.0, base=base,
                                   pattern=[[-32, HEADS], [-1, DS]], channel_multiplier=1).then_inc(iota_done, 1)

        @block.tensor
        def _(pe):
            def transpose_keys(b, g, h, first):
                if h == 0:
                    pe.wait_ge(k_in[g % 2], (b * 2 + g // 2 + 1) * PG * 16)
                if not (first and g == 0 and h < 2):
                    pe.wait_ge(kt_ready[h % 2], b * 8 + g * 2 + h // 2)
                if not first and g == 0 and h == 0:
                    pe.wait_ge(new_read, b)
                for j in range(PG):
                    ins = pe.transpose(m.ps[:, 4 + h % 2, j * 128:j * 128 + 128],
                                       K[:, g % 2, j, h * 128:h * 128 + 128], m.ident[:, :])
                ins.then_inc(kt_done, 1)

            def score(b, u, g, h):
                pe.wait_ge(kt_ready[h % 2], b * 8 + g * 2 + h // 2 + 1)
                return pe.matmul(m.ps[32 * h:32 * h + 32, g, :], qb[:, u, h, :], KT[:, g % 2, h, :],
                                 start=True, stop=True)

            def transpose_map(b, u, g):
                if g:
                    pe.wait_ge(pt_ready, b * NPG + g)
                else:
                    pe.wait_ge(exp_done, b + 1)
                    pe.wait_ge(o_ready, b + 1)
                for j in range(PG):
                    p = (g * PG + j) * 128
                    ins = pe.transpose(m.ps[:, 7, j * 128:j * 128 + 128], P[:, u, p:p + 128], m.ident[:, :])
                ins.then_inc(pt_done, 1)

            def values(b, u, g):
                pe.wait_ge(pt_ready, b * NPG + g + 1)
                for j in range(PG):
                    pe.matmul(m.ps[:, 6, :], PT[:, g % 2, j * 128:j * 128 + 128], V[:, u, g * PG + j, :],
                              start=(g == 0 and j == 0), stop=False)

            def new_values(b, u):
                pe.wait_ge(new_read, b + 2)
                pe.matmul(m.ps[:, 6, :], PTn[:, :], Vn[:, u, :], start=False, stop=True).then_inc(av_done, 1)

            def pick(b, u):
                pe.wait_ge(acc_ready, b + 1)
                pe.wait_ge(c_ready, b + 1)
                for h in range(HEADS):
                    ins = pe.matmul(m.ps[:, 7, h * DS:h * DS + DS], O[:, h * 128:h * 128 + 128],
                                    C[:, u, h * DS:h * DS + DS], start=True, stop=True)
                ins.then_inc(picked, 1)

            def unit(b, u, i):
                last = isinstance(b, int) and b == DB - 1
                pe.wait_ge(qb_ready, b + 1)
                if i is not None:
                    pe.wait_ge(exp_done, b)
                for g in range(1, NPG):
                    for h in range(HEADS):
                        transpose_keys(b, g, h, i is None)
                        score(b, u, g - 1, h)
                    if i is not None:
                        if g == 1:
                            pe.wait_ge(v_in[1 - u], i * VROUND + VROUND)
                        else:
                            values(b - 1, 1 - u, g - 2)
                        transpose_map(b - 1, 1 - u, g - 1)
                for h in range(HEADS):
                    score(b, u, NPG - 1, h)
                for h in range(HEADS):
                    ins = pe.matmul(m.ps[32 * h:32 * h + 32, 4, 0:DS], qb[:, u, h, :],
                                    kb[:, u, h, :], start=True, stop=True)
                ins.then_inc(scored, 1)
                if i is not None:
                    pe.transpose(PT_NEW, P[:, 1 - u, KEYS:KEYS + DS], m.ident[:, :]).then_inc(new_done, 1)
                    values(b - 1, 1 - u, 2)
                    transpose_map(b - 1, 1 - u, 3)
                if not last:
                    for h in range(2):
                        transpose_keys(b + 1, 0, h, False)
                if i is not None:
                    values(b - 1, 1 - u, 3)
                    new_values(b - 1, 1 - u)
                if not last:
                    for h in range(2, HEADS):
                        transpose_keys(b + 1, 0, h, False)
                if i is not None:
                    pick(b - 1, 1 - u)
            for h in range(HEADS):
                transpose_keys(0, 0, h, True)
            requests(pe, unit)
            pe.wait_ge(v_in[1], DB // 2 * VROUND)
            pe.wait_ge(new_read, DB)
            pe.wait_ge(exp_done, DB)
            pe.transpose(PT_NEW, P[:, 1, KEYS:KEYS + DS], m.ident[:, :]).then_inc(new_done, 1)
            for g in range(NPG):
                transpose_map(DB - 1, 1, g)
                values(DB - 1, 1, g)
            new_values(DB - 1, 1)
            pick(DB - 1, 1)
            pe.wait_ge(o_squared, 1)
            pe.matmul(m.ps[:, 0, 0:HEADS * NS], m.ones[:, :], so[:, :, :].rearrange("p h t -> p (h t)"),
                      start=True, stop=True).then_inc(o_meaned, 1)

        @block.scalar
        def _(act):
            load_ln_exp(nc, act)

            def keys(b, g):
                for h in (1, 3):
                    act.wait_ge(kt_done, b * 16 + g * 4 + h + 1)
                    act.activation(KT[:, g % 2, h, :], m.ps[:, 5, :], ACT.Copy).then_inc(kt_ready[1], 1)

            def map_out(b, g):
                act.wait_ge(pt_done, b * NPG + g + 1)
                act.activation(PT[:, g % 2, :], m.ps[:, 7, :], ACT.Copy).then_inc(pt_ready, 1)

            def unit(b, u, i):
                for g in range(1, NPG):
                    keys(b, g)
                    if i is not None and g >= 2:
                        map_out(b - 1, g - 1)
                act.wait_ge(max_ready, b + 1)
                act.activation(P[:, u, 0:KEYS], flat[:, 0:KEYS], ACT.Exp, bias=nmx[:, :], accum_out=l[:, 0:1])
                act.activation(P[:, u, KEYS:KEYS + DS], sN[:, :], ACT.Exp, bias=nmx[:, :],
                               accum_out=l[:, 1:2]).then_inc(exp_done, 1)
                if not (isinstance(b, int) and b == DB - 1):
                    keys(b + 1, 0)
            keys(0, 0)
            requests(act, unit)
            for g in (1, 2):
                map_out(DB - 1, g)
            act.wait_ge(o_ready, DB + 1)
            act.activation(so[:, :, :], oS[:, :, :], ACT.Square).then_inc(o_squared, 1)
            act.wait_ge(o_meaned, 1)
            mean = m.ps[:, 0, 0:HEADS * NS].rearrange("p (h t) -> p h t", h=HEADS)
            act.activation(ro[:, :, :], mean, ACT.Ln, bias=m.eps[:, :]).then_inc(o_read, 1)
            act.wait_ge(o_read, 1)
            act.activation(ro[:, :, :], ro[:, :, :], ACT.Exp, scale=-0.5).then_inc(ro_ready, 1)

        @block.vector
        def _(dve):
            setup = Steps(dve, setup_step)
            dve.wait_ge(iota_done, 6)
            setup(dve.tensor_scalar(tq[:, :], pr[:, :], DS - 1, None, ALU.bitwise_and))
            setup(dve.scalar_tensor_tensor(pat[:, :], pat1[:, :], m.coef[:, 1:2], pat0[:, :], ALU.mult, ALU.add))
            setup.wait()
            setup(dve.tensor_copy(tqf[:, :], tq[:, :]))
            setup.wait()
            setup(dve.tensor_scalar(cmask[:, :], tk[:, :], tqf[:, :], NEG, ALU.is_gt, ALU.mult))
            setup.wait()
            dve.sem_inc(o_ready, 1)
            step = Steps(dve, dve_step)

            def keys(b, g):
                for h in (0, 2):
                    dve.wait_ge(kt_done, b * 16 + g * 4 + h + 1)
                    dve.tensor_copy(KT[:, g % 2, h, :], m.ps[:, 4, :]).then_inc(kt_ready[0], 1)

            def queries(b, u):
                dve.tensor_copy(kb[:, u, :, :], m.kS[:, :, bass.ds(b * DS, DS)])
                dve.tensor_copy(qb[:, u, :, :], m.qbd[:, :, bass.ds(b, 1), :].squeeze(2)).then_inc(qb_ready, 1)

            def map_out(b, g):
                dve.wait_ge(pt_done, b * NPG + g + 1)
                dve.tensor_copy(PT[:, g % 2, :], m.ps[:, 7, :]).then_inc(pt_ready, 1)

            def new_map(b):
                dve.wait_ge(new_done, b + 1)
                dve.tensor_copy(PTn[:, :], PT_NEW).then_inc(new_read, 1)

            def collect(b):
                dve.wait_ge(av_done, b + 1)
                dve.tensor_copy(O[:, :], m.ps[:, 6, :]).then_inc(acc_ready, 1)

            def unit(b, u, i):
                last = isinstance(b, int) and b == DB - 1
                for g in range(1, NPG):
                    keys(b, g)
                    if i is not None and g == 1:
                        map_out(b - 1, 0)
                dve.wait_ge(scored, b + 1)
                if i is not None:
                    dve.wait_ge(new_done, b)
                step(dve.tensor_tensor(sN[:, :], S_NEW, cmask[:, :], ALU.add))
                if i is not None:
                    new_map(b - 1)
                step.wait()
                if i is None:
                    dve.sem_inc(new_read, 1)
                step(dve.tensor_reduce(mx[:, 0:1], flat[:, 0:KEYS], AX.X, ALU.max))
                step(dve.tensor_reduce(mx[:, 1:2], sN[:, :], AX.X, ALU.max))
                step.wait()
                dve.tensor_reduce(nmx[:, :], mx[:, :], AX.X, ALU.max, negate=True).then_inc(max_ready, 1)
                if i is not None:
                    map_out(b - 1, 3)
                if not last:
                    queries(b + 1, 1 - u)
                    keys(b + 1, 0)
                dve.wait_ge(exp_done, b + 1)
                step(dve.tensor_tensor(r[:, :], l[:, 0:1], l[:, 1:2], ALU.add))
                step.wait()
                step(dve.reciprocal(r[:, :], r[:, :]))
                step.wait()
                dve.tensor_scalar(C[:, u, :], pat[:, :], r[:, :], None, ALU.mult).then_inc(c_ready, 1)
                if i is not None:
                    collect(b - 1)
                    place(b - 1)

            def place(b):
                dve.wait_ge(picked, b + 1)
                dve.tensor_copy(oS[:, :, bass.ds(b * DS, DS)], OT.rearrange("p (h t) -> p h t", h=HEADS)).then_inc(o_ready, 1)
            queries(0, 0)
            keys(0, 0)
            unit(0, 0, None)
            with dve.Fori(0, DB // 2 - 1) as i:
                step.begin(i, 10)
                unit(i * 2 + 1, 1, i)
                unit(i * 2 + 2, 0, i)
                step.end(DB // 2 - 1)
            unit(DB - 1, 1, DB // 2 - 1)
            new_map(DB - 1)
            map_out(DB - 1, 0)
            map_out(DB - 1, 3)
            collect(DB - 1)
            place(DB - 1)
            dve.wait_ge(ro_ready, 1)
            dve.scalar_tensor_tensor(m.mixT[:, 0:HEADS, SEQ:TOK], oS[:, :, :], m.subw[:, :], ro[:, :, :],
                                     ALU.mult, ALU.mult)


def mix_phase(nc, a, m):
    NR = NG + NE
    with ExitStack() as ctx:
        sb, sem = scope(nc, ctx)
        wst = sb("m_wst", [128, 2, D])
        woh, wol = sb("m_woh", [128, KD, D], F32R), sb("m_wol", [128, KD, D], F32R)
        mh, ml = sb("m_mh", [128, 2, KD, 128], F32R), sb("m_ml", [128, 2, KD, 128], F32R)
        xT = sb("m_xT", [128, 2, KD, 128])
        wr = sb("m_wr", [128, KD, NR])
        br = sb("m_br", [128, NR])
        xb = sb("m_xb", [128, 2, D])
        hs = sb("m_hs", [128, 2, D])
        ss = sb("m_ss", [128, 2])
        LG = sb("m_LG", [128, TILES, NR])
        place = sb("m_place", [128, TILES, EG])
        gm, gz, tm, v1, v2, w1, w2 = (sb(f"m_{n}", [128, TILES]) for n in ("gm", "gz", "tm", "v1", "v2", "w1", "w2"))
        t4, ohg, oh1, oh2, es, ge = (sb(f"m_{n}", [128, TILES, EG]) for n in ("t4", "ohg", "oh1", "oh2", "es", "ge"))
        t16 = sb("m_t16", [128, TILES, NG, EG])
        sel1, sel2, sel, pos = (sb(f"m_{n}", [128, TILES, NE]) for n in ("sel1", "sel2", "sel", "pos"))
        pre = sb("m_pre", [128, TILES + 1, NE])
        before = sb("m_before", [128, 128])
        valid = sb("m_valid", [128, TILES])
        tokf = sb("m_tokf", [128, TILES])
        zero = sb("m_zero", [SLOTS, 128])
        one16 = sb("m_one16", [128, NE])
        cnt, tl, cumf, base = (sb(f"m_{n}", [128, NE]) for n in ("cnt", "tl", "cumf", "base"))
        cnti, tli = sb("m_cnti", [128, NE], I32), sb("m_tli", [128, NE], I32)
        posf = sb("m_posf", [128, 2, TILES])
        tilef = sb("m_tilef", [1, SLOTS])
        over = sb("m_over", [1, SLOTS, NE])
        ef = sb("m_ef", [1, SLOTS])
        third = sb("m_third", [1, SLOTS], I32)
        rows_t = sb("m_rows_t", [SLOTS, 128])
        wo_in = [sem("m_wo_in0"), sem("m_wo_in1")]
        wr_in = sem("m_wr_in")
        x_in = [sem("m_x_in0"), sem("m_x_in1")]
        gate = sem("m_gate")
        w_rounded, w_split, mix_rounded, mix_split = (sem(f"m_{n}") for n in (
            "w_rounded", "w_split", "mix_rounded", "mix_split"))
        mixed, h_ready, squared, hs_ready, transposed, evacuated, routed, logits = (sem(f"m_{n}") for n in (
            "mixed", "h_ready", "squared", "hs_ready", "transposed", "evacuated", "routed", "logits"))
        act_step, dve_step, pool_step = sem("m_act_step"), sem("m_dve_step"), sem("m_pool_step")
        shifted, exp_done, v_diff, exp2_done = (sem(f"m_{n}") for n in ("shifted", "exp_done", "v_diff", "exp2_done"))
        hn_stored = [sem("m_hn_stored0"), sem("m_hn_stored1")]
        zeroed, scattered, rows_in = (sem(f"m_{n}") for n in ("zeroed", "scattered", "rows_in"))
        sel_ready, counted, pos_ready, rows_done = (sem(f"m_{n}") for n in ("sel_ready", "counted", "pos_ready", "rows_done"))
        block = ctx.enter_context(nc.Block())
        wo_d = a.w_out[0, :, :].rearrange("(k p) n -> p k n", p=128)
        xp = a.x_prompt[0, :, :].rearrange("(t p) d -> t p d", p=128)
        wrg = a.w_router_grp[0, :, :].rearrange("(k p) n -> p k n", p=128)
        wre = a.w_router_exp[0, :, :].rearrange("(k p) n -> p k n", p=128)

        @block.sync
        def _(sp):
            def store(t):
                sp.wait_ge(hs_ready, t + 1)
                sp.dma_start(m.hn_rows[t * 128:t * 128 + rows(t), :], hs[0:rows(t), t % 2, :]).then_inc(hn_stored[t % 2], 16)

            for t in range(TILES):
                if t >= 2:
                    store(t - 2)
                u, n = t % 2, rows(t)
                if t >= 2:
                    sp.wait_ge(h_ready, 2 * (t - 1))
                src = xp[t, :, :] if t < NT else a.x_sample.rearrange("b t d -> (b t) d")
                sp.dma_start(xb[0:n, u, :], src).then_inc(x_in[u], 16)
                if t == 0:
                    for k in range(KD):
                        if k >= 2:
                            sp.wait_ge(w_split, k - 1)
                        sp.dma_start(wst[:, k % 2, :], wo_d[:, k, :]).then_inc(wo_in[k % 2], 16)
                    with nc.allow_non_contiguous_dma("small router weights"):
                        sp.dma_start(wr[:, :, 0:NG], wrg).then_inc(wr_in, 16)
                        sp.dma_start(wr[:, :, NG:NR], wre).then_inc(wr_in, 16)
                        sp.dma_start(br[:, 0:NG], a.b_router_grp[0, :].partition_broadcast(128)).then_inc(wr_in, 16)
                        sp.dma_start(br[:, NG:NR], a.b_router_exp[0, :].partition_broadcast(128)).then_inc(wr_in, 16)

            store(TILES - 2)
            store(TILES - 1)
            sp.wait_ge(scattered, 16 * 2 * TILES)
            sp.dma_start(rows_t[:, :], m.slot_rows.rearrange("(i p) o -> i (p o)", p=128)).then_inc(rows_in, 16)
            sp.wait_ge(hn_stored[0], 16 * (TILES // 2 + 1))
            sp.wait_ge(hn_stored[1], 16 * (TILES // 2))

        @block.gpsimd
        def _(pool):
            step = Steps(pool, pool_step)

            def do(ins):
                step(ins)
                step.wait()

            def split_mix(t):
                u, n = t % 2, rows(t)
                if t >= 2:
                    pool.wait_ge(mixed, 2 * (t - 1))
                    pool.sem_inc(gate, 1)
                pool.tensor_copy(mh[:, u, :, 0:n], m.mixT[:, :, cols(t)]).then_inc(mix_rounded, 1)
                pool.wait_ge(mix_rounded, t + 1)
                pool.tensor_tensor(ml[:, u, :, 0:n], m.mixT[:, :, cols(t)], mh[:, u, :, 0:n], ALU.subtract).then_inc(mix_split, 1)
            split_mix(0)
            split_mix(1)
            do(pool.memset(LG[:, :, :], 0.0))
            for e in range(EG):
                do(pool.memset(place[:, :, e:e + 1], float(EG - e)))
            do(pool.memset(before[:, :], 0.0))
            do(pool.affine_select(out=before[:, :], in_=before[:, :], compare_op=ALU.is_ge, fill=1.0,
                                  base=0, pattern=[[-1, 128]], channel_multiplier=1))
            do(pool.memset(valid[:, :], 1.0))
            do(pool.memset(valid[NS:128, NT:TILES], 0.0))
            do(pool.memset(pre[:, 0, :], 0.0))
            do(pool.memset(one16[:, :], 1.0))
            do(pool.memset(zero[:, :], 0.0))
            pool.dma_start(m.slot_rows.rearrange("(i p) o -> i (p o)", p=128), zero[:, :]).then_inc(zeroed, 16)
            do(pool.iota(tokf[:, :], [[128, TILES]], base=0, channel_multiplier=1, allow_small_or_imprecise_dtypes=True))
            do(pool.iota(tilef[:, :], [[1, SLOTS]], base=0, channel_multiplier=0, allow_small_or_imprecise_dtypes=True))
            for t in range(2, TILES):
                split_mix(t)
            pool.wait_ge(zeroed, 16)
            pool.wait_ge(pos_ready, 1)
            for p in (m.pos1, m.pos2):
                for t in range(TILES):
                    n = rows(t)
                    pool.indirect_dma_start(m.slot_rows, bass.IndirectOffsetOnAxis(ap=p[0:n, t:t + 1], axis=0),
                                            tokf[0:n, t:t + 1], None).then_inc(scattered, 16)
            pool.wait_ge(scattered, 16 * 2 * TILES)

        POOL_ALL = EG + 10

        @block.tensor
        def _(pe):
            def project(t):
                u, n = t % 2, rows(t)
                for b in range(2):
                    if b == 0:
                        pe.wait_ge(mix_split, t + 1)
                    if t >= 2:
                        pe.wait_ge(h_ready, 2 * (t - 2) + b + 1)
                    for k in range(KD):
                        if t == 0 and b == 0:
                            pe.wait_ge(w_split, k + 1)
                        for i, (left, right) in enumerate(((mh, woh), (mh, wol), (ml, woh))):
                            ins = pe.matmul(m.ps[0:n, 2 * u + b, :], left[:, u, k, 0:n], right[:, k, b * 512:b * 512 + 512],
                                            start=(k == 0 and i == 0), stop=(k == KD - 1 and i == 2))
                    ins.then_inc(mixed, 1)

            def route(t):
                u, n = t % 2, rows(t)
                pe.wait_ge(hs_ready, t + 1)
                for b in range(2):
                    if t >= 1:
                        pe.wait_ge(evacuated, 2 * (t - 1) + b + 1)
                    for c in range(4):
                        k = 4 * b + c
                        ins = pe.transpose(m.ps[:, 4 + b, c * 128:c * 128 + n], hs[0:n, u, k * 128:k * 128 + 128],
                                           m.ident[0:n, 0:n])
                    ins.then_inc(transposed, 1)
                pe.wait_ge(evacuated, 2 * t + 2)
                if t == 0:
                    pe.wait_ge(wr_in, 64)
                if t >= 2:
                    pe.wait_ge(logits, t - 1)
                for k in range(KD):
                    ins = pe.matmul(m.ps[0:n, 6 + u, 0:NR], xT[:, u, k, 0:n], wr[:, k, :],
                                    start=(k == 0), stop=(k == KD - 1))
                ins.then_inc(routed, 1)
            def count():
                pe.wait_ge(sel_ready, 1)
                s = sel[:, :, :].rearrange("p t e -> p (t e)")
                pe.matmul(m.ps[:, 0, 0:TILES * NE], before[:, :], s, start=True, stop=True)
                pe.matmul(m.ps[:, 1, 0:TILES * NE], m.ones[:, :], s, start=True, stop=True).then_inc(counted, 1)

            def turn_rows():
                pe.wait_ge(rows_in, 16)
                pe.transpose(m.ps[:, 2, 0:SLOTS], rows_t[:, :], m.ident[0:SLOTS, 0:SLOTS]).then_inc(rows_done, 1)
            project(0)
            for t in range(TILES):
                if t + 1 < TILES:
                    project(t + 1)
                route(t)
            count()
            turn_rows()

        @block.scalar
        def _(act):
            load_ln_exp(nc, act)
            for k in range(KD):
                act.wait_ge(wo_in[k % 2], (k // 2 + 1) * 16)
                act.activation(woh[:, k, :], wst[:, k % 2, :], ACT.Copy).then_inc(w_rounded, 1)
            step = Steps(act, act_step)
            for t in range(TILES):
                u, n = t % 2, rows(t)
                act.wait_ge(h_ready, 2 * t + 2)
                if t >= 2:
                    act.wait_ge(transposed, 2 * (t - 1))
                    act.wait_ge(hn_stored[u], 16 * (t // 2))
                step(act.activation(hs[0:n, u, :], m.Y[0:n, t, :], ACT.Square, accum_out=ss[0:n, u:u + 1]))
                step.wait()
                step(act.activation(ss[0:n, u:u + 1], ss[0:n, u:u + 1], ACT.Ln, scale=1.0 / D, bias=m.eps[0:n, :]))
                step.wait()
                step(act.activation(ss[0:n, u:u + 1], ss[0:n, u:u + 1], ACT.Exp, scale=-0.5))
                step.wait()
                act.activation(hs[0:n, u, :], m.Y[0:n, t, :], ACT.Copy, scale=ss[0:n, u:u + 1]).then_inc(hs_ready, 1)
            act.wait_ge(shifted, 1)
            act.activation(t4[:, :, :], t4[:, :, :], ACT.Exp).then_inc(exp_done, 1)
            act.wait_ge(v_diff, 1)
            act.activation(w2[:, :], w2[:, :], ACT.Exp).then_inc(exp2_done, 1)

        @block.vector
        def _(dve):
            step = Steps(dve, dve_step)

            def add_x(t):
                u, n = t % 2, rows(t)
                dve.wait_ge(x_in[u], (t // 2 + 1) * 16)
                for b in range(2):
                    dve.wait_ge(mixed, 2 * t + b + 1)
                    c = slice(b * 512, b * 512 + 512)
                    dve.tensor_tensor(m.Y[0:n, t, c], m.ps[0:n, 2 * u + b, :], xb[0:n, u, c], ALU.add).then_inc(h_ready, 1)

            for k in range(KD):
                dve.wait_ge(w_rounded, k + 1)
                dve.tensor_tensor(wol[:, k, :], wst[:, k % 2, :], woh[:, k, :], ALU.subtract).then_inc(w_split, 1)
            dve.wait_ge(pool_step, POOL_ALL)
            add_x(0)
            for t in range(TILES):
                u, n = t % 2, rows(t)
                if t + 1 < TILES:
                    add_x(t + 1)
                for b in range(2):
                    dve.wait_ge(transposed, 2 * t + b + 1)
                    i = m.ps[:, 4 + b, :].rearrange("p (c n) -> p c n", c=4)[:, :, 0:n]
                    wn = m.n2w[:, 4 * b:4 * b + 4].unsqueeze(2).to_broadcast([128, 4, n])
                    dve.tensor_tensor(xT[:, u, 4 * b:4 * b + 4, 0:n], i, wn, ALU.mult).then_inc(evacuated, 1)
                dve.wait_ge(routed, t + 1)
                if t == 0:
                    dve.wait_ge(wr_in, 64)
                dve.tensor_tensor(LG[0:n, t, :], m.ps[0:n, 6 + u, 0:NR], br[0:n, :], ALU.add).then_inc(logits, 1)
            dve.wait_ge(logits, TILES)
            wide = lambda x: x[:, :].unsqueeze(2).to_broadcast([128, TILES, EG])

            def do(ins):
                step(ins)
                step.wait()

            def first_max(oh, x, mx):
                do(dve.tensor_reduce(mx[:, :], x, AX.X, ALU.max))
                do(dve.tensor_tensor(oh[:, :, :], x, wide(mx), ALU.is_equal))
                do(dve.tensor_tensor(oh[:, :, :], oh[:, :, :], place[:, :, :], ALU.mult))
                do(dve.tensor_reduce(tm[:, :], oh[:, :, :], AX.X, ALU.max))
                do(dve.tensor_tensor(oh[:, :, :], place[:, :, :], wide(tm), ALU.is_equal))
            G = LG[:, :, 0:NG]
            first_max(ohg, G, gm)
            do(dve.tensor_tensor(t4[:, :, :], G, wide(gm), ALU.subtract))
            dve.sem_inc(shifted, 1)
            dve.wait_ge(exp_done, 1)
            do(dve.tensor_reduce(gz[:, :], t4[:, :, :], AX.X, ALU.add))
            do(dve.reciprocal(gz[:, :], gz[:, :]))
            E4 = LG[:, :, NG:NR].rearrange("p t (g e) -> p t g e", g=NG)
            do(dve.tensor_tensor(t16[:, :, :, :], E4, ohg[:, :, :].unsqueeze(3).to_broadcast([128, TILES, NG, EG]), ALU.mult))
            do(dve.tensor_reduce(es[:, :, :], t16[:, :, :, :].rearrange("p t g e -> p t e g"), AX.X, ALU.add))
            first_max(oh1, es[:, :, :], v1)
            do(dve.scalar_tensor_tensor(es[:, :, :], oh1[:, :, :], -BIG, es[:, :, :], ALU.mult, ALU.add))
            first_max(oh2, es[:, :, :], v2)
            do(dve.tensor_tensor(w2[:, :], v2[:, :], v1[:, :], ALU.subtract))
            dve.sem_inc(v_diff, 1)
            dve.wait_ge(exp2_done, 1)
            do(dve.tensor_scalar(w1[:, :], w2[:, :], 1.0, None, ALU.add))
            do(dve.reciprocal(w1[:, :], w1[:, :]))
            do(dve.tensor_tensor(m.w1[:, :], w1[:, :], gz[:, :], ALU.mult))
            do(dve.tensor_tensor(m.w2[:, :], w2[:, :], m.w1[:, :], ALU.mult))

            ohg4 = ohg[:, :, :].unsqueeze(3).to_broadcast([128, TILES, NG, EG])
            for s, oh in ((sel1, oh1), (sel2, oh2)):
                do(dve.tensor_tensor(s[:, :, :].rearrange("p t (g e) -> p t g e", g=NG), ohg4,
                                     oh[:, :, :].unsqueeze(2).to_broadcast([128, TILES, NG, EG]), ALU.mult))
            do(dve.tensor_tensor(sel[:, :, :], sel1[:, :, :], sel2[:, :, :], ALU.add))
            do(dve.tensor_tensor(sel[:, :, :], sel[:, :, :], valid[:, :].unsqueeze(2).to_broadcast([128, TILES, NE]), ALU.mult))
            dve.sem_inc(sel_ready, 1)
            dve.wait_ge(counted, 1)
            for t in range(TILES):
                do(dve.scalar_tensor_tensor(pre[:, t + 1, :], m.ps[:, 1, t * NE:t * NE + NE], 128.0, pre[:, t, :],
                                            ALU.mult, ALU.add))
            do(dve.tensor_scalar(cnti[:, :], pre[:, TILES, :], 127.0, None, ALU.add))
            do(dve.tensor_scalar(tli[:, :], cnti[:, :], 7, None, ALU.logical_shift_right))
            do(dve.tensor_copy(tl[:, :], tli[:, :]))
            do(dve.tensor_tensor_scan(cumf[:, :], one16[:, :], tl[:, :], 0.0, ALU.mult, ALU.add))
            do(dve.tensor_tensor(base[:, :], cumf[:, :], tl[:, :], ALU.subtract))
            do(dve.tensor_scalar(base[:, :], base[:, :], 128.0, None, ALU.mult))
            do(dve.tensor_tensor(pos[:, :, :], m.ps[:, 0, 0:TILES * NE].rearrange("p (t e) -> p t e", e=NE),
                                 pre[:, 0:TILES, :], ALU.add))
            do(dve.tensor_tensor(pos[:, :, :], pos[:, :, :], base[:, :].unsqueeze(1).to_broadcast([128, TILES, NE]), ALU.add))
            for n, (s, p) in enumerate(((sel1, m.pos1), (sel2, m.pos2))):
                do(dve.tensor_tensor(s[:, :, :], s[:, :, :], pos[:, :, :], ALU.mult))
                do(dve.tensor_reduce(posf[:, n, :], s[:, :, :], AX.X, ALU.add))
                do(dve.tensor_copy(p[:, :], posf[:, n, :]))
            dve.sem_inc(pos_ready, 1)
            do(dve.tensor_copy(m.cum[:, :], cumf[0:1, :]))
            do(dve.tensor_tensor(over[:, :, :], tilef[:, :].unsqueeze(2).to_broadcast([1, SLOTS, NE]),
                                 cumf[0:1, :].unsqueeze(1).to_broadcast([1, SLOTS, NE]), ALU.is_ge))
            do(dve.tensor_reduce(ef[:, :], over[:, :, :], AX.X, ALU.add))
            do(dve.tensor_scalar(ef[:, :], ef[:, :], float(NE - 1), None, ALU.min))
            do(dve.tensor_copy(m.tile_expert[:, :], ef[:, :]))
            do(dve.tensor_scalar(third[:, :], ef[:, :], 11.0, None, ALU.mult))
            do(dve.tensor_scalar(third[:, :], third[:, :], 5, None, ALU.logical_shift_right))
            do(dve.scalar_tensor_tensor(m.tile_ring[:, :], third[:, :], -3.0, ef[:, :], ALU.mult, ALU.add))
            dve.wait_ge(rows_done, 1)
            do(dve.tensor_copy(m.slot_tok[:, :], m.ps[:, 2, 0:SLOTS]))


def moe_phase(nc, a, out, m):
    FC = FF // 128
    EW = KD * 2 * FF
    with ExitStack() as ctx:
        sb, sem = scope(nc, ctx)
        ring = sb("e_ring", [128, RING * (EW + FC * D)])
        up_w = ring[:, 0:RING * EW].rearrange("p (r k f) -> p r k f", r=RING, k=KD)
        down_w = ring[:, RING * EW:].rearrange("p (r f n) -> p (r f) n", r=RING, f=FC)
        up_k = ring[:, 0:RING * EW].rearrange("p (r f) -> p r f", f=2 * FF)
        spare = sb("e_spare", [128, 6 * D])
        xg = spare[:, 0:2 * D].rearrange("p (u d) -> p u d", u=2)
        xgT = spare[:, 2 * D:4 * D].rearrange("p (u k n) -> p u k n", u=2, k=KD)
        oE = spare[:, 4 * D:6 * D].rearrange("p (u d) -> p u d", u=2)
        hid = sb("e_hid", [128, 2, FF])
        sg = sb("e_sg", [128, 2, FF])
        hT = sb("e_hT", [128, 2, FF])
        idx = sb("e_idx", [128, 2], I32)
        back = m.mixT[:, :, :].rearrange("p k t -> p (k t)")[:, 0:8 * D].rearrange("p (s j d) -> p s j d", s=4, j=TOP)
        w_in = [sem(f"e_w_in{r}") for r in range(RING)]
        w_ready, tile_done = sem("e_w_ready"), sem("e_tile_done")
        idx_ready, x_in, x_turned, xt_ready = sem("e_idx_ready"), [sem("e_x_in0"), sem("e_x_in1")], sem("e_x_turned"), sem("e_xt_ready")
        up_done, silu_done, hid_ready, h_turned, ht_ready = (sem(f"e_{n}") for n in (
            "up_done", "silu_done", "hid_ready", "h_turned", "ht_ready"))
        down_done, o_left, o_right = sem("e_down_done"), sem("e_o_left"), sem("e_o_right")
        o_stored = [sem("e_o_stored0"), sem("e_o_stored1")]
        back_in = [sem(f"e_back_in{s}") for s in range(4)]
        act_gate, pool_gate = sem("e_act_gate"), sem("e_pool_gate")
        added1, added, y_stored = sem("e_added1"), sem("e_added"), sem("e_y_stored")
        block = ctx.enter_context(nc.Block())
        wg_d = a.w_gate[0, :, :, :].rearrange("e (k p) f -> e p k f", p=128)
        wu_d = a.w_up[0, :, :, :].rearrange("e (k p) f -> e p k f", p=128)
        wd_d = a.w_down[0, :, :, :].rearrange("e (k p) n -> e p k n", p=128)
        orow = m.expert_rows.rearrange("(i p) d -> i p d", p=128)

        @block.sync
        def _(sp):
            def load(e, r):
                sp.dma_start(up_w[:, r, :, 0:FF], wg_d[e, :, :, :]).then_inc(w_in[r], 16)
                sp.dma_start(up_w[:, r, :, FF:2 * FF], wu_d[e, :, :, :]).then_inc(w_in[r], 16)
                sp.dma_start(down_w[:, FC * r:FC * r + FC, :], wd_d[e, :, :, :]).then_inc(w_in[r], 16)

            def landed(r, turn):
                sp.wait_ge(w_in[r], turn * 48 + 48)
                sp.sem_inc(w_ready, 1)

            def replace(e, r, turn):
                tiles = sp.value_load(m.cum[0:1, bass.ds(e - RING, 1)], min_val=0, max_val=SLOTS)
                sp.wait_ge(tile_done, tiles + 1)
                load(e, r)
                landed((r - 1) % RING, turn if r else turn - 1)
            for r in range(RING):
                load(r, r)
            landed(0, 0)
            landed(1, 0)
            with sp.Fori(1, NE // RING) as j:
                for r in range(RING):
                    replace(j * RING + r, r, j)
            replace(NE - 1, 0, NE // RING)
            landed(0, NE // RING)

        @block.gpsimd
        def _(pool):
            def gather(i, u, turn):
                if turn is not None:
                    pool.wait_ge(x_in[u], turn * 16)
                    pool.wait_ge(x_turned, i - 1)
                pool.tensor_copy(idx[:, u:u + 1], m.slot_tok[:, bass.ds(i, 1)]).then_inc(idx_ready, 1)
                pool.wait_ge(idx_ready, i + 1)
                pool.sem_inc(pool_gate, 1)
                pool.indirect_dma_start(xg[:, u, :], None, m.hn_rows,
                                        bass.IndirectOffsetOnAxis(ap=idx[:, u:u + 1], axis=0)).then_inc(x_in[u], 16)
            gather(0, 0, None)
            gather(1, 1, None)
            with pool.Fori(1, SLOTS // 2) as j:
                for u in range(2):
                    gather(j * 2 + u, u, j)
            for u in range(2):
                pool.wait_ge(o_stored[u], SLOTS // 2 * 16)
            for t in range(TILES):
                n, s = rows(t), t % 4
                if t >= 4:
                    pool.wait_ge(added, t - 3)
                for j, p in enumerate((m.pos1, m.pos2)):
                    pool.indirect_dma_start(back[0:n, s, j, :], None, m.expert_rows,
                                            bass.IndirectOffsetOnAxis(ap=p[0:n, t:t + 1], axis=0)).then_inc(back_in[s], 16)

        @block.tensor
        def _(pe):
            def turn_x(i, u, turn):
                pe.wait_ge(x_in[u], turn * 16 + 16)
                if not (isinstance(i, int) and i == 0):
                    pe.wait_ge(xt_ready, i)
                for k in range(KD):
                    ins = pe.transpose(m.ps[:, k // 4, k % 4 * 128:k % 4 * 128 + 128],
                                       xg[:, u, k * 128:k * 128 + 128], m.ident[:, :])
                ins.then_inc(x_turned, 1)

            used = pe.value_load(m.cum[0:1, NE - 1:NE], min_val=0, max_val=SLOTS)

            def if_used(i, full, nothing):
                if isinstance(i, int) and i < TOP * TOK // 128:
                    full()
                else:
                    with pe.If(used > i):
                        full()
                    with pe.Else():
                        nothing()

            def expert_of(i):
                e = pe.value_load(m.tile_expert[0:1, bass.ds(i, 1)], min_val=0, max_val=NE - 1)
                r = pe.value_load(m.tile_ring[0:1, bass.ds(i, 1)], min_val=0, max_val=RING - 1)
                return e, r

            def up(i, u):
                e, r = expert_of(i)
                pe.wait_ge(xt_ready, i + 1)
                pe.wait_ge(w_ready, e + 1)
                def full():
                    for k in range(KD):
                        ins = pe.matmul(m.ps[:, 2 + u, :], xgT[:, u, k, :], up_k[:, bass.ds(r * KD + k, 1), :].squeeze(1),
                                        start=(k == 0), stop=(k == KD - 1))
                    ins.then_inc(up_done, 1)

                def nothing():
                    pe.matmul(m.ps[:, 2 + u, 0:EG], xgT[:, u, 0, :], up_w[:, 0, 0, 0:EG], start=True, stop=True).then_inc(up_done, 1)
                if_used(i, full, nothing)

            def down(i, u):
                r = pe.value_load(m.tile_ring[0:1, bass.ds(i, 1)], min_val=0, max_val=RING - 1)
                pe.wait_ge(hid_ready, i + 1)
                for f in range(FC):
                    ins = pe.transpose(m.ps[:, 4 + u, f * 128:f * 128 + 128], hid[:, u, f * 128:f * 128 + 128], m.ident[:, :])
                ins.then_inc(h_turned, 1)
                pe.wait_ge(ht_ready, i + 1)
                if not (isinstance(i, int) and i == 0):
                    pe.wait_ge(o_left, i)
                    pe.wait_ge(o_right, i)
                def full():
                    for b in range(2):
                        for f in range(FC):
                            ins = pe.matmul(m.ps[:, 6 + b, :], hT[:, u, f * 128:f * 128 + 128],
                                            down_w[:, bass.ds(r * FC + f, 1), b * 512:b * 512 + 512].squeeze(1),
                                            start=(f == 0), stop=(f == FC - 1))
                        ins.then_inc(tile_done if b else down_done, 1)

                def nothing():
                    for b in range(2):
                        pe.matmul(m.ps[:, 6 + b, 0:EG], hT[:, u, 0:128], down_w[:, 0, 0:EG],
                                  start=True, stop=True).then_inc(tile_done if b else down_done, 1)
                if_used(i, full, nothing)

            pe.sem_inc(tile_done, 1)
            turn_x(0, 0, 0)
            turn_x(1, 1, 0)
            up(0, 0)
            up(1, 1)
            turn_x(2, 0, 1)
            down(0, 0)
            with pe.Fori(1, SLOTS // 2 - 1) as j:
                turn_x(j * 2 + 1, 1, j)
                up(j * 2, 0)
                down(j * 2 - 1, 1)
                turn_x(j * 2 + 2, 0, j + 1)
                up(j * 2 + 1, 1)
                down(j * 2, 0)
            turn_x(SLOTS - 1, 1, SLOTS // 2 - 1)
            up(SLOTS - 2, 0)
            down(SLOTS - 3, 1)
            up(SLOTS - 1, 1)
            down(SLOTS - 2, 0)
            down(SLOTS - 1, 1)

        @block.scalar
        def _(act):
            def silu(i, u):
                act.wait_ge(up_done, i + 1)
                act.activation(sg[:, u, :], m.ps[:, 2 + u, 0:FF], ACT.Silu).then_inc(silu_done, 1)

            def rest(i, u, turn):
                act.wait_ge(h_turned, i + 1)
                act.activation(hT[:, u, :], m.ps[:, 4 + u, 0:FF], ACT.Copy).then_inc(ht_ready, 1)
                act.wait_ge(down_done, i + 1)
                if not (isinstance(turn, int) and turn == 0):
                    act.wait_ge(o_stored[u], turn * 16)
                act.activation(oE[:, u, 0:512], m.ps[:, 6, :], ACT.Copy).then_inc(o_left, 1)
                act.wait_ge(o_left, i + 1)
                act.wait_ge(o_right, i + 1)
                act.sem_inc(act_gate, 1)
                act.dma_start(orow[i, :, :], oE[:, u, :]).then_inc(o_stored[u], 16)
            silu(0, 0)
            silu(1, 1)
            rest(0, 0, 0)
            silu(2, 0)
            rest(1, 1, 0)
            silu(3, 1)
            rest(2, 0, 1)
            with act.Fori(2, SLOTS // 2) as j:
                silu(j * 2, 0)
                rest(j * 2 - 1, 1, j - 1)
                silu(j * 2 + 1, 1)
                rest(j * 2, 0, j)
            rest(SLOTS - 1, 1, SLOTS // 2 - 1)

            for t in range(TILES):
                act.wait_ge(added, t + 1)
                dst = out.y_prompt[0, t * 128:t * 128 + 128, :] if t < NT else out.y_sample.rearrange("b t d -> (b t) d")
                act.dma_start(dst, m.Y[0:rows(t), t, :]).then_inc(y_stored, 16)
            act.wait_ge(y_stored, 16 * TILES)

        @block.vector
        def _(dve):
            def turn(i, u):
                for b in range(2):
                    if b == 0:
                        dve.wait_ge(x_turned, i + 1)
                    p = m.ps[:, b, :].rearrange("p (c n) -> p c n", c=4)
                    wn = m.n2w[:, 4 * b:4 * b + 4].unsqueeze(2).to_broadcast([128, 4, 128])
                    ins = dve.tensor_tensor(xgT[:, u, 4 * b:4 * b + 4, :], p, wn, ALU.mult)
                ins.then_inc(xt_ready, 1)

            def hidden(i, u):
                dve.wait_ge(silu_done, i + 1)
                dve.tensor_tensor(hid[:, u, :], sg[:, u, :], m.ps[:, 2 + u, FF:2 * FF], ALU.mult).then_inc(hid_ready, 1)

            def right(i, u, turn_):
                dve.wait_ge(tile_done, i + 2)
                if not (isinstance(turn_, int) and turn_ == 0):
                    dve.wait_ge(o_stored[u], turn_ * 16)
                dve.tensor_copy(oE[:, u, 512:1024], m.ps[:, 7, :]).then_inc(o_right, 1)
            turn(0, 0)
            turn(1, 1)
            hidden(0, 0)
            hidden(1, 1)
            turn(2, 0)
            right(0, 0, 0)
            turn(3, 1)
            hidden(2, 0)
            right(1, 1, 0)
            turn(4, 0)
            hidden(3, 1)
            right(2, 0, 1)
            with dve.Fori(2, SLOTS // 2 - 1) as j:
                turn(j * 2 + 1, 1)
                hidden(j * 2, 0)
                right(j * 2 - 1, 1, j - 1)
                turn(j * 2 + 2, 0)
                hidden(j * 2 + 1, 1)
                right(j * 2, 0, j)
            turn(SLOTS - 1, 1)
            hidden(SLOTS - 2, 0)
            right(SLOTS - 3, 1, SLOTS // 2 - 2)
            hidden(SLOTS - 1, 1)
            right(SLOTS - 2, 0, SLOTS // 2 - 1)
            right(SLOTS - 1, 1, SLOTS // 2 - 1)
            for t in range(TILES):
                n, s = rows(t), t % 4
                dve.wait_ge(back_in[s], (t // 4 + 1) * 32)
                y = m.Y[0:n, t, :]
                dve.scalar_tensor_tensor(y, back[0:n, s, 0, :], m.w1[0:n, t:t + 1], y, ALU.mult, ALU.add).then_inc(added1, 1)
                dve.wait_ge(added1, t + 1)
                dve.scalar_tensor_tensor(y, back[0:n, s, 1, :], m.w2[0:n, t:t + 1], y, ALU.mult, ALU.add).then_inc(added, 1)


_INS = ["x_prompt", "x_sample", "cache_k", "cache_v", "state_hgrn", "page_table", "norm1_w", "w_in", "q_norm_w",
        "k_norm_w", "lambda_q1", "lambda_k1", "lambda_q2", "lambda_k2", "subln_w", "hg_lb", "hg_norm_w", "w_out",
        "norm2_w", "w_router_grp", "b_router_grp", "w_router_exp", "b_router_exp", "w_gate", "w_up", "w_down"]
_OUTS = [("y_prompt", (1, SEQ, D)), ("y_sample", (DB, DS, D)), ("k_prompt", (1, 1, SEQ, HEADS, 128)),
         ("v_prompt", (1, 1, SEQ, HEADS, 128)), ("hgrn_prompt", (1, 1, HEADS, 128, 128)),
         ("k_sample", (1, DB, DS, HEADS, 128)), ("v_sample", (1, DB, DS, HEADS, 128)),
         ("hgrn_sample", (1, DB, HEADS, 128, 128))]


def kernel(**inputs):
    import numpy as _np
    import concourse.bacc as _bacc
    from concourse.bass_utils import run_bass_kernel_spmd as _run

    nc = _bacc.Bacc("TRN2", target_bir_lowering=False, num_devices=1)
    arrays, a, out = {}, Named(), Named()
    for name in _INS:
        x = _np.ascontiguousarray(inputs[name])
        arrays[f"in_{name}"] = x
        a.__dict__[name] = nc.dram_tensor(f"in_{name}", x.shape, mybir.dt.from_np(x.dtype), kind="ExternalInput").ap()
    for name, shape in _OUTS:
        out.__dict__[name] = nc.dram_tensor(f"out_{name}", shape, F32, kind="ExternalOutput").ap()
    build(nc, a, out)
    r = _run(nc, [arrays], core_ids=[0])
    return tuple(r.results[0][f"out_{name}"] for name, _ in _OUTS)
```
